# Optimizing a Trainium2 kernel written in Bass

```python
import math
import jax
import jax.numpy as jnp
from jax import lax
import numpy as np

D_MODEL = 1024
BATCH = 1
SEQ = 256
DEPTH = 1

HEAD_DIM = 64
MIX_WIDTH = D_MODEL // 4
N_BRANCH = 4
Q_BLOCK = 128

LRU_WIDTH = MIX_WIDTH
LRU_BLOCKS = 4
LRU_BLOCK = LRU_WIDTH // LRU_BLOCKS
CONV_WIDTH = 4
LRU_C = 8.0
LRU_A_MIN = 0.9
LRU_A_MAX = 0.999

SWA_HEADS = MIX_WIDTH // HEAD_DIM
SWA_KV_HEADS = 2
SWA_WINDOW = 128

DIFF_HEADS = 4
DIFF_DIM = MIX_WIDTH // (2 * DIFF_HEADS)
DIFF_SUBLN_EPS = 1e-5

NSA_HEADS = MIX_WIDTH // HEAD_DIM
NSA_CMP_LEN = 32
NSA_CMP_STRIDE = 16
NSA_SLC_LEN = 64
NSA_TOPK = 16
NSA_WINDOW = 512
NSA_FORCED_SCORE = 1e4

REL_BUCKETS = 32
REL_MAX_DIST = 128
N_BIAS_HEADS = SWA_HEADS + DIFF_HEADS + NSA_HEADS

N_GROUPS = 4
EXPERTS_PER_GROUP = 8
N_EXPERTS = N_GROUPS * EXPERTS_PER_GROUP
TOPK_IN_GROUP = 2
EXPERT_FF = D_MODEL // 4
ROUTER_BIAS_SCALE = 0.01

NORM_EPS = 1e-6
NEG_INF = -1e30
TINY = 1e-30

IN_SPLITS = (
    LRU_WIDTH, LRU_WIDTH,
    SWA_HEADS * HEAD_DIM, SWA_KV_HEADS * HEAD_DIM, SWA_KV_HEADS * HEAD_DIM,
    2 * DIFF_HEADS * DIFF_DIM, 2 * DIFF_HEADS * DIFF_DIM, 2 * DIFF_HEADS * DIFF_DIM,
    NSA_HEADS * HEAD_DIM,
    HEAD_DIM, HEAD_DIM, HEAD_DIM, HEAD_DIM, HEAD_DIM, HEAD_DIM,
    3 * NSA_HEADS,
)
N_IN = sum(IN_SPLITS)

kernel_name = 'hybrid_griffin_gated_nsa_diff_moe'

def rmsnorm(x, g, eps=NORM_EPS):
    xf = x.astype(jnp.float32)
    y = xf * lax.rsqrt(jnp.mean(xf * xf, axis=-1, keepdims=True) + eps)
    return (y * g.astype(jnp.float32)).astype(x.dtype)

def t5_bucket(dist):
    n = jnp.maximum(dist, 0)
    exact = REL_BUCKETS // 2
    scaled = jnp.log(jnp.maximum(n, 1).astype(jnp.float32) / exact) / math.log(REL_MAX_DIST / exact)
    large = jnp.minimum(exact + (scaled * (REL_BUCKETS - exact)).astype(jnp.int32), REL_BUCKETS - 1)
    return jnp.where(n < exact, n, large)

def masked_softmax(s, mask, sink=None):
    s = jnp.where(mask, s, NEG_INF)
    m = jnp.max(s, axis=-1, keepdims=True)
    if sink is not None:
        m = jnp.maximum(m, sink)
    p = jnp.where(mask, jnp.exp(s - m), 0.0)
    denom = jnp.sum(p, axis=-1, keepdims=True)
    if sink is not None:
        denom = denom + jnp.exp(sink - m)
    return p / jnp.maximum(denom, TINY)

def split_columns(proj):
    offs = np.cumsum(IN_SPLITS)[:-1].tolist()
    return jnp.split(proj, offs, axis=-1)

def rglru_mixer(xa, gate, conv_w, conv_b, w_a, b_a, w_x, b_x, lam):
    f32 = jnp.float32
    Bsz, S, W = xa.shape
    xp = jnp.pad(xa.astype(f32), ((0, 0), (CONV_WIDTH - 1, 0), (0, 0)))
    xc = conv_b.astype(f32) + xp[:, 0:S] * conv_w[0].astype(f32)
    for i in range(1, CONV_WIDTH):
        xc = xc + xp[:, i:i + S] * conv_w[i].astype(f32)
    xb = xc.reshape(Bsz, S, LRU_BLOCKS, LRU_BLOCK)
    r = jax.nn.sigmoid(jnp.einsum('bshi,hij->bshj', xb, w_a.astype(f32)).reshape(Bsz, S, W) + b_a.astype(f32))
    i_g = jax.nn.sigmoid(jnp.einsum('bshi,hij->bshj', xb, w_x.astype(f32)).reshape(Bsz, S, W) + b_x.astype(f32))
    log_a = -LRU_C * r * jax.nn.softplus(-lam.astype(f32))
    a = jnp.exp(log_a)
    mult = jnp.sqrt(-jnp.expm1(2.0 * log_a))
    mult = jnp.where(jnp.arange(S)[None, :, None] == 0, 1.0, mult)
    b = mult * i_g * xc

    def combine(e, l):
        return (e[0] * l[0], l[0] * e[1] + l[1])

    _, hs = lax.associative_scan(combine, (a, b), axis=1)
    return (hs * jax.nn.gelu(gate.astype(f32))).astype(xa.dtype)

def banded_attention(q, k, v, window, bias_tab, sinks=None):
    f32 = jnp.float32
    Bsz, S, Hq, dh = q.shape
    Hkv = k.shape[2]
    G = Hq // Hkv
    nb = S // Q_BLOCK
    nback = -(-window // Q_BLOCK)
    kw_len = (nback + 1) * Q_BLOCK

    def windows(t):
        tp = jnp.pad(t.astype(f32), ((0, 0), (nback * Q_BLOCK, 0), (0, 0), (0, 0)))
        tp = tp.reshape(Bsz, nb + nback, Q_BLOCK, Hkv, dh)
        return jnp.concatenate([tp[:, i:i + nb] for i in range(nback + 1)], axis=2)

    kb, vb = windows(k), windows(v)
    qb = q.astype(f32).reshape(Bsz, nb, Q_BLOCK, Hkv, G, dh)
    s = jnp.einsum('bnqhgd,bnkhd->bnhgqk', qb, kb) * dh ** -0.5
    dist = jnp.arange(Q_BLOCK)[:, None] - jnp.arange(kw_len)[None, :] + nback * Q_BLOCK
    kpos = (jnp.arange(nb)[:, None, None] - nback) * Q_BLOCK + jnp.arange(kw_len)[None, None, :]
    mask = (dist >= 0) & (dist < window) & (kpos >= 0)
    bias = jnp.transpose(bias_tab[t5_bucket(dist)], (2, 0, 1)).reshape(Hkv, G, Q_BLOCK, kw_len)
    sink = None if sinks is None else sinks.astype(f32).reshape(1, 1, Hkv, G, 1, 1)
    p = masked_softmax(s + bias, mask[None, :, None, None], sink)
    o = jnp.einsum('bnhgqk,bnkhd->bnqhgd', p, vb)
    return o.reshape(Bsz, S, Hq * dh).astype(q.dtype)

def diff_lambda_init(layer):
    return 0.8 - 0.6 * math.exp(-0.3 * layer)

def diff_attention(q, k, v, lq1, lk1, lq2, lk2, subln_g, lambda_init, bias_tab):
    f32 = jnp.float32
    Bsz, S, H, _, d = q.shape
    nb = S // Q_BLOCK
    lam = (jnp.exp(jnp.sum(lq1.astype(f32) * lk1.astype(f32)))
           - jnp.exp(jnp.sum(lq2.astype(f32) * lk2.astype(f32))) + lambda_init)
    kf = k.astype(f32)
    vf = v.astype(f32)
    qb = jnp.moveaxis(q.astype(f32).reshape(Bsz, nb, Q_BLOCK, H, 2, d), 1, 0)
    kpos = jnp.arange(S)

    def one_block(args):
        q_blk, n = args
        qpos = n * Q_BLOCK + jnp.arange(Q_BLOCK)
        dist = qpos[:, None] - kpos[None, :]
        bias = jnp.transpose(bias_tab[t5_bucket(dist)], (2, 0, 1))[None, :, None]
        s = jnp.einsum('bqhmd,bkhmd->bhmqk', q_blk, kf) * d ** -0.5 + bias
        p = masked_softmax(s, dist >= 0)
        attn = p[:, :, 0] - lam * p[:, :, 1]
        return jnp.einsum('bhqk,bkhe->bqhe', attn, vf)

    o = lax.map(one_block, (qb, jnp.arange(nb)))
    o = jnp.moveaxis(o, 0, 1).reshape(Bsz, S, H, 2 * d)
    o = rmsnorm(o, subln_g, DIFF_SUBLN_EPS) * (1.0 - lambda_init)
    return o.reshape(Bsz, S, H * 2 * d).astype(q.dtype)

def nsa_compress(t, pos_emb, w1, w2, cmp_idx):
    f32 = jnp.float32
    blocks = t.astype(f32)[:, cmp_idx] + pos_emb.astype(f32)
    flat = blocks.reshape(t.shape[0], cmp_idx.shape[0], -1)
    return jax.nn.gelu(flat @ w1.astype(f32)) @ w2.astype(f32)

def nsa_selection_aggregator(n_cmp, n_slc):
    ratio_s = NSA_SLC_LEN // NSA_CMP_STRIDE
    ratio_c = NSA_CMP_LEN // NSA_CMP_STRIDE
    w = np.convolve(np.ones(ratio_s), np.ones(ratio_c)).astype(np.float32)
    cj = np.arange(n_slc)[:, None] * ratio_s - (ratio_c - 1) + np.arange(w.size)[None, :]
    jj = np.broadcast_to(np.arange(n_slc)[:, None], cj.shape)
    ww = np.broadcast_to(w[None, :], cj.shape)
    keep = (cj >= 0) & (cj < n_cmp)
    agg = np.zeros((n_cmp, n_slc), np.float32)
    np.add.at(agg, (cj[keep], jj[keep]), ww[keep])
    return jnp.asarray(agg)

def nsa_attention(q, k_cmp, v_cmp, k_slc, v_slc, k_win, v_win, gates,
                  pos_k, w1_k, w2_k, pos_v, w1_v, w2_v, bias_tab):
    f32 = jnp.float32
    Bsz, S, H, dh = q.shape
    nb = S // Q_BLOCK
    n_cmp = (S - NSA_CMP_LEN) // NSA_CMP_STRIDE + 1
    n_slc = S // NSA_SLC_LEN
    top_n = min(NSA_TOPK, n_slc)
    cmp_idx = jnp.asarray(np.arange(n_cmp)[:, None] * NSA_CMP_STRIDE + np.arange(NSA_CMP_LEN)[None, :])
    kc = nsa_compress(k_cmp, pos_k, w1_k, w2_k, cmp_idx)
    vc = nsa_compress(v_cmp, pos_v, w1_v, w2_v, cmp_idx)
    cmp_end = jnp.arange(n_cmp) * NSA_CMP_STRIDE + NSA_CMP_LEN - 1
    agg = nsa_selection_aggregator(n_cmp, n_slc)
    slc_ids = jnp.arange(n_slc)
    slc_start = slc_ids * NSA_SLC_LEN
    ks = k_slc.astype(f32)
    vs = v_slc.astype(f32)
    scale = dh ** -0.5
    qb = jnp.moveaxis(q.astype(f32).reshape(Bsz, nb, Q_BLOCK, H, dh), 1, 0)

    def one_block(args):
        q_blk, n = args
        qpos = n * Q_BLOCK + jnp.arange(Q_BLOCK)
        dist_c = qpos[:, None] - cmp_end[None, :]
        bias_c = jnp.transpose(bias_tab[t5_bucket(dist_c)], (2, 0, 1))
        s_c = jnp.einsum('bqhd,bcd->bhqc', q_blk, kc) * scale + bias_c
        p_c = masked_softmax(s_c, dist_c >= 0)
        o_c = jnp.einsum('bhqc,bcd->bqhd', p_c, vc)
        imp = jnp.einsum('bhqc,cj->bqj', p_c, agg)
        cur = qpos // NSA_SLC_LEN
        valid = slc_start[None, :] <= qpos[:, None]
        forced = ((slc_ids[None, :] == 0) | (slc_ids[None, :] == cur[:, None])
                  | (slc_ids[None, :] == cur[:, None] - 1))
        imp = jnp.where(forced, NSA_FORCED_SCORE, jnp.where(valid, imp, -1.0))
        _, sel = lax.top_k(imp, top_n)
        kpos = (sel[..., None] * NSA_SLC_LEN + jnp.arange(NSA_SLC_LEN)).reshape(Bsz, Q_BLOCK, top_n * NSA_SLC_LEN)
        kg = jax.vmap(lambda kk, pp: kk[pp])(ks, kpos)
        vg = jax.vmap(lambda vv, pp: vv[pp])(vs, kpos)
        dist_s = qpos[None, :, None] - kpos
        bias_s = jnp.moveaxis(bias_tab[t5_bucket(dist_s)], -1, 1)
        s_s = jnp.einsum('bqhd,bqkd->bhqk', q_blk, kg) * scale + bias_s
        p_s = masked_softmax(s_s, (dist_s >= 0)[:, None])
        o_s = jnp.einsum('bhqk,bqkd->bqhd', p_s, vg)
        return o_c, o_s

    o_c, o_s = lax.map(one_block, (qb, jnp.arange(nb)))
    o_c = jnp.moveaxis(o_c, 0, 1).reshape(Bsz, S, H, dh)
    o_s = jnp.moveaxis(o_s, 0, 1).reshape(Bsz, S, H, dh)
    o_w = banded_attention(q, k_win[:, :, None], v_win[:, :, None], NSA_WINDOW, bias_tab)
    o_w = o_w.astype(f32).reshape(Bsz, S, H, dh)
    g = jax.nn.sigmoid(gates.astype(f32))
    o = g[..., 0:1] * o_c + g[..., 1:2] * o_s + g[..., 2:3] * o_w
    return o.reshape(Bsz, S, H * dh).astype(q.dtype)

def hier_moe(h, w_grp, b_grp, w_exp, b_exp, w_g, w_u, w_d):
    f32 = jnp.float32
    Bsz, S, D = h.shape
    t = h.reshape(-1, D)
    T = t.shape[0]
    grp_logits = (t @ w_grp).astype(f32) + b_grp.astype(f32)
    grp_prob = jax.nn.softmax(grp_logits, axis=-1)
    _, g_sel = lax.top_k(grp_logits, 1)
    g_w = jnp.take_along_axis(grp_prob, g_sel, axis=-1)
    exp_logits = ((t @ w_exp).astype(f32) + b_exp.astype(f32)).reshape(T, N_GROUPS, EXPERTS_PER_GROUP)
    in_grp = jnp.take_along_axis(exp_logits, g_sel[:, :, None], axis=1)[:, 0]
    top_v, top_i = lax.top_k(in_grp, TOPK_IN_GROUP)
    top_w = jax.nn.softmax(top_v, axis=-1) * g_w
    eid = g_sel * EXPERTS_PER_GROUP + top_i
    combine = jnp.sum(jax.nn.one_hot(eid, N_EXPERTS, dtype=f32) * top_w[..., None], axis=1)
    y = jnp.zeros((T, D), f32)
    for e in range(N_EXPERTS):
        he = jax.nn.silu(t @ w_g[e]) * (t @ w_u[e])
        y = y + combine[:, e:e + 1] * (he @ w_d[e]).astype(f32)
    return y.reshape(Bsz, S, D).astype(h.dtype)

def setup_inputs(seed: int = 0) -> dict:
    key = jax.random.key(seed)
    ks = iter(jax.random.split(key, 64))
    f32 = jnp.float32
    L = DEPTH

    def nrm(shape, scale):
        return jax.random.normal(next(ks), shape, f32) * scale

    def gain(shape):
        return 1.0 + nrm(shape, 0.02)

    x = nrm((BATCH, SEQ, D_MODEL), 1.0)
    u = jax.random.uniform(next(ks), (L, LRU_WIDTH), f32, LRU_A_MIN, LRU_A_MAX)
    a0 = u ** (1.0 / LRU_C)
    lru_lambda = jnp.log(a0) - jnp.log1p(-a0)
    flat_cmp = NSA_CMP_LEN * HEAD_DIM
    return {
        'x': x,
        'rel_bias': nrm((REL_BUCKETS, N_BIAS_HEADS), 0.5),
        'final_norm_g': gain((D_MODEL,)),
        'mix_norm_g': gain((L, D_MODEL)),
        'w_in': nrm((L, D_MODEL, N_IN), D_MODEL ** -0.5),
        'conv_w': nrm((L, CONV_WIDTH, LRU_WIDTH), CONV_WIDTH ** -0.5),
        'conv_b': nrm((L, LRU_WIDTH), 0.01),
        'lru_w_a': nrm((L, LRU_BLOCKS, LRU_BLOCK, LRU_BLOCK), LRU_BLOCK ** -0.5),
        'lru_b_a': nrm((L, LRU_WIDTH), 0.01),
        'lru_w_x': nrm((L, LRU_BLOCKS, LRU_BLOCK, LRU_BLOCK), LRU_BLOCK ** -0.5),
        'lru_b_x': nrm((L, LRU_WIDTH), 0.01),
        'lru_lambda': lru_lambda,
        'swa_sinks': nrm((L, SWA_HEADS), 0.5),
        'diff_lq1': nrm((L, DIFF_DIM), 0.1),
        'diff_lk1': nrm((L, DIFF_DIM), 0.1),
        'diff_lq2': nrm((L, DIFF_DIM), 0.1),
        'diff_lk2': nrm((L, DIFF_DIM), 0.1),
        'diff_subln_g': gain((L, 2 * DIFF_DIM)),
        'nsa_pos_k': nrm((L, NSA_CMP_LEN, HEAD_DIM), 0.02),
        'nsa_w1_k': nrm((L, flat_cmp, HEAD_DIM), flat_cmp ** -0.5),
        'nsa_w2_k': nrm((L, HEAD_DIM, HEAD_DIM), HEAD_DIM ** -0.5),
        'nsa_pos_v': nrm((L, NSA_CMP_LEN, HEAD_DIM), 0.02),
        'nsa_w1_v': nrm((L, flat_cmp, HEAD_DIM), flat_cmp ** -0.5),
        'nsa_w2_v': nrm((L, HEAD_DIM, HEAD_DIM), HEAD_DIM ** -0.5),
        'w_gate': nrm((L, N_BRANCH, D_MODEL, D_MODEL), D_MODEL ** -0.5),
        'b_gate': nrm((L, N_BRANCH, D_MODEL), 0.01),
        'w_branch': nrm((L, N_BRANCH, MIX_WIDTH, D_MODEL), MIX_WIDTH ** -0.5),
        'w_out': nrm((L, D_MODEL, D_MODEL), D_MODEL ** -0.5),
        'ffn_norm_g': gain((L, D_MODEL)),
        'w_router_grp': nrm((L, D_MODEL, N_GROUPS), D_MODEL ** -0.5),
        'b_router_grp': nrm((L, N_GROUPS), ROUTER_BIAS_SCALE),
        'w_router_exp': nrm((L, D_MODEL, N_EXPERTS), D_MODEL ** -0.5),
        'b_router_exp': nrm((L, N_EXPERTS), ROUTER_BIAS_SCALE),
        'w_exp_gate': nrm((L, N_EXPERTS, D_MODEL, EXPERT_FF), D_MODEL ** -0.5),
        'w_exp_up': nrm((L, N_EXPERTS, D_MODEL, EXPERT_FF), D_MODEL ** -0.5),
        'w_exp_down': nrm((L, N_EXPERTS, EXPERT_FF, D_MODEL), EXPERT_FF ** -0.5),
    }

def reference(x, rel_bias, final_norm_g, mix_norm_g, w_in, conv_w, conv_b, lru_w_a, lru_b_a,
              lru_w_x, lru_b_x, lru_lambda, swa_sinks, diff_lq1, diff_lk1, diff_lq2, diff_lk2,
              diff_subln_g, nsa_pos_k, nsa_w1_k, nsa_w2_k, nsa_pos_v, nsa_w1_v, nsa_w2_v,
              w_gate, b_gate, w_branch, w_out, ffn_norm_g, w_router_grp, b_router_grp,
              w_router_exp, b_router_exp, w_exp_gate, w_exp_up, w_exp_down):
    Bsz, S, _ = x.shape
    bias_f = rel_bias.astype(jnp.float32)
    bias_swa = bias_f[:, :SWA_HEADS]
    bias_diff = bias_f[:, SWA_HEADS:SWA_HEADS + DIFF_HEADS]
    bias_nsa = bias_f[:, SWA_HEADS + DIFF_HEADS:]
    for l in range(DEPTH):
        h = rmsnorm(x, mix_norm_g[l])
        (a_x, a_g, b_q, b_k, b_v, c_q, c_k, c_v, d_q,
         d_kc, d_vc, d_ks, d_vs, d_kw, d_vw, d_g) = split_columns(h @ w_in[l])
        y_a = rglru_mixer(a_x, a_g, conv_w[l], conv_b[l], lru_w_a[l], lru_b_a[l],
                          lru_w_x[l], lru_b_x[l], lru_lambda[l])
        y_b = banded_attention(b_q.reshape(Bsz, S, SWA_HEADS, HEAD_DIM),
                               b_k.reshape(Bsz, S, SWA_KV_HEADS, HEAD_DIM),
                               b_v.reshape(Bsz, S, SWA_KV_HEADS, HEAD_DIM),
                               SWA_WINDOW, bias_swa, swa_sinks[l])
        y_c = diff_attention(c_q.reshape(Bsz, S, DIFF_HEADS, 2, DIFF_DIM),
                             c_k.reshape(Bsz, S, DIFF_HEADS, 2, DIFF_DIM),
                             c_v.reshape(Bsz, S, DIFF_HEADS, 2 * DIFF_DIM),
                             diff_lq1[l], diff_lk1[l], diff_lq2[l], diff_lk2[l],
                             diff_subln_g[l], diff_lambda_init(l), bias_diff)
        y_d = nsa_attention(d_q.reshape(Bsz, S, NSA_HEADS, HEAD_DIM), d_kc, d_vc, d_ks, d_vs,
                            d_kw, d_vw, d_g.reshape(Bsz, S, NSA_HEADS, 3),
                            nsa_pos_k[l], nsa_w1_k[l], nsa_w2_k[l],
                            nsa_pos_v[l], nsa_w1_v[l], nsa_w2_v[l], bias_nsa)
        ys = (y_a, y_b, y_c, y_d)
        merged = jnp.zeros_like(x)
        for br in range(N_BRANCH):
            gate = jax.nn.sigmoid(h @ w_gate[l, br] + b_gate[l, br])
            merged = merged + gate * (ys[br] @ w_branch[l, br])
        x = x + merged @ w_out[l]
        x = x + hier_moe(rmsnorm(x, ffn_norm_g[l]), w_router_grp[l], b_router_grp[l],
                         w_router_exp[l], b_router_exp[l], w_exp_gate[l], w_exp_up[l], w_exp_down[l])
    return rmsnorm(x, final_norm_g)


_drawn_inputs = setup_inputs


def setup_inputs(seed=0):
    import zlib

    import numpy as np

    out = dict(_drawn_inputs(seed))
    spreads = {}
    factors = {'final_norm_g': 3.011,
     'conv_b': 3.246,
     'lru_b_a': 8.0,
     'lru_b_x': 8.0,
     'swa_sinks': 8.0,
     'diff_lq1': 4.973,
     'diff_lq2': 2.905,
     'diff_lk2': 8.0,
     'diff_subln_g': 2.888,
     'nsa_pos_k': 8.0,
     'nsa_pos_v': 3.106,
     'b_gate': 8.0,
     'ffn_norm_g': 2.992,
     'b_router_grp': 3.123,
     'b_router_exp': 5.443}
    for name, (base, spread) in spreads.items():
        noise = np.random.default_rng([zlib.crc32(name.encode()), seed]).standard_normal(out[name].shape)
        drawn = base * np.exp(spread * noise) if base else spread * noise
        out[name] = jnp.asarray(drawn.astype(out[name].dtype))
    for name, factor in factors.items():
        out[name] = (out[name] * factor).astype(out[name].dtype)
    return out
```

```python
import math

import numpy as np

import concourse.bass as bass
from concourse import mybir
from contextlib import ExitStack

P = 128
S, D = 256, 1024
TT = S // P
KT = D // P
MW, DH = 256, 64
NH = 4
NB = 12
BUCKETS, MAXD = 32, 128
NCMP = (S - 32) // 16 + 1
E, GRP, EPG, FF = 32, 4, 8, 256
CAP = 64
PAIRS = E // 2
PASSES = S // CAP
NEG = -1e30
TINY = 1e-30
W_SLOT = 4096
SLOTS = 6
MW_BIAS = 512
IN_TAIL = 396
GELU_C, GELU_K = 0.044715, math.sqrt(2.0 / math.pi)
FAMILIES = ("swa", "diff0", "diff1", "sel", "win")

COLUMNS = [("ident", 128), ("mix_g", KT), ("tab", NB), ("onehot", MW_BIAS),
           ("conv_w", 8), ("conv_b", 2), ("b_a", 2), ("b_x", 2), ("lam", 2),
           ("subln_g", 1), ("b_gate", 32), ("sinks", NH), ("lq1", 32), ("lq2", 32), ("lk1", 32), ("lk2", 32),
           ("w_a", 128), ("w_x", 128), ("w2", DH), ("pos_k", 16), ("pos_v", 16),
           ("upper", 128), ("ones", 128), ("iota", CAP), ("iota8", 8), ("b_router", 36), ("w_router", KT * 36)]


def column_offsets(names):
    at, out = 0, {}
    for name, n in COLUMNS:
        if name in names:
            out[name] = (at, n)
            at += n
    return out, at


FIRST_PART = {"ident", "mix_g", "tab", "onehot"}
SECOND_PART = {name for name, _ in COLUMNS} - FIRST_PART

CHUNKS = ["in_a", "in_b", "in_tail", "w1", "in_cqk", "in_cvdq",
          "g00", "g01", "g10", "g11", "branch01", "branch23",
          "g20", "g30", "g21", "g31", "out0", "out1"]
CHUNK_SLOT = [0, 1, 2, 3, 4, 5, 0, 1, 2, 3, 4, 5, 0, 1, 2, 3, 0, 1]
CHUNK_LAST = {"in_a": "ag", "in_b": "bkvb", "in_tail": "vsg", "w1": "h1", "in_cqk": "ck", "in_cvdq": "dq",
              "g00": "g0_1", "g01": "g0_3", "g10": "g1_1", "g11": "g1_3", "branch01": "b3_1", "branch23": "b3_3",
              "g20": "g2_1", "g30": "g3_1", "g21": "g2_3", "g31": "g3_3", "out0": "x1_10", "out1": "x1_11"}
PAIR_SLOTS = ((2, 3, 4), (5, 0, 1))


def chunk_use(i):
    return CHUNK_SLOT[:i].count(CHUNK_SLOT[i])


def psum_items():
    ring, names = 6, []

    def fam(f):
        return [f"s_{f}_{part}" for part in ("a0", "a1", "b0", "b1")]

    def tps(f):
        return [f"tp_{f}_{h}" for h in range(NH)]
    order = (["vec", "xT0", "xT1", "xT2", "xT3", "ax", "ag", "bq", "bkvb", "kcks", "vsg"] + fam("swa")
             + ["h1", "cq", "ck", "lr", "lx"] + fam("diff0") + ["vc", "dq"] + fam("diff1")
             + ["g0_0", "g0_1"] + tps("swa") + ["kc2", "vc2", "sc_a", "sc_b"] + fam("sel") + ["g0_2", "g0_3"]
             + tps("diff") + ["oc"] + fam("win") + ["g1_0", "g1_1", "ycT"] + tps("sel")
             + ["tpc0", "tpc1", "g1_2", "g1_3"] + tps("win"))
    for n2 in range(4):
        order += [f"b{n2}_0", f"b{n2}_1", f"g2_{n2}", f"b{n2}_2", f"g3_{n2}", f"b{n2}_3"]
    order += ["x1_00", "x1_10", "x1_01", "x1_11", "hT0", "hT1", "hT2", "hT3", "rl", "rank"]
    for i, name in enumerate(order):
        names.append((name, i % ring))
    names += [("yb0", 6), ("yb1", 7), ("yd0", 6), ("yd1", 7)]
    by_head = ("yb0", "yb1", "oc")
    uses, fulls, out = [0] * 8, [0] * 8, {}
    for name, bank in names:
        fulls[bank] += name not in by_head
        out[name] = (bank, uses[bank], fulls[bank])
        uses[bank] += 1
    return out, uses


def decoder_layer(nc, pa, pb, w_in_full, w_in_tail, w1, w_gates, w_branch, w_out, w_moe, x, g_ffn, g_fin, out):
    f32 = mybir.dt.float32
    bf16 = mybir.dt.bfloat16
    i32 = mybir.dt.int32
    ALU = mybir.AluOpType
    ACT = mybir.ActivationFunctionType
    X = mybir.AxisListType.X

    ctx = ExitStack()
    with ctx:
        def sb(name, n, dt=f32, p=P):
            return ctx.enter_context(nc.sbuf_tensor(name, [p, n], dt))

        def sem(name):
            return ctx.enter_context(nc.semaphore(name))

        bias_rows = nc.dram_tensor("bias_rows", [NB, P, MW_BIAS], f32, kind="Internal")

        ring = sb("weight_slots", SLOTS * W_SLOT)
        slot = [ring[:, s * W_SLOT:(s + 1) * W_SLOT] for s in range(SLOTS)]
        offs_a, n_a = column_offsets(FIRST_PART)
        offs_b, n_b = column_offsets(SECOND_PART)
        par_a, par_b = sb("params_a", n_a), sb("params_b", n_b)

        def par(name):
            if name in offs_a:
                o, n = offs_a[name]
                return par_a[:, o:o + n]
            o, n = offs_b[name]
            return par_b[:, o:o + n]

        def cut(t, widths):
            at, parts = 0, []
            for n in widths:
                parts.append(t[:, at:at + n])
                at += n
            return parts

        x_sb = sb("x_sb", TT * D)
        hT = sb("hT", KT * S)
        gates = sb("gates", 2 * KT * S)
        shared = sb("shared", 3 * 1536 + 8 * 256 + 4 * 384)
        fam_buf = [shared[:, i * 1536:(i + 1) * 1536] for i in range(3)]
        bias8 = shared[:, 4608:4608 + 2048].rearrange("p (h j) -> p h j", h=8)
        bias4 = shared[:, 6656:6656 + 1536].rearrange("p (h j) -> p h j", h=4)
        xn = shared[:, 0:TT * D]
        merged = shared[:, 0:KT * S]
        branch_tmp = shared[:, 2048:2560]
        late_gate = shared[:, 2560:3072]
        (h2, xgT, tb0, tb1, he, silu_g, onehot_g, gc0, gc1, yexp) = cut(
            shared, [TT * D, KT * P, 512, 512, 256, 256, 256, 256, 256, D])
        h2T = hT
        x1 = x_sb
        gffn, gfin = gates[:, 0:D], gates[:, D:2 * D]
        x2 = gates[:, 2 * D:4 * D]
        lru_tr, lru_ti, lru_t, lru_s = cut(gates[:, 2048:4096], [512] * 4)
        ax, ag, xc = sb("ax", 2 * (S + 3)), sb("ag", 512), sb("xc", 512)
        lru_w = sb("lru_w", 512)
        ya = sb("ya", 512)
        yb = sb("yb", 512)
        bq, kb, cq, ck, dq = (sb(n, 512) for n in ("bq", "kb", "cq", "ck", "dq"))
        yd, yc = bq, cq
        ks2, kw2, kc2, vc2 = (sb(n, 256) for n in ("ks2", "kw2", "kc2", "vc2"))
        v_b, v_sw, v_c = sb("v_b", 256), sb("v_sw", 256), sb("v_c", 512)
        pt = sb("pt", 4 * 384)
        vec = pt[0:NB, 0:MW_BIAS]
        o_c = sb("o_c", 512)
        lru_scratch = o_c
        pc_s = sb("pc_s", 8 * 16)
        pcT = shared[0:16, 1536:2560]
        small = sb("small", 340)
        (ss, rt, rstd, lam4, sp2, sp_a, sp_b, sp_c, bga, bgx, fac, den, negm, mx, es, gsig, h1, h1a, h1b, kcT, vc_d,
         ssc, rc, cmx) = cut(
            small, [2, 2, 2, 8, 2, 2, 2, 2, 2, 2, 8, 40, 40, 40, 8, 24, 15, 15, 15, 15, 64, 8, 8, 8])
        bgh = sb("bgh", 32)
        gsubln = sb("gsubln", 1)
        route = pt[:, 0:510]
        (rlog, mgrp, cgrp, ogrp, gsum, gexp, ing, v1, v2, c8, o1, in2, o2, wts, comb, selm, slotv, cnt,
         cmax) = cut(route, [72, 2, 8, 8, 2, 64, 16, 2, 2, 16, 16, 16, 16, 8, 72, 72, 72, 36, 1])
        cmax_i = sb("cmax_i", 1, i32)
        zeros16 = sb("zeros16", P, bf16)

        psum = [ctx.enter_context(nc.psum_tensor(f"bank{b}", [P, 512], f32)) for b in range(8)]
        items, bank_uses = psum_items()

        params_a_in, params_b_in, norm_g_in = sem("params_a_in"), sem("params_b_in"), sem("norm_g_in")
        x_in = [sem(f"x_in{t}") for t in range(TT)]
        slot_full = [sem(f"slot_full{s}") for s in range(SLOTS)]
        bank_full = [sem(f"bank_full{b}") for b in range(8)]
        bank_free = [sem(f"bank_free{b}") for b in range(8)]
        vec_ready, rows_stored, bias_in = sem("vec_ready"), sem("rows_stored"), sem("bias_in")
        dve_step, act_step = sem("dve_step"), sem("act_step")
        squares_ready, ms_ready, root_ready, xn_ready, hT_a, hT_d = (
            sem(n) for n in ("squares_ready", "ms_ready", "root_ready", "xn_ready", "hT_a", "hT_d"))
        ax_ready, xc_ready, lru_par_ready, lru_tanh_ready, gelu_in, ya_ready = (
            sem(n) for n in ("ax_ready", "xc_ready", "lru_par_ready", "lru_tanh_ready", "gelu_in", "ya_ready"))
        bq_ready, kb_ready, kc_ready, ks_ready, cq_ready, ck_ready, dq_ready = (
            sem(n) for n in ("bq_ready", "kb_ready", "kc_ready", "ks_ready", "cq_ready", "ck_ready", "dq_ready"))
        dgate_raw, dgate_tanh = sem("dgate_raw"), sem("dgate_tanh")
        blocks_ready, h1_raw, h1_tanh, h1_ready, kc2_ready = (
            sem(n) for n in ("blocks_ready", "h1_raw", "h1_tanh", "h1_ready", "kc2_ready"))
        sp_in, sp_exp, lam_in, lam_exp = sem("sp_in"), sem("sp_exp"), sem("lam_in"), sem("lam_exp")
        neg_ready, exp_ready, p_ready = (sem(n) for n in ("neg_ready", "exp_ready", "p_ready"))
        cmp_in, cmp_exp, pc_ready, pcT_ready = (sem(n) for n in ("cmp_in", "cmp_exp", "pc_ready", "pcT_ready"))
        pt_ready, pt_used, v_ready = sem("pt_ready"), sem("pt_used"), sem("v_ready")
        oc_squares, oc_root, oc_ready = sem("oc_squares"), sem("oc_root"), sem("oc_ready")
        yb_ready, yc_ready, yd_ready = sem("yb_ready"), sem("yc_ready"), sem("yd_ready")
        gate_ready, late_used, merged_ready = sem("gate_ready"), sem("late_used"), sem("merged_ready")
        x1_ready, h2_ready, h2T_ready = sem("x1_ready"), sem("h2_ready"), sem("h2T_ready")
        grp_in, grp_exp, sel_ready, count_ready = (sem(n) for n in ("grp_in", "grp_exp", "sel_ready", "count_ready"))
        onehot_ready, gather_done, xg_a, xg_d, gu_done, silu_done, he_ready = (
            sem(n) for n in ("onehot_ready", "gather_done", "xg_a", "xg_d", "gu_done", "silu_done", "he_ready"))
        tr_done, tb_ready, scatter_done, down_done, yexp_a, yexp_d, pass_ready = (
            sem(n) for n in ("tr_done", "tb_ready", "scatter_done", "down_done", "yexp_a", "yexp_d", "pass_ready"))
        x2_ready, fin_in, fin_squares, fin_ms, fin_root, out_ready, out_stored = (
            sem(n) for n in ("x2_ready", "fin_in", "fin_squares", "fin_ms", "fin_root", "out_ready", "out_stored"))
        ax_pads, slots_moved = sem("ax_pads"), sem("slots_moved")
        weighted_ready, pass_primed = sem("weighted_ready"), sem("pass_primed")

        FAM_NO = {f: i for i, f in enumerate(FAMILIES)}
        FAM_BUF = {"swa": 0, "diff0": 1, "diff1": 2, "sel": 0, "win": 2}
        TP_FAMS = ("swa", "diff", "sel", "win")
        TP_BUF = {"swa": 0, "diff": 1, "sel": 0, "win": 2}

        def fam_q1(f):
            return fam_buf[FAM_BUF[f]][:, 0:1024].rearrange("p (h k) -> p h k", h=NH)

        def fam_q0(f):
            return fam_buf[FAM_BUF[f]][:, 1024:1536].rearrange("p (h k) -> p h k", h=NH)

        def expert_base(s):
            return CHUNK_SLOT.count(s)

        block = ctx.enter_context(nc.Block())

        @block.sync
        def _(sp):
            for t in range(TT):
                sp.dma_start(x_sb[:, t * D:(t + 1) * D], x[t * P:(t + 1) * P, :]).then_inc(x_in[t], 16)
            sources = {"in_a": w_in_full[0], "in_b": w_in_full[1], "in_cqk": w_in_full[2], "in_cvdq": w_in_full[3],
                       "in_tail": w_in_tail, "w1": w1, "branch01": w_branch[0], "branch23": w_branch[1],
                       "out0": w_out[0], "out1": w_out[1]}
            for br in range(4):
                for nh in range(2):
                    sources[f"g{br}{nh}"] = w_gates[2 * br + nh]
            last_in = {}

            def after_last_chunk(s):
                if s in last_in:
                    bank, _, full = items[CHUNK_LAST[last_in[s]]]
                    sp.wait_ge(bank_full[bank], full)

            for i, name in enumerate(CHUNKS):
                s = CHUNK_SLOT[i]
                after_last_chunk(s)
                src = sources[name]
                sp.dma_start(slot[s][:, 0:src.shape[1]], src).then_inc(slot_full[s], 16)
                last_in[s] = name
            for p in range(2):
                for j, s in enumerate(PAIR_SLOTS[p]):
                    after_last_chunk(s)
                    sp.dma_start(slot[s], w_moe[3 * p + j]).then_inc(slot_full[s], 16)

            def load_experts(c, first):
                with sp.Fori(first, PAIRS // 2) as it:
                    for p in range(2):
                        for j, s in enumerate(PAIR_SLOTS[p]):
                            sp.wait_ge(down_done if j == 2 else gu_done, it * 2 + c * PAIRS + (p - 1))
                            sp.dma_start(slot[s], w_moe[bass.ds(it * 6 + (3 * p + j), 1), :, :]
                                         .rearrange("o p n -> (o p) n")).then_inc(slot_full[s], 16)

            load_experts(0, 1)
            sp.wait_ge(count_ready, 1)
            most = sp.value_load(cmax_i[0:1, 0:1], min_val=0, max_val=S)
            with sp.If(most > CAP):
                with sp.Fori(1, PASSES) as c:
                    load_experts(c, 0)
            for t in range(TT):
                sp.wait_ge(out_ready, t + 1)
                sp.dma_start(out[t * P:(t + 1) * P, :], x2[:, t * D:(t + 1) * D]).then_inc(out_stored, 16)
            sp.wait_ge(out_stored, 16 * TT)

        @block.gpsimd
        def _(pool):
            pool.wait_ge(vec_ready, 1)
            pool.dma_start(bias_rows.ap(), vec.unsqueeze(1).broadcast_to([NB, P, MW_BIAS])).then_inc(rows_stored, 16)
            pool.wait_ge(rows_stored, 16)
            for heads, first, dst in ((8, 0, bias8), (4, 8, bias4)):
                src = bass.AP(tensor=bias_rows, offset=first * P * MW_BIAS + P - 1,
                              ap=[[MW_BIAS - 1, P], [P * MW_BIAS, heads], [1, dst.shape[2]]])
                pool.dma_start(dst, src).then_inc(bias_in, 16)
            pool.wait_ge(merged_ready, 4)
            for dst, src in ((gffn, g_ffn), (gfin, g_fin)):
                pool.dma_start(dst, src.partition_broadcast(P)).then_inc(norm_g_in, 16)

        @block.tensor
        def _(pe):
            mm = nc.tensor.matmul
            ident = par("ident")

            def begin(name):
                bank, use, _ = items[name]
                if use:
                    pe.wait_ge(bank_free[bank], use)
                return psum[bank]

            def end(name, last):
                last.then_inc(bank_full[items[name][0]], 1)

            def chunk(name):
                i = CHUNKS.index(name)
                pe.wait_ge(slot_full[CHUNK_SLOT[i]], 16 * (chunk_use(i) + 1))
                return slot[CHUNK_SLOT[i]]

            def hT_t(k, t):
                return hT[:, k * S + t * P:k * S + (t + 1) * P]

            def channels(dst, w, width, col, n=P):
                for k in range(KT):
                    last = mm(dst, w[:, k * width + col:k * width + col + n], hT[:, k * S:(k + 1) * S],
                              start=(k == 0), stop=(k == KT - 1))
                return last

            pe.wait_ge(params_a_in, 16)
            b = begin("vec")
            end("vec", mm(b[0:NB, :], par("tab")[0:BUCKETS + 2, :], par("onehot")[0:BUCKETS + 2, :],
                          start=True, stop=True))
            for j in range(4):
                b = begin(f"xT{j}")
                for k in (2 * j, 2 * j + 1):
                    for t in range(TT):
                        if j == 0 and k == 0:
                            pe.wait_ge(xn_ready, t + 1)
                        last = nc.tensor.transpose(b[:, (k % 2) * S + t * P:(k % 2) * S + (t + 1) * P],
                                                   xn[:, t * D + k * P:t * D + (k + 1) * P], ident)
                end(f"xT{j}", last)
            pe.wait_ge(hT_a, 2)
            pe.wait_ge(hT_d, 2)

            def two_blocks(name, w, width, cols):
                b = begin(name)
                for j, col in enumerate(cols):
                    last = channels(b[:, j * S:(j + 1) * S], w, width, col)
                end(name, last)
                return last

            def tokens(dst, w, width, t, col, n):
                for k in range(KT):
                    last = mm(dst, hT_t(k, t), w[:, k * width + col:k * width + col + n],
                              start=(k == 0), stop=(k == KT - 1))
                return last

            w = chunk("in_a")
            two_blocks("ax", w, 512, (0, P))
            last = two_blocks("ag", w, 512, (2 * P, 3 * P))
            w = chunk("in_b")
            two_blocks("bq", w, 512, (0, P))
            b = begin("bkvb")
            channels(b[:, 0:S], w, 512, 2 * P)
            for t in range(TT):
                last = tokens(b[:, S + t * P:S + (t + 1) * P], w, 512, t, 3 * P, P)
            end("bkvb", last)
            w = chunk("in_tail")
            two_blocks("kcks", w, IN_TAIL, (0, P))
            b = begin("vsg")
            for t in range(TT):
                tokens(b[:, t * P:(t + 1) * P], w, IN_TAIL, t, 2 * P, P)
            for t in range(TT):
                last = tokens(b[:, S + t * NB:S + (t + 1) * NB], w, IN_TAIL, t, 384, NB)
            end("vsg", last)

            def scores(f, q, k_of, d, rows_of):
                for part, heads in (("a", (0, 2)), ("b", (1, 3))):
                    b0, b1 = begin(f"s_{f}_{part}0"), begin(f"s_{f}_{part}1")
                    for j, h in enumerate(heads):
                        r, c = rows_of(h)
                        last0 = mm(b0[:, j * P:(j + 1) * P], q[r:r + d, c:c + P], k_of(h)[:, 0:P],
                                   start=True, stop=True)
                        last1 = mm(b1[:, j * S:(j + 1) * S], q[r:r + d, c + P:c + S], k_of(h), start=True, stop=True)
                    end(f"s_{f}_{part}0", last0)
                    end(f"s_{f}_{part}1", last1)

            def rows64(h):
                return DH * (h % 2), S * (h // 2)

            pe.wait_ge(bq_ready, 1)
            pe.wait_ge(kb_ready, 1)
            scores("swa", bq, lambda h: kb[DH * (h % 2):DH * (h % 2) + DH, S * (h // 2):S * (h // 2) + S], DH, rows64)

            w = chunk("w1")
            pe.wait_ge(blocks_ready, 1)
            b = begin("h1")
            for kv, src in enumerate((kc2, vc2)):
                src3 = src[:, :].rearrange("p (c i) -> p i c", i=16)
                for i in range(16):
                    last = mm(b[kv * DH:(kv + 1) * DH, 0:NCMP], w[:, kv * 1024 + i * DH:kv * 1024 + (i + 1) * DH],
                              src3[:, i, 0:NCMP], start=(i == 0), stop=(i == 15))
            end("h1", last)

            w = chunk("in_cqk")
            two_blocks("cq", w, 512, (0, P))
            two_blocks("ck", w, 512, (2 * P, 3 * P))

            pe.wait_ge(params_b_in, 16)
            pe.wait_ge(xc_ready, 1)
            for name, wname in (("lr", "w_a"), ("lx", "w_x")):
                b = begin(name)
                for cb in range(2):
                    for half in range(2):
                        r = DH * half
                        last = mm(b[r:r + DH, cb * S:(cb + 1) * S], par(wname)[r:r + DH, cb * DH:(cb + 1) * DH],
                                  xc[r:r + DH, cb * S:(cb + 1) * S], start=True, stop=True)
                end(name, last)

            def diff_scores(m):
                def k_of(h):
                    r = DH * (h % 2) + 32 * m
                    return ck[r:r + 32, S * (h // 2):S * (h // 2) + S]
                scores(f"diff{m}", cq, k_of, 32, lambda h: (DH * (h % 2) + 32 * m, S * (h // 2)))

            pe.wait_ge(cq_ready, 1)
            pe.wait_ge(ck_ready, 1)
            diff_scores(0)
            w = chunk("in_cvdq")
            b = begin("vc")
            for t in range(TT):
                last = tokens(b[:, t * 256:(t + 1) * 256], w, 512, t, 0, 256)
            end("vc", last)
            two_blocks("dq", w, 512, (2 * P, 3 * P))
            diff_scores(1)

            def gate_item(br, n2):
                nh = n2 // 2
                w = chunk(f"g{br}{nh}")
                two_blocks(f"g{br}_{n2}", w, 512, ((n2 % 2) * 256, (n2 % 2) * 256 + P))

            def transposes(f, h):
                if h == 0:
                    pe.wait_ge(p_ready, TP_FAMS.index(f) + 1)
                buf = fam_buf[TP_BUF[f]]
                b = begin(f"tp_{f}_{h}")
                nc.tensor.transpose(b[:, 0:P], buf[:, 1024 + h * P:1024 + (h + 1) * P], ident)
                nc.tensor.transpose(b[:, P:2 * P], buf[:, h * S:h * S + P], ident)
                last = nc.tensor.transpose(b[:, 2 * P:3 * P], buf[:, h * S + P:(h + 1) * S], ident)
                end(f"tp_{f}_{h}", last)

            def pt_of(f, h):
                u = TP_FAMS.index(f) * NH + h
                pe.wait_ge(pt_ready, u + 1)
                return pt[:, (u % 4) * 384:(u % 4 + 1) * 384]

            def values(dst, f, h, v_of, start=True, stop=True):
                p = pt_of(f, h)
                mm(dst[:, 0:S], v_of(0), p[:, 0:S], start=start, stop=False)
                mm(dst[:, P:S], v_of(1), p[:, S:S + P], start=False, stop=stop).then_inc(pt_used, 1)

            gate_item(0, 0)
            gate_item(0, 1)
            pe.wait_ge(v_ready, 3)
            yb_bank = [begin("yb0"), begin("yb1")]

            def swa_values(h):
                r = DH * (h % 2)
                values(yb_bank[h // 2][r:r + DH, :], "swa", h,
                       lambda t: v_b[:, t * P + DH * (h // 2):t * P + DH * (h // 2) + DH])

            transposes("swa", 0)
            for h in range(1, NH):
                transposes("swa", h)
                swa_values(h - 1)
            swa_values(NH - 1)

            pe.wait_ge(h1_ready, 1)
            b = begin("kc2")
            mm(b[0:DH, 0:NCMP], par("w2")[0:DH, :], h1b[0:DH, :], start=True, stop=True)
            last = mm(b[DH:P, 0:NCMP], par("w2")[0:DH, :], h1b[0:DH, :], start=True, stop=True)
            end("kc2", last)
            b = begin("vc2")
            end("vc2", mm(b[0:NCMP, 0:DH], h1b[DH:P, :], par("w2")[DH:P, :], start=True, stop=True))
            pe.wait_ge(kc2_ready, 1)
            pe.wait_ge(dq_ready, 1)
            for part, heads in (("a", (0, 2)), ("b", (1, 3))):
                b = begin(f"sc_{part}")
                for t in range(TT):
                    for j, h in enumerate(heads):
                        r, c = rows64(h)
                        last = mm(b[:, (t * 2 + j) * 16:(t * 2 + j) * 16 + NCMP],
                                  dq[r:r + DH, c + t * P:c + (t + 1) * P], kcT[r:r + DH, :], start=True, stop=True)
                end(f"sc_{part}", last)
            pe.wait_ge(ks_ready, 1)
            scores("sel", dq, lambda h: ks2[DH * (h % 2):DH * (h % 2) + DH, :], DH, rows64)
            pe.wait_ge(yb_ready, 2)
            gate_item(0, 2)
            gate_item(0, 3)

            transposes("diff", 0)
            oc_bank = None

            def diff_values(h):
                p = pt_of("diff", h)
                mm(oc_bank[:, h * DH:(h + 1) * DH], p[:, 0:P], v_c[:, h * DH:(h + 1) * DH], start=True, stop=True)
                mm(oc_bank[:, 256 + h * DH:256 + (h + 1) * DH], p[:, P:2 * P], v_c[:, h * DH:(h + 1) * DH],
                   start=True, stop=False)
                return mm(oc_bank[:, 256 + h * DH:256 + (h + 1) * DH], p[:, 2 * P:3 * P],
                          v_c[:, 256 + h * DH:256 + (h + 1) * DH], start=False, stop=True).then_inc(pt_used, 1)

            for h in range(1, NH):
                transposes("diff", h)
            oc_bank = begin("oc")
            for h in range(NH):
                diff_values(h)
            scores("win", dq, lambda h: kw2[DH * (h % 2):DH * (h % 2) + DH, :], DH, rows64)
            gate_item(1, 0)
            gate_item(1, 1)
            pe.wait_ge(oc_ready, 1)
            b = begin("ycT")
            for j in range(2):
                for t in range(TT):
                    last = nc.tensor.transpose(b[:, j * S + t * P:j * S + (t + 1) * P],
                                               o_c[:, t * 256 + j * P:t * 256 + (j + 1) * P], ident)
            end("ycT", last)

            yd_bank = [begin("yd0"), begin("yd1")]

            def nsa_values(f, h, v_at, start):
                r = DH * (h % 2)
                values(yd_bank[h // 2][r:r + DH, :], f, h,
                       lambda t: v_sw[:, t * P + v_at:t * P + v_at + DH], start=start, stop=False)

            transposes("sel", 0)
            for h in range(1, NH):
                transposes("sel", h)
                nsa_values("sel", h - 1, 0, True)
            nsa_values("sel", NH - 1, 0, True)
            pe.wait_ge(pc_ready, 1)
            for j in range(2):
                b = begin(f"tpc{j}")
                for h in (2 * j, 2 * j + 1):
                    for t in range(TT):
                        last = nc.tensor.transpose(b[0:NCMP, (h % 2) * S + t * P:(h % 2) * S + (t + 1) * P],
                                                   pc_s[:, (t * NH + h) * 16:(t * NH + h) * 16 + NCMP], ident)
                end(f"tpc{j}", last)
            gate_item(1, 2)
            gate_item(1, 3)
            transposes("win", 0)
            for h in range(1, NH):
                transposes("win", h)
                nsa_values("win", h - 1, DH, False)
            nsa_values("win", NH - 1, DH, False)
            pe.wait_ge(pcT_ready, 2)
            for h in range(NH):
                r = DH * (h % 2)
                last = mm(yd_bank[h // 2][r:r + DH, 0:S], vc_d[0:NCMP, :], pcT[0:NCMP, h * S:(h + 1) * S],
                          start=False, stop=True)
                if h % 2:
                    last.then_inc(bank_full[6 + h // 2], 1)

            ys = (ya, yb, yc, yd)
            pe.wait_ge(ya_ready, 1)
            pe.wait_ge(yb_ready, 2)
            for n2 in range(4):
                for br in range(4):
                    if br >= 2:
                        gate_item(br, n2)
                    if n2 == 0 and br == 2:
                        pe.wait_ge(yc_ready, 1)
                    if n2 == 0 and br == 3:
                        pe.wait_ge(yd_ready, 2)
                    w = chunk("branch01" if br < 2 else "branch23")
                    b = begin(f"b{n2}_{br}")
                    for j in range(2):
                        n = 2 * n2 + j
                        for k in range(2):
                            last = mm(b[:, j * S:(j + 1) * S], w[:, (br % 2) * 2048 + k * D + n * P:
                                                                 (br % 2) * 2048 + k * D + (n + 1) * P],
                                      ys[br][:, k * S:(k + 1) * S], start=(k == 0), stop=(k == 1))
                    end(f"b{n2}_{br}", last)
            pe.wait_ge(merged_ready, 4)
            for nh in range(2):
                w = chunk(f"out{nh}")
                for t in range(TT):
                    b = begin(f"x1_{t}{nh}")
                    for k in range(KT):
                        last = mm(b[:, :], merged[:, k * S + t * P:k * S + (t + 1) * P],
                                  w[:, k * 512:(k + 1) * 512], start=(k == 0), stop=(k == KT - 1))
                    end(f"x1_{t}{nh}", last)

            pe.wait_ge(h2_ready, 2)
            for j in range(4):
                b = begin(f"hT{j}")
                for k in (2 * j, 2 * j + 1):
                    for t in range(TT):
                        last = nc.tensor.transpose(b[:, (k % 2) * S + t * P:(k % 2) * S + (t + 1) * P],
                                                   h2[:, t * D + k * P:t * D + (k + 1) * P], ident)
                end(f"hT{j}", last)
            pe.wait_ge(h2T_ready, 4)
            b = begin("rl")
            for t in range(TT):
                for k in range(KT):
                    last = mm(b[:, t * 36:(t + 1) * 36], hT_t(k, t), par("w_router")[:, k * 36:(k + 1) * 36],
                              start=(k == 0), stop=(k == KT - 1))
            end("rl", last)
            pe.wait_ge(sel_ready, 1)
            b = begin("rank")
            sel3 = selm.rearrange("p (t e) -> p t e", t=TT)
            mm(b[:, 0:36], par("upper"), sel3[:, 0, :], start=True, stop=True)
            mm(b[:, 36:72], par("ones"), sel3[:, 0, :], start=True, stop=False)
            mm(b[:, 36:72], par("upper"), sel3[:, 1, :], start=False, stop=True)
            mm(b[:, 72:108], par("ones"), sel3[:, 0, :], start=True, stop=False)
            last = mm(b[:, 72:108], par("ones"), sel3[:, 1, :], start=False, stop=True)
            end("rank", last)

            y_bank, gu_bank, tr_bank, cd = psum[0:4], psum[4], psum[5], psum[6:8]
            for bk in range(8):
                if bank_uses[bk]:
                    pe.wait_ge(bank_free[bk], bank_uses[bk])
            pe.wait_ge(pass_ready, 1)
            zeros512 = zeros16[:, :].unsqueeze(1).broadcast_to([P, 4, P])
            for bk in y_bank:
                mm(bk[:, :], zeros16[:, :], zeros512, start=True, stop=False, skip_group_check=True)

            def gather(one_hots):
                pe.wait_ge(onehot_ready, one_hots)
                for k in range(KT):
                    for t in range(TT):
                        last = mm(cd[k // 4][:, (k % 4) * P:(k % 4 + 1) * P],
                                  h2[:, t * D + k * P:t * D + (k + 1) * P], onehot_g[:, t * P:(t + 1) * P],
                                  start=(t == 0), stop=(t == 1))
                last.then_inc(gather_done, 1)

            def scatter(tb, stop=False):
                for t in range(TT):
                    for nh in range(2):
                        last = mm(y_bank[2 * t + nh][:, :], tb[:, 256 + t * P:256 + (t + 1) * P],
                                  yexp[:, nh * 512:(nh + 1) * 512], start=False, stop=stop, skip_group_check=True)
                return last

            tbs = (tb0, tb1)

            def expert_pass(c):
                n17 = c * 17
                pe.wait_ge(pass_ready, c + 1)
                gather(c * 18 + 1)
                with pe.Fori(0, PAIRS // 2) as it:
                    for p in range(2):
                        i = it * 2 + p
                        s_gu, s_dn = PAIR_SLOTS[p][0:2], PAIR_SLOTS[p][2]
                        pe.wait_ge(xg_a, i + n17 + 1)
                        pe.wait_ge(xg_d, i + n17 + 1)
                        pe.wait_ge(he_ready, i + c * PAIRS + 1)
                        for s in s_gu:
                            pe.wait_ge(slot_full[s], (it + (c * (PAIRS // 2) + expert_base(s) + 1)) * 16)
                        for k in range(KT):
                            for e in range(2):
                                last = mm(gu_bank[e * CAP:(e + 1) * CAP, :],
                                          xgT[:, k * P + e * CAP:k * P + (e + 1) * CAP],
                                          slot[s_gu[e]][:, k * 512:(k + 1) * 512],
                                          start=(k == 0), stop=(k == KT - 1))
                        last.then_inc(gu_done, 1)
                        pe.wait_ge(yexp_a, i + c * PAIRS + 1)
                        pe.wait_ge(yexp_d, i + c * PAIRS + 1)
                        gather(i + c * 18 + 2)
                        pe.wait_ge(he_ready, i + c * PAIRS + 2)
                        pe.wait_ge(tb_ready, i + c * PAIRS + 1)
                        gc = (gc0, gc1)[p]
                        for j in range(2):
                            nc.tensor.transpose(tr_bank[:, j * P:(j + 1) * P], he[:, j * P:(j + 1) * P], ident)
                        for t in range(TT):
                            last = nc.tensor.transpose(tr_bank[:, 256 + t * P:256 + (t + 1) * P],
                                                       gc[:, t * P:(t + 1) * P], ident)
                        last.then_inc(tr_done, 1)
                        scatter(tbs[1 - p]).then_inc(scatter_done, 1)
                        pe.wait_ge(tb_ready, i + c * PAIRS + 2)
                        pe.wait_ge(xg_a, i + n17 + 2)
                        pe.wait_ge(xg_d, i + n17 + 2)
                        pe.wait_ge(slot_full[s_dn], (it + (c * (PAIRS // 2) + expert_base(s_dn) + 1)) * 16)
                        tb = tbs[p]
                        for nh in range(2):
                            for j in range(2):
                                for e in range(2):
                                    last = mm(cd[nh][e * CAP:(e + 1) * CAP, :],
                                              tb[:, j * P + e * CAP:j * P + (e + 1) * CAP],
                                              slot[s_dn][:, e * 2048 + j * D + nh * 512:e * 2048 + j * D + (nh + 1) * 512],
                                              start=(j == 0), stop=(j == 1))
                        last.then_inc(down_done, 1)
                n = c * PAIRS + PAIRS
                pe.wait_ge(yexp_a, n + 1)
                pe.wait_ge(yexp_d, n + 1)
                scatter(tb1).then_inc(scatter_done, 1)

            expert_pass(0)
            pe.wait_ge(count_ready, 1)
            most = pe.value_load(cmax_i[0:1, 0:1], min_val=0, max_val=S)
            with pe.If(most > CAP):
                with pe.Fori(1, PASSES) as c:
                    expert_pass(c)
            for bk in y_bank:
                last = mm(bk[:, :], zeros16[:, :], zeros512, start=False, stop=True, skip_group_check=True)
            last.then_inc(x2_ready, 1)

        @block.scalar
        def _(act):
            step = [0]

            def link(ins):
                step[0] += 1
                ins.then_inc(act_step, 1)
                act.wait_ge(act_step, step[0])

            f = nc.scalar.activation

            def full(name):
                bank, _, value = items[name]
                act.wait_ge(bank_full[bank], value)
                return psum[bank]

            def free(name):
                return bank_free[items[name][0]]

            act.dma_start(par_a[:, :], pa).then_inc(params_a_in, 16)
            act.dma_start(par_b[:, :], pb).then_inc(params_b_in, 16)
            for t in range(TT):
                act.wait_ge(x_in[t], 16)
                f(xn[:, t * D:(t + 1) * D], x_sb[:, t * D:(t + 1) * D], ACT.Square,
                  accum_out=ss[:, t:t + 1]).then_inc(squares_ready, 1)
            act.wait_ge(ms_ready, 1)
            f(rt[:, :], ss[:, :], ACT.Sqrt).then_inc(root_ready, 1)
            act.wait_ge(sp_in, 1)
            f(sp_b[:, :], sp_a[:, :], ACT.Exp).then_inc(sp_exp, 1)
            act.wait_ge(lam_in, 1)
            f(lam4[:, 2:4], lam4[:, 0:2], ACT.Exp).then_inc(lam_exp, 1)

            def h_transposed(j):
                b = full(f"xT{j}")
                f(hT[:, 2 * j * S:(2 * j + 1) * S], b[:, 0:S], ACT.Copy, scale=par("mix_g")[:, 2 * j:2 * j + 1])
                f(hT[:, (2 * j + 1) * S:(2 * j + 2) * S], b[:, S:2 * S], ACT.Copy,
                  scale=par("mix_g")[:, 2 * j + 1:2 * j + 2]).then_inc(free(f"xT{j}"), 1)
                act.wait_ge(free(f"xT{j}"), items[f"xT{j}"][1] + 1)
                act.sem_inc(hT_a, 1)

            act.wait_ge(params_a_in, 16)
            h_transposed(0)
            h_transposed(2)
            act.wait_ge(ax_pads, 1)
            b = full("ax")
            f(ax[:, :].rearrange("p (c s) -> p c s", c=2)[:, :, 3:S + 3], b[:, :].rearrange("p (c s) -> p c s", c=2),
              ACT.Copy).then_inc(free("ax"), 1)
            act.wait_ge(free("ax"), items["ax"][1] + 1)
            act.sem_inc(ax_ready, 1)

            def copy_out(name, dst, ready):
                b = full(name)
                f(dst[:, :], b[:, :], ACT.Copy).then_inc(free(name), 1)
                act.wait_ge(free(name), items[name][1] + 1)
                act.sem_inc(ready, 1)

            copy_out("bq", bq, bq_ready)
            b = full("kcks")
            for half in range(2):
                r = half * DH
                f(kc2[r:r + DH, :], b[0:DH, 0:S], ACT.Copy)
                f(vc2[r:r + DH, :], b[DH:P, 0:S], ACT.Copy)
                f(ks2[r:r + DH, :], b[0:DH, S:2 * S], ACT.Copy)
                last = f(kw2[r:r + DH, :], b[DH:P, S:2 * S], ACT.Copy)
            last.then_inc(free("kcks"), 1)
            act.wait_ge(free("kcks"), items["kcks"][1] + 1)
            act.sem_inc(kc_ready, 1)
            act.sem_inc(ks_ready, 1)
            act.wait_ge(dgate_raw, 1)
            f(gsig[:, :], gsig[:, :], ACT.Tanh, scale=0.5).then_inc(dgate_tanh, 1)

            def exps(fam):
                n = FAM_NO[fam]
                act.wait_ge(neg_ready, n + 1)
                for j, (probs, o) in enumerate(((fam_q1(fam), 0), (fam_q0(fam), 4))):
                    for h in range(NH):
                        c = n * 8 + o + h
                        last = f(probs[:, h, :], probs[:, h, :], ACT.Exp, bias=negm[:, c:c + 1],
                                 accum_out=den[:, c:c + 1])
                if fam == "swa":
                    last.then_inc(act_step, 1)
                    step[0] += 1
                    act.wait_ge(act_step, step[0])
                    last = f(es[:, :], es[:, :], ACT.Exp)
                last.then_inc(exp_ready, 1)

            exps("swa")
            act.wait_ge(h1_raw, 1)
            f(h1a[:, :], h1a[:, :], ACT.Tanh, scale=GELU_K).then_inc(h1_tanh, 1)
            copy_out("cq", cq, cq_ready)
            act.wait_ge(lru_par_ready, 1)
            act.wait_ge(gelu_in, 1)
            f(lru_w[:, :], lru_w[:, :], ACT.Tanh, scale=GELU_K)
            for name, dst, bias in (("lr", lru_tr, bga), ("lx", lru_ti, bgx)):
                b = full(name)
                for cb in range(2):
                    last = f(dst[:, cb * S:(cb + 1) * S], b[:, cb * S:(cb + 1) * S], ACT.Tanh, scale=0.5,
                             bias=bias[:, cb:cb + 1])
                last.then_inc(free(name), 1)
                act.wait_ge(free(name), items[name][1] + 1)
            for cb in range(2):
                last = f(lru_t[:, cb * S:(cb + 1) * S], lru_tr[:, cb * S:(cb + 1) * S], ACT.Tanh,
                         scale=sp2[:, cb:cb + 1], bias=sp2[:, cb:cb + 1])
            link(last)
            exps("diff0")
            copy_out("dq", dq, dq_ready)
            exps("diff1")
            f(lru_s[:, :], lru_t[:, :], ACT.Sqrt).then_inc(lru_tanh_ready, 1)

            gate_no = [0]

            def gate_tanh(br, n2, dst):
                b = full(f"g{br}_{n2}")
                for j in range(2):
                    n = 2 * n2 + j
                    last = f(dst[:, j * S:(j + 1) * S], b[:, j * S:(j + 1) * S], ACT.Tanh, scale=0.5,
                             bias=bgh[:, br * KT + n:br * KT + n + 1])
                last.then_inc(free(f"g{br}_{n2}"), 1)
                act.wait_ge(free(f"g{br}_{n2}"), items[f"g{br}_{n2}"][1] + 1)
                act.sem_inc(gate_ready, 1)

            def early_gate(br, n2):
                gate_tanh(br, n2, gates[:, br * KT * S + n2 * 512:br * KT * S + (n2 + 1) * 512])

            def probs_out(fam, h):
                u = TP_FAMS.index(fam) * NH + h
                b = full(f"tp_{fam}_{h}")
                if u >= 4:
                    act.wait_ge(pt_used, u - 3)
                f(pt[:, (u % 4) * 384:(u % 4 + 1) * 384], b[:, 0:384], ACT.Copy).then_inc(pt_ready, 1)
                act.wait_ge(pt_ready, u + 1)
                act.sem_inc(free(f"tp_{fam}_{h}"), 1)

            early_gate(0, 0)
            early_gate(0, 1)
            act.wait_ge(bias_in, 32)
            for h in range(NH):
                probs_out("swa", h)
            exps("sel")
            act.wait_ge(cmp_in, 1)
            f(pc_s[:, :].rearrange("p (a c) -> p a c", c=16)[:, :, 0:NCMP],
              pc_s[:, :].rearrange("p (a c) -> p a c", c=16)[:, :, 0:NCMP], ACT.Exp).then_inc(cmp_exp, 1)
            early_gate(0, 2)
            early_gate(0, 3)
            for h in range(NH):
                probs_out("diff", h)
            act.wait_ge(oc_squares, 1)
            f(rc[:, :], ssc[:, :], ACT.Sqrt).then_inc(oc_root, 1)
            exps("win")
            act.wait_ge(ya_ready, 1)
            early_gate(1, 0)
            early_gate(1, 1)
            for h in range(NH):
                probs_out("sel", h)
            for j in range(2):
                b = full(f"tpc{j}")
                f(pcT[0:NCMP, j * 512:(j + 1) * 512], b[0:NCMP, :], ACT.Copy).then_inc(free(f"tpc{j}"), 1)
                act.wait_ge(free(f"tpc{j}"), items[f"tpc{j}"][1] + 1)
                act.sem_inc(pcT_ready, 1)
            early_gate(1, 2)
            early_gate(1, 3)
            for h in range(NH):
                probs_out("win", h)
            for n2 in range(4):
                for br in (2, 3):
                    n = 2 * n2 + br - 2
                    if n:
                        act.wait_ge(late_used, n)
                    else:
                        act.wait_ge(pt_used, 12)
                    gate_tanh(br, n2, late_gate)
            for t in range(TT):
                act.wait_ge(x1_ready, 2 * (t + 1) if t else 3)
                f(x2[:, t * D:(t + 1) * D], x1[:, t * D:(t + 1) * D], ACT.Square,
                  accum_out=ss[:, t:t + 1]).then_inc(squares_ready, 1)
            act.wait_ge(ms_ready, 2)
            f(rt[:, :], ss[:, :], ACT.Sqrt).then_inc(root_ready, 1)
            for j in (0, 2):
                b = full(f"hT{j}")
                f(h2T[:, 2 * j * S:(2 * j + 2) * S], b[:, :], ACT.Copy).then_inc(free(f"hT{j}"), 1)
                act.wait_ge(free(f"hT{j}"), items[f"hT{j}"][1] + 1)
                act.sem_inc(h2T_ready, 1)
            act.wait_ge(grp_in, 1)
            f(gexp[:, 0:10], gexp[:, 0:10], ACT.Exp).then_inc(grp_exp, 1)

            gu_bank, cd = psum[4], psum[6:8]

            def expert_pass(c):
                def tokens_out(n):
                    act.wait_ge(gather_done, n)
                    f(xgT[:, 0:512], cd[0][:, :], ACT.Copy).then_inc(xg_a, 1)

                tokens_out(c * 17 + 1)
                with act.Fori(0, PAIRS // 2) as it:
                    for p in range(2):
                        i = it * 2 + p
                        act.wait_ge(gu_done, i + c * PAIRS + 1)
                        act.wait_ge(he_ready, i + c * PAIRS + 1)
                        f(silu_g[:, :], gu_bank[:, 0:FF], ACT.Silu).then_inc(silu_done, 1)
                        tokens_out(i + c * 17 + 2)
                        act.wait_ge(down_done, i + c * PAIRS + 1)
                        f(yexp[:, 0:512], cd[0][:, :], ACT.Copy).then_inc(yexp_a, 1)

            act.sem_inc(yexp_a, 1)
            expert_pass(0)
            act.wait_ge(count_ready, 1)
            most = act.value_load(cmax_i[0:1, 0:1], min_val=0, max_val=S)
            with act.If(most > CAP):
                with act.Fori(1, PASSES) as c:
                    expert_pass(c)
            for t in range(TT):
                act.wait_ge(fin_in, t + 1)
                f(h2[:, t * D:(t + 1) * D], x2[:, t * D:(t + 1) * D], ACT.Square,
                  accum_out=ss[:, t:t + 1]).then_inc(fin_squares, 1)
            act.wait_ge(fin_ms, 1)
            f(rt[:, :], ss[:, :], ACT.Sqrt).then_inc(fin_root, 1)

        @block.vector
        def _(dve):
            v = nc.vector
            step = [0]

            def link(ins):
                step[0] += 1
                ins.then_inc(dve_step, 1)
                dve.wait_ge(dve_step, step[0])

            counts = {}

            def tell(ins, s):
                counts[s.name] = counts.get(s.name, 0) + 1
                ins.then_inc(s, 1)
                dve.wait_ge(s, counts[s.name])

            def full(name):
                bank, _, value = items[name]
                dve.wait_ge(bank_full[bank], value)
                return psum[bank]

            def release(name, ins):
                bank, use, _ = items[name]
                ins.then_inc(bank_free[bank], 1)
                dve.wait_ge(bank_free[bank], use + 1)

            def mean_root(n):
                dve.wait_ge(squares_ready, 2 * n)
                tell(v.tensor_scalar(ss[:, :], ss[:, :], 1.0 / D, 1e-6, ALU.mult, ALU.add), ms_ready)
                dve.wait_ge(root_ready, n)
                link(v.reciprocal(rstd[:, :], rt[:, :]))

            tell(v.memset(ax[:, :].rearrange("p (c s) -> p c s", c=2)[:, :, 0:3], 0.0), ax_pads)
            link(v.memset(zeros16[:, :], 0.0))
            b = full("vec")
            release("vec", v.tensor_copy(vec, b[0:NB, :]))
            dve.sem_inc(vec_ready, 1)
            mean_root(1)
            for t in range(TT):
                tell(v.tensor_scalar(xn[:, t * D:(t + 1) * D], x_sb[:, t * D:(t + 1) * D], rstd[:, t:t + 1], None,
                                     ALU.mult), xn_ready)
            dve.wait_ge(params_b_in, 16)
            link(v.tensor_scalar(sp_c[:, :], par("lam"), -1.0, None, ALU.mult))
            tell(v.tensor_tensor(sp_a[:, :], par("lam"), sp_c[:, :], ALU.min), sp_in)
            link(v.tensor_tensor(lru_scratch[:, 0:32], par("lq1"), par("lk1"), ALU.mult))
            link(v.tensor_tensor(lru_scratch[:, 32:64], par("lq2"), par("lk2"), ALU.mult))
            tell(v.reduce_sum(lam4[:, 0:2], lru_scratch[:, 0:64].rearrange("p (a b) -> p a b", a=2), axis=X), lam_in)
            link(v.tensor_scalar(bga[:, :], par("b_a"), 0.5, None, ALU.mult))
            link(v.tensor_scalar(bgx[:, :], par("b_x"), 0.5, None, ALU.mult))
            link(v.tensor_scalar(bgh[:, :], par("b_gate"), 0.5, None, ALU.mult))
            link(v.tensor_scalar(gsubln[:, :], par("subln_g"), 0.8, None, ALU.mult))

            def h_transposed(j):
                b = full(f"xT{j}")
                link(v.tensor_scalar(hT[:, 2 * j * S:(2 * j + 1) * S], b[:, 0:S], par("mix_g")[:, 2 * j:2 * j + 1],
                                     None, ALU.mult))
                release(f"xT{j}", v.tensor_scalar(hT[:, (2 * j + 1) * S:(2 * j + 2) * S], b[:, S:2 * S],
                                                  par("mix_g")[:, 2 * j + 1:2 * j + 2], None, ALU.mult))
                dve.sem_inc(hT_d, 1)

            h_transposed(1)
            h_transposed(3)
            dve.wait_ge(sp_exp, 1)
            link(v.tensor_scalar(sp_a[:, :], sp_b[:, :], 2.0, None, ALU.add))
            link(v.reciprocal(sp_a[:, :], sp_a[:, :]))
            link(v.tensor_tensor(sp_a[:, :], sp_a[:, :], sp_b[:, :], ALU.mult))
            link(v.tensor_tensor(sp_b[:, :], sp_a[:, :], sp_a[:, :], ALU.mult))
            link(v.tensor_scalar(sp2[:, :], sp_b[:, :], 1.0 / 17, 1.0 / 15, ALU.mult, ALU.add))
            for n in (13, 11, 9, 7, 5, 3, 1):
                link(v.tensor_tensor(sp2[:, :], sp2[:, :], sp_b[:, :], ALU.mult))
                link(v.tensor_scalar(sp2[:, :], sp2[:, :], 1.0 / n, None, ALU.add))
            link(v.tensor_tensor(sp2[:, :], sp2[:, :], sp_a[:, :], ALU.mult))
            link(v.tensor_scalar(sp_c[:, :], sp_c[:, :], 0.0, None, ALU.max))
            link(v.tensor_scalar(sp2[:, :], sp2[:, :], 2.0, None, ALU.mult))
            link(v.tensor_tensor(sp2[:, :], sp2[:, :], sp_c[:, :], ALU.add))
            tell(v.tensor_scalar(sp2[:, :], sp2[:, :], 2.0, None, ALU.mult), lru_par_ready)
            dve.wait_ge(lam_exp, 1)
            link(v.tensor_tensor(lam4[:, 4:5], lam4[:, 3:4], lam4[:, 2:3], ALU.subtract))
            link(v.tensor_scalar(lam4[:, 4:5], lam4[:, 4:5], -0.2, None, ALU.add))

            b = full("ag")
            release("ag", v.tensor_copy(ag[:, :], b[:, :]))
            b = full("bkvb")
            for kv in range(2):
                for half in range(2):
                    r = half * DH
                    v.tensor_copy(kb[r:r + DH, kv * S:(kv + 1) * S], b[kv * DH:(kv + 1) * DH, 0:S])
            release("bkvb", v.tensor_copy(v_b[:, :], b[:, S:2 * S]))
            dve.sem_inc(kb_ready, 1)
            dve.sem_inc(v_ready, 1)
            b = full("vsg")
            v.tensor_copy(v_sw[:, :], b[:, 0:S])
            release("vsg", v.tensor_copy(gsig[:, :], b[:, S:S + 2 * NB]))
            dve.sem_inc(dgate_raw, 1)
            dve.sem_inc(v_ready, 1)

            def to_sigmoid():
                dve.wait_ge(dgate_tanh, 1)
                link(v.tensor_scalar(gsig[:, :], gsig[:, :], 0.5, 0.5, ALU.mult, ALU.add))

            def family_scores(fam, scale, bias_h, first):
                n = FAM_NO[fam]
                q1, q0 = fam_q1(fam), fam_q0(fam)
                for part, h in (("a", 0), ("b", 1)):
                    for qt, dst, keys in ((0, q0, slice(P, S)), (1, q1, slice(0, S))):
                        name = f"s_{fam}_{part}{qt}"
                        width = keys.stop - keys.start
                        release(name, v.scalar_tensor_tensor(
                            dst[:, h:NH:2, :], full(name)[:, 0:2 * width].rearrange("p (h k) -> p h k", h=2), scale,
                            bias_h[:, first + h:first + NH:2, keys], ALU.mult, ALU.add))
                c = n * 8
                link(v.reduce_max(mx[:, c:c + 4], q1, axis=X))
                link(v.reduce_max(mx[:, c + 4:c + 8], q0, axis=X))
                if fam == "swa":
                    for j in (0, 4):
                        link(v.tensor_tensor(mx[:, j:j + 4], mx[:, j:j + 4], par("sinks"), ALU.max))
                        link(v.tensor_tensor(es[:, j:j + 4], par("sinks"), mx[:, j:j + 4], ALU.subtract))
                tell(v.tensor_scalar(negm[:, c:c + 8], mx[:, c:c + 8], -1.0, None, ALU.mult), neg_ready)

            def inverse_sums(fam):
                n = FAM_NO[fam]
                dve.wait_ge(exp_ready, n + 1)
                d = den[:, n * 8:n * 8 + 8]
                if fam == "swa":
                    link(v.tensor_tensor(d, d, es[:, :], ALU.add))
                link(v.tensor_scalar(d, d, TINY, None, ALU.max))
                link(v.reciprocal(fac[:, :], d))

            def scale_probs(fam):
                for o, probs in ((0, fam_q1(fam)), (4, fam_q0(fam))):
                    for h in range(NH):
                        last = v.tensor_scalar(probs[:, h, :], probs[:, h, :], fac[:, o + h:o + h + 1], None, ALU.mult)
                return last

            def gate_factors(which):
                g = gsig[:, :].rearrange("p (t h g) -> p t h g", t=TT, h=NH)
                link(v.tensor_tensor(fac[:, 0:4], fac[:, 0:4], g[:, 1, :, which], ALU.mult))
                link(v.tensor_tensor(fac[:, 4:8], fac[:, 4:8], g[:, 0, :, which], ALU.mult))

            dve.wait_ge(bias_in, 32)
            family_scores("swa", DH ** -0.5, bias8, 0)
            dve.wait_ge(ax_ready, 1)
            for cb in range(2):
                src = ax[:, cb * (S + 3):(cb + 1) * (S + 3)]
                dst = xc[:, cb * S:(cb + 1) * S]
                link(v.tensor_scalar(dst, src[:, 0:S], par("conv_w")[:, cb:cb + 1], par("conv_b")[:, cb:cb + 1],
                                     ALU.mult, ALU.add))
                for i in range(1, 4):
                    link(v.scalar_tensor_tensor(dst, src[:, i:i + S], par("conv_w")[:, 2 * i + cb:2 * i + cb + 1], dst,
                                                ALU.mult, ALU.add))
            dve.sem_inc(xc_ready, 1)
            dve.wait_ge(kc_ready, 1)
            for src, pos in ((kc2, "pos_k"), (vc2, "pos_v")):
                lo = src[0:DH, :].rearrange("p (c i) -> p c i", i=16)
                hi = src[DH:P, :].rearrange("p (c i) -> p c i", i=16)
                link(v.tensor_tensor(lo, lo, par(pos)[0:DH, :].unsqueeze(1).broadcast_to([DH, 16, 16]), ALU.add))
                link(v.tensor_tensor(hi[:, 0:15, :], hi[:, 1:16, :],
                                     par(pos)[DH:P, :].unsqueeze(1).broadcast_to([DH, 15, 16]), ALU.add))
            dve.sem_inc(blocks_ready, 1)
            link(v.tensor_tensor(lru_w[:, :], ag[:, :], ag[:, :], ALU.mult))
            link(v.tensor_scalar(lru_w[:, :], lru_w[:, :], GELU_C, 1.0, ALU.mult, ALU.add))
            tell(v.tensor_tensor(lru_w[:, :], lru_w[:, :], ag[:, :], ALU.mult), gelu_in)
            b = full("h1")
            release("h1", v.tensor_copy(h1[:, :], b[:, 0:NCMP]))
            link(v.tensor_tensor(h1a[:, :], h1[:, :], h1[:, :], ALU.mult))
            link(v.tensor_scalar(h1a[:, :], h1a[:, :], GELU_C, 1.0, ALU.mult, ALU.add))
            tell(v.tensor_tensor(h1a[:, :], h1a[:, :], h1[:, :], ALU.mult), h1_raw)
            b = full("ck")
            release("ck", v.tensor_copy(ck[:, :], b[:, :]))
            dve.sem_inc(ck_ready, 1)
            inverse_sums("swa")
            tell(scale_probs("swa"), p_ready)
            dve.wait_ge(h1_tanh, 1)
            link(v.scalar_tensor_tensor(h1b[:, :], h1a[:, :], 1.0, h1[:, :], ALU.add, ALU.mult))
            tell(v.tensor_scalar(h1b[:, :], h1b[:, :], 0.5, None, ALU.mult), h1_ready)
            family_scores("diff0", 32 ** -0.5, bias8, 4)
            b = full("vc")
            release("vc", v.tensor_copy(v_c[:, :], b[:, :]))
            dve.sem_inc(v_ready, 1)
            family_scores("diff1", 32 ** -0.5, bias8, 4)
            to_sigmoid()
            dve.wait_ge(lru_tanh_ready, 1)
            link(v.scalar_tensor_tensor(xc[:, :], lru_ti[:, :], 1.0, xc[:, :], ALU.add, ALU.mult))
            xc3 = xc[:, :].rearrange("p (c s) -> p c s", c=2)
            link(v.tensor_scalar(lru_scratch[:, 0:2].unsqueeze(2), xc3[:, :, 0:1], 0.5, None, ALU.mult))
            link(v.tensor_scalar(lru_tr[:, :], lru_t[:, :], 1.0, None, ALU.add))
            link(v.reciprocal(lru_tr[:, :], lru_tr[:, :]))
            link(v.tensor_scalar(lru_t[:, :], lru_t[:, :], -1.0, 1.0, ALU.mult, ALU.add))
            link(v.tensor_tensor(lru_t[:, :], lru_t[:, :], lru_tr[:, :], ALU.mult))
            link(v.tensor_tensor(xc[:, :], xc[:, :], lru_s[:, :], ALU.mult))
            link(v.tensor_tensor(xc[:, :], xc[:, :], lru_tr[:, :], ALU.mult))
            link(v.tensor_copy(xc3[:, :, 0:1], lru_scratch[:, 0:2].unsqueeze(2)))
            for cb in range(2):
                c = slice(cb * S, (cb + 1) * S)
                link(v.tensor_tensor_scan(lru_s[:, c], lru_t[:, c], xc[:, c], 0.0, ALU.mult, ALU.add))
            link(v.scalar_tensor_tensor(ag[:, :], lru_w[:, :], 1.0, ag[:, :], ALU.add, ALU.mult))
            link(v.scalar_tensor_tensor(ya[:, :], lru_s[:, :], 0.5, ag[:, :], ALU.mult, ALU.mult))
            dve.sem_inc(ya_ready, 1)
            inverse_sums("diff1")
            link(v.tensor_scalar(fac[:, :], fac[:, :], lam4[:, 4:5], None, ALU.mult))
            link(scale_probs("diff1"))
            inverse_sums("diff0")
            for o, p0, p1 in ((0, fam_q1("diff0"), fam_q1("diff1")), (4, fam_q0("diff0"), fam_q0("diff1"))):
                for h in range(NH):
                    last = v.scalar_tensor_tensor(p0[:, h, :], p0[:, h, :], fac[:, o + h:o + h + 1], p1[:, h, :],
                                                  ALU.mult, ALU.add)
            tell(last, p_ready)
            b = full("kc2")
            release("kc2", v.tensor_copy(kcT[:, :], b[:, 0:NCMP]))
            b = full("vc2")
            release("vc2", v.tensor_copy(vc_d[0:NCMP, :], b[0:NCMP, 0:DH]))
            dve.sem_inc(kc2_ready, 1)
            for j in range(2):
                dve.wait_ge(pt_used, 2 * j + 2)
                b = psum[items[f"yb{j}"][0]]
                release(f"yb{j}", v.tensor_copy(yb[:, j * S:(j + 1) * S], b[:, 0:S]))
                dve.sem_inc(yb_ready, 1)
            pc3 = pc_s[:, :].rearrange("p (a c) -> p a c", c=16)
            cmask = lru_w[:, 0:128].rearrange("p (a c) -> p a c", c=16)
            for t in range(TT):
                at = 31 + P * (1 - t)
                link(v.tensor_scalar(cmask[:, t * 4:t * 4 + 4, 0:NCMP], bias4[:, :, at:at + 16 * (NCMP - 1) + 1:16],
                                     -1e29, None, ALU.is_gt))
            for part, h in (("a", 0), ("b", 1)):
                b = full(f"sc_{part}")
                sc3 = b[:, 0:DH].rearrange("p (a c) -> p a c", c=16)
                for t in range(TT):
                    at = 31 + P * (1 - t)
                    ins = v.scalar_tensor_tensor(pc3[:, t * 4 + h:t * 4 + 4:2, 0:NCMP],
                                                 sc3[:, t * 2:t * 2 + 2, 0:NCMP], DH ** -0.5,
                                                 bias4[:, h:NH:2, at:at + 16 * (NCMP - 1) + 1:16],
                                                 ALU.mult, ALU.add)
                    if t == TT - 1:
                        release(f"sc_{part}", ins)
                    else:
                        link(ins)
            pcv, cmv = pc3[:, :, 0:NCMP], cmask[:, :, 0:NCMP]
            link(v.reduce_max(cmx[:, :], pcv, axis=X))
            tell(v.tensor_tensor(pcv, pcv, cmx[:, :].unsqueeze(2).broadcast_to([P, 8, NCMP]), ALU.subtract), cmp_in)
            family_scores("sel", DH ** -0.5, bias4, 0)
            dve.wait_ge(cmp_exp, 1)
            link(v.tensor_tensor(pcv, pcv, cmv, ALU.mult))
            link(v.reduce_sum(cmx[:, :], pcv, axis=X))
            link(v.tensor_scalar(cmx[:, :], cmx[:, :], TINY, None, ALU.max))
            link(v.reciprocal(cmx[:, :], cmx[:, :]))
            g4 = gsig[:, :].rearrange("p (a g) -> p a g", g=3)
            link(v.tensor_tensor(cmx[:, :], cmx[:, :], g4[:, :, 0], ALU.mult))
            tell(v.tensor_tensor(pcv, pcv, cmx[:, :].unsqueeze(2).broadcast_to([P, 8, NCMP]), ALU.mult), pc_ready)
            inverse_sums("sel")
            gate_factors(1)
            tell(scale_probs("sel"), p_ready)
            dve.wait_ge(pt_used, 8)
            b = psum[items["oc"][0]]
            release("oc", v.tensor_copy(o_c[:, :], b[:, :]))
            link(v.tensor_tensor(xc[:, :], o_c[:, :], o_c[:, :], ALU.mult))
            link(v.reduce_sum(ssc[:, :], xc[:, :].rearrange("p (a d) -> p a d", d=DH), axis=X))
            tell(v.tensor_scalar(ssc[:, :], ssc[:, :], 1.0 / DH, 1e-5, ALU.mult, ALU.add), oc_squares)
            family_scores("win", DH ** -0.5, bias4, 0)
            dve.wait_ge(oc_root, 1)
            link(v.reciprocal(rc[:, :], rc[:, :]))
            oc3 = o_c[:, :].rearrange("p (a d) -> p a d", d=DH)
            tell(v.tensor_tensor(oc3, oc3, rc[:, :].unsqueeze(2).broadcast_to([P, 8, DH]), ALU.mult), oc_ready)
            b = full("ycT")
            release("ycT", v.tensor_scalar(yc[:, :], b[:, :], gsubln[:, 0:1], None, ALU.mult))
            dve.sem_inc(yc_ready, 1)
            inverse_sums("win")
            gate_factors(2)
            tell(scale_probs("win"), p_ready)
            for j in range(2):
                b = full(f"yd{j}")
                release(f"yd{j}", v.tensor_copy(yd[:, j * S:(j + 1) * S], b[:, 0:S]))
                dve.sem_inc(yd_ready, 1)
            dve.wait_ge(pt_used, 16)
            for n2 in range(4):
                dst = merged[:, n2 * 512:(n2 + 1) * 512]
                for br in range(4):
                    dve.wait_ge(gate_ready, 8 if br < 2 else 8 + 2 * n2 + br - 1)
                    g = gates[:, br * KT * S + n2 * 512:br * KT * S + (n2 + 1) * 512] if br < 2 else late_gate
                    b = full(f"b{n2}_{br}")
                    release(f"b{n2}_{br}", v.scalar_tensor_tensor(branch_tmp if br else dst, g, 1.0, b[:, :],
                                                                  ALU.add, ALU.mult))
                    if br >= 2:
                        dve.sem_inc(late_used, 1)
                    if br == 3:
                        tell(v.tensor_tensor(dst, dst, branch_tmp, ALU.add), merged_ready)
                    elif br:
                        link(v.tensor_tensor(dst, dst, branch_tmp, ALU.add))
            for nh in range(2):
                for t in range(TT):
                    c = slice(t * D + nh * 512, t * D + (nh + 1) * 512)
                    b = full(f"x1_{t}{nh}")
                    release(f"x1_{t}{nh}", v.scalar_tensor_tensor(x1[:, c], b[:, :], 0.5, x_sb[:, c], ALU.mult,
                                                                  ALU.add))
                    dve.sem_inc(x1_ready, 1)
            mean_root(2)
            dve.wait_ge(norm_g_in, 32)
            for t in range(TT):
                tell(v.scalar_tensor_tensor(h2[:, t * D:(t + 1) * D], x1[:, t * D:(t + 1) * D], rstd[:, t:t + 1],
                                            gffn, ALU.mult, ALU.mult), h2_ready)
            for j in (1, 3):
                b = full(f"hT{j}")
                release(f"hT{j}", v.tensor_copy(h2T[:, 2 * j * S:(2 * j + 2) * S], b[:, :]))
                dve.sem_inc(h2T_ready, 1)

            link(v.memset(selm[:, :], 0.0))
            link(v.memset(comb[:, :], 0.0))
            b = full("rl")
            r3 = rlog.rearrange("p (t n) -> p t n", t=TT)
            release("rl", v.tensor_tensor(r3, b[:, 0:72].rearrange("p (t n) -> p t n", t=TT),
                                          par("b_router").unsqueeze(1).broadcast_to([P, TT, 36]), ALU.add))
            lg, le = r3[:, :, 0:GRP], r3[:, :, GRP:36]

            def first_of(onehot, vals, top, n, cand):
                link(v.reduce_max(top, vals, axis=X))
                link(v.tensor_tensor(cand, vals, top.unsqueeze(2).broadcast_to([P, TT, n]), ALU.not_equal))
                iota = par("iota8")[:, 0:n].unsqueeze(1).broadcast_to([P, TT, n])
                link(v.tensor_scalar(cand, cand, 100.0, None, ALU.mult))
                link(v.tensor_tensor(cand, cand, iota, ALU.add))
                link(v.tensor_reduce(wts[:, 6:8], cand, X, ALU.min))
                link(v.tensor_tensor(onehot, iota, wts[:, 6:8].unsqueeze(2).broadcast_to([P, TT, n]), ALU.is_equal))

            og, cg = ogrp.rearrange("p (t n) -> p t n", t=TT), cgrp.rearrange("p (t n) -> p t n", t=TT)
            first_of(og, lg, mgrp, GRP, cg)
            ge = gexp.rearrange("p (t g n) -> p t g n", t=TT, g=GRP)
            for g in range(GRP):
                link(v.tensor_tensor(ge[:, :, g, :], le[:, :, g * EPG:(g + 1) * EPG],
                                     og[:, :, g:g + 1].broadcast_to([P, TT, EPG]), ALU.mult))
            i3 = ing.rearrange("p (t n) -> p t n", t=TT)
            link(v.reduce_sum(i3, ge.rearrange("p t g n -> p t n g"), axis=X))
            o13, o23 = o1.rearrange("p (t n) -> p t n", t=TT), o2.rearrange("p (t n) -> p t n", t=TT)
            c83, in23 = c8.rearrange("p (t n) -> p t n", t=TT), in2.rearrange("p (t n) -> p t n", t=TT)
            first_of(o13, i3, v1, EPG, c83)
            link(v.scalar_tensor_tensor(in23, o13, NEG, i3, ALU.mult, ALU.add))
            first_of(o23, in23, v2, EPG, c83)
            link(v.tensor_tensor(gexp[:, 0:8].rearrange("p (t n) -> p t n", t=TT), lg,
                                 mgrp.unsqueeze(2).broadcast_to([P, TT, GRP]), ALU.subtract))
            tell(v.tensor_tensor(gexp[:, 8:10], v2, v1, ALU.subtract), grp_in)
            s3 = selm.rearrange("p (t n) -> p t n", t=TT)
            k3 = comb.rearrange("p (t n) -> p t n", t=TT)
            link(v.tensor_tensor(c83, o13, o23, ALU.add))
            for g in range(GRP):
                link(v.tensor_tensor(s3[:, :, g * EPG:(g + 1) * EPG], c83,
                                     og[:, :, g:g + 1].broadcast_to([P, TT, EPG]), ALU.mult))
            dve.sem_inc(sel_ready, 1)
            dve.wait_ge(grp_exp, 1)
            link(v.reduce_sum(gsum, gexp[:, 0:8].rearrange("p (t n) -> p t n", t=TT), axis=X))
            link(v.tensor_scalar(wts[:, 0:2], gexp[:, 8:10], 1.0, None, ALU.add))
            link(v.tensor_tensor(wts[:, 0:2], wts[:, 0:2], gsum, ALU.mult))
            link(v.reciprocal(wts[:, 0:2], wts[:, 0:2]))
            link(v.tensor_tensor(wts[:, 2:4], wts[:, 0:2], gexp[:, 8:10], ALU.mult))
            link(v.tensor_tensor(o13, o13, wts[:, 0:2].unsqueeze(2).broadcast_to([P, TT, EPG]), ALU.mult))
            link(v.tensor_tensor(o23, o23, wts[:, 2:4].unsqueeze(2).broadcast_to([P, TT, EPG]), ALU.mult))
            link(v.tensor_tensor(o13, o13, o23, ALU.add))
            for g in range(GRP):
                link(v.tensor_tensor(k3[:, :, g * EPG:(g + 1) * EPG], o13,
                                     og[:, :, g:g + 1].broadcast_to([P, TT, EPG]), ALU.mult))
            b = full("rank")
            link(v.scalar_tensor_tensor(slotv[:, :], b[:, 0:72], 1.0, selm[:, :], ALU.add, ALU.mult))
            link(v.tensor_scalar(slotv[:, :], slotv[:, :], -1.0, None, ALU.add))
            release("rank", v.tensor_copy(cnt[:, :], b[:, 72:108]))
            link(v.reduce_max(cmax[:, :], cnt[:, :], axis=X))
            tell(v.tensor_copy(cmax_i[:, :], cmax[:, :]), count_ready)
            link(v.memset(yexp[:, :], 0.0))

            gu_bank, tr_bank, cd = psum[4], psum[5], psum[6:8]
            slots3 = slotv.rearrange("p (t e) -> p t e", t=TT)
            oh4 = onehot_g.rearrange("p (t e s) -> p t e s", t=TT, e=2)
            iota4 = par("iota").unsqueeze(1).unsqueeze(1).broadcast_to([P, TT, 2, CAP])

            def one_hots(n, at, gc):
                v.tensor_tensor(oh4, slots3[:, :, at].unsqueeze(3).broadcast_to([P, TT, 2, CAP]), iota4,
                                ALU.is_equal).then_inc(onehot_ready, 1)
                dve.wait_ge(onehot_ready, n)
                v.tensor_tensor(gc.rearrange("p (t e s) -> p t e s", t=TT, e=2), oh4,
                                k3[:, :, at].unsqueeze(3).broadcast_to([P, TT, 2, CAP]),
                                ALU.mult).then_inc(weighted_ready, 1)
                dve.wait_ge(weighted_ready, n)

            def expert_pass(c):
                def tokens_out(n):
                    dve.wait_ge(gather_done, n)
                    v.tensor_copy(xgT[:, 512:1024], cd[1][:, :]).then_inc(xg_d, 1)

                v.memset(tb1[:, 256:512], 0.0).then_inc(pass_ready, 1)
                one_hots(c * 18 + 1, slice(0, 2), gc0)
                tokens_out(c * 17 + 1)
                one_hots(c * 18 + 2, slice(2, 4), gc1)
                dve.sem_inc(pass_primed, 1)
                with dve.Fori(0, PAIRS // 2) as it:
                    for p in range(2):
                        i = it * 2 + p
                        n = i + c * PAIRS
                        dve.wait_ge(silu_done, n + 1)
                        v.tensor_tensor(he[:, :], silu_g[:, :], gu_bank[:, FF:2 * FF], ALU.mult).then_inc(he_ready, 1)
                        tokens_out(i + c * 17 + 2)
                        dve.wait_ge(tr_done, n + 1)
                        v.tensor_copy((tb0, tb1)[p], tr_bank[:, :]).then_inc(tb_ready, 1)
                        one_hots(i + c * 18 + 3, bass.ds(it * 4 + (2 * p + 4), 2), (gc0, gc1)[p])
                        dve.wait_ge(down_done, n + 1)
                        v.tensor_copy(yexp[:, 512:1024], cd[1][:, :]).then_inc(yexp_d, 1)

            for s in (he_ready, tb_ready, yexp_d):
                dve.sem_inc(s, 1)
            expert_pass(0)
            most = dve.value_load(cmax_i[0:1, 0:1], min_val=0, max_val=S)
            with dve.If(most > CAP):
                with dve.Fori(1, PASSES) as c:
                    dve.wait_ge(scatter_done, c * 17)
                    v.tensor_scalar(slotv[:, :], slotv[:, :], -float(CAP), None, ALU.add).then_inc(slots_moved, 1)
                    dve.wait_ge(slots_moved, c)
                    expert_pass(c)
            dve.wait_ge(x2_ready, 1)
            for t in range(TT):
                for nh in range(2):
                    c = slice(t * D + nh * 512, t * D + (nh + 1) * 512)
                    ins = v.tensor_tensor(x2[:, c], psum[2 * t + nh][:, :], x1[:, c], ALU.add)
                ins.then_inc(fin_in, 1)
            dve.wait_ge(fin_squares, 2)
            tell(v.tensor_scalar(ss[:, :], ss[:, :], 1.0 / D, 1e-6, ALU.mult, ALU.add), fin_ms)
            dve.wait_ge(fin_root, 1)
            link(v.reciprocal(rstd[:, :], rt[:, :]))
            for t in range(TT):
                v.scalar_tensor_tensor(x2[:, t * D:(t + 1) * D], x2[:, t * D:(t + 1) * D], rstd[:, t:t + 1], gfin,
                                       ALU.mult, ALU.mult).then_inc(out_ready, 1)


def kernel(**inputs):
    import concourse.bacc as _bacc
    from concourse import mybir as _mybir
    from concourse.bass_utils import run_bass_kernel_spmd as _run

    a = {k: np.asarray(v) for k, v in inputs.items()}
    f32 = np.float32

    def by_rows(w):
        k, n = w.shape
        return np.ascontiguousarray(w.reshape(k // P, P, n).transpose(1, 0, 2).reshape(P, -1))

    def by_channel(v):
        return np.ascontiguousarray(v.reshape(-1, P).T)

    def rows_of(v):
        return np.broadcast_to(v.reshape(1, -1), (P, v.size))

    dist = 255 - np.arange(MW_BIAS)
    n = np.maximum(dist, 0)
    exact = BUCKETS // 2
    scaled = np.log(np.maximum(n, 1).astype(f32) / f32(exact)) / f32(math.log(MAXD / exact))
    large = np.minimum(exact + (scaled * f32(BUCKETS - exact)).astype(np.int32), BUCKETS - 1)
    bucket = np.where(n < exact, n, large)
    onehot = np.zeros((P, MW_BIAS), f32)
    onehot[bucket, np.arange(MW_BIAS)] = 1.0
    onehot[0:BUCKETS, dist < 0] = 0.0
    onehot[BUCKETS] = dist < 0
    onehot[BUCKETS + 1] = dist >= 128
    tab = np.zeros((P, NB), f32)
    tab[0:BUCKETS] = a["rel_bias"]
    tab[BUCKETS] = NEG
    tab[BUCKETS + 1, 0:NH] = NEG

    def lru_blocks(w):
        return w.reshape(2, 2, DH, DH).transpose(1, 2, 0, 3).reshape(P, 2 * DH)

    def positions(p):
        return p.reshape(2, 16, DH).transpose(0, 2, 1).reshape(P, 16)

    def w1_of(w):
        return w.reshape(2, 16, DH, DH).transpose(0, 2, 1, 3).reshape(P, 16 * DH)

    parts = {
        "ident": np.eye(P, dtype=f32), "mix_g": by_channel(a["mix_norm_g"][0]), "tab": tab, "onehot": onehot,
        "conv_w": by_channel(a["conv_w"][0]), "conv_b": by_channel(a["conv_b"][0]),
        "b_a": by_channel(a["lru_b_a"][0]), "b_x": by_channel(a["lru_b_x"][0]),
        "lam": by_channel(a["lru_lambda"][0]),
        "subln_g": np.concatenate([a["diff_subln_g"][0]] * 2).reshape(P, 1),
        "b_gate": by_channel(a["b_gate"][0]), "sinks": rows_of(a["swa_sinks"][0]),
        "lq1": rows_of(a["diff_lq1"][0]), "lk1": rows_of(a["diff_lk1"][0]),
        "lq2": rows_of(a["diff_lq2"][0]), "lk2": rows_of(a["diff_lk2"][0]),
        "w_a": lru_blocks(a["lru_w_a"][0]), "w_x": lru_blocks(a["lru_w_x"][0]),
        "w2": np.concatenate([a["nsa_w2_k"][0], a["nsa_w2_v"][0]]),
        "pos_k": positions(a["nsa_pos_k"][0]), "pos_v": positions(a["nsa_pos_v"][0]),
        "upper": np.triu(np.ones((P, P), f32), 1), "ones": np.ones((P, P), f32),
        "iota": rows_of(np.arange(CAP, dtype=f32)), "iota8": rows_of(np.arange(8, dtype=f32)),
        "b_router": rows_of(np.concatenate([a["b_router_grp"][0], a["b_router_exp"][0]])),
        "w_router": by_rows(np.concatenate([a["w_router_grp"][0], a["w_router_exp"][0]], axis=1)),
    }

    def packed(names):
        return np.ascontiguousarray(np.concatenate([parts[n] for n, _ in COLUMNS if n in names], axis=1))

    w_in = a["w_in"][0]
    gate = a["w_gate"][0]
    eg, eu, ed = a["w_exp_gate"][0], a["w_exp_up"][0], a["w_exp_down"][0]
    w_moe = np.empty((PAIRS, 3, P, W_SLOT), f32)
    for e in range(2):
        gu = w_moe[:, e].reshape(PAIRS, P, KT, 2, FF)
        for j, w in enumerate((eg, eu)):
            gu[:, :, :, j, :] = w[e::2].reshape(PAIRS, KT, P, FF).transpose(0, 2, 1, 3)
        w_moe[:, 2].reshape(PAIRS, P, 2, 2, D)[:, :, e] = ed[e::2].reshape(PAIRS, 2, P, D).transpose(0, 2, 1, 3)
    arrays = {
        "pa": packed(FIRST_PART), "pb": packed(SECOND_PART),
        "w_in_full": np.stack([by_rows(w_in[:, c:c + 512]) for c in (0, 512, 1024, 1536)]),
        "w_in_tail": by_rows(np.concatenate([w_in[:, c:c + n] for c, n in (
            (2048, 128), (2176, 64), (2304, 64), (2240, 64), (2368, 64), (2432, 12))], axis=1)),
        "w1": np.concatenate([w1_of(a["nsa_w1_k"][0]), w1_of(a["nsa_w1_v"][0])], axis=1),
        "w_gates": np.stack([by_rows(gate[br][:, c:c + 512]) for br in range(4) for c in (0, 512)]),
        "w_branch": np.stack([np.concatenate([by_rows(a["w_branch"][0][br + j]) for j in range(2)], axis=1)
                              for br in (0, 2)]),
        "w_out": np.stack([by_rows(a["w_out"][0][:, c:c + 512]) for c in (0, 512)]),
        "w_moe": w_moe.reshape(PAIRS * 3, P, W_SLOT),
        "x": a["x"][0], "g_ffn": a["ffn_norm_g"][0], "g_fin": a["final_norm_g"],
    }
    nc = _bacc.Bacc("TRN2", target_bir_lowering=False, num_devices=1)
    dt = _mybir.dt.float32
    args = {n: nc.dram_tensor(f"in_{n}_dram", v.shape, dt, kind="ExternalInput").ap() for n, v in arrays.items()}
    out = nc.dram_tensor("out_0_dram", (S, D), dt, kind="ExternalOutput").ap()
    decoder_layer(nc, out=out, **args)
    r = _run(nc, [{f"in_{n}_dram": np.ascontiguousarray(v) for n, v in arrays.items()}], core_ids=[0])
    return r.results[0]["out_0_dram"].reshape(1, S, D)
```

```python
import math

import numpy as np

import concourse.bass as bass
from concourse import mybir
from contextlib import ExitStack

P = 128
S, D = 256, 1024
TT = S // P
KT = D // P
MW, DH = 256, 64
NH = 4
NB = 12
BUCKETS, MAXD = 32, 128
NCMP = (S - 32) // 16 + 1
E, GRP, EPG, FF = 32, 4, 8, 256
CAP = 64
PAIRS = E // 2
PASSES = S // CAP
NEG = -1e30
TINY = 1e-30
SLOT_COLS = 2 * S + S
W_SLOT = 4096
SLOTS = 6
BIAS_ROWS = 32
MW_BIAS = 512
IN_TAIL = 396
GELU_C, GELU_K = 0.044715, math.sqrt(2.0 / math.pi)
FAMILIES = ("swa", "diff0", "diff1", "sel", "win")

COLUMNS = [("ident", 128), ("mix_g", KT), ("ffn_g", KT), ("tab", NB), ("onehot", MW_BIAS),
           ("conv_w", 8), ("conv_b", 2), ("b_a", 2), ("b_x", 2), ("lam", 2),
           ("subln_g", 1), ("b_gate", 32), ("sinks", NH), ("lq1", 32), ("lq2", 32), ("lk1", 32), ("lk2", 32),
           ("w_a", 128), ("w_x", 128), ("w2", DH), ("pos_k", 16), ("pos_v", 16),
           ("upper", 128), ("ones", 128), ("iota", CAP), ("iota8", 8), ("b_router", 36), ("w_router", KT * 36)]


def column_offsets(names):
    at, out = 0, {}
    for name, n in COLUMNS:
        if name in names:
            out[name] = (at, n)
            at += n
    return out, at


FIRST_PART = {"ident", "mix_g", "tab", "onehot"}
SECOND_PART = {name for name, _ in COLUMNS} - FIRST_PART

GATE_ORDER = [(br, n2) for br in (0, 1) for n2 in range(4)] + [(br, n2) for n2 in range(4) for br in (2, 3)]
CHUNK_TABLE = [("in_a", 0, "ag"), ("in_b", 1, "bkvb"), ("in_tail", 2, "vsg"), ("in_cqk", 3, "ck"), ("w1", 4, "h1"),
               ("in_cvdq", 5, "dq"), ("g0_0", 1, "g0_0"), ("g0_1", 2, "g0_1"), ("g0_2", 3, "g0_2"),
               ("g0_3", 4, "g0_3"), ("g1_0", 5, "g1_0"), ("branch01", 1, "b3_1"), ("branch23", 2, "b3_3")]
CHUNK_TABLE += [(f"g{br}_{n2}", 3 + i % 3, f"g{br}_{n2}") for i, (br, n2) in enumerate(GATE_ORDER[5:])]
CHUNK_TABLE += [("out0", 5, "x1_10"), ("out1", 3, "x1_11")]
CHUNKS = [name for name, _, _ in CHUNK_TABLE]
CHUNK_SLOT = [s for _, s, _ in CHUNK_TABLE]
CHUNK_LAST = {name: item for name, _, item in CHUNK_TABLE}
PAIR_SLOTS = ((0, 1, 2), (4, 5, 3))
HALF = W_SLOT // 2


def chunk_use(i):
    return CHUNK_SLOT[:i].count(CHUNK_SLOT[i])


def psum_items():
    ring, names = 6, []

    def fam(f):
        return [f"s_{f}_{part}" for part in ("a0", "a1", "b0", "b1")]

    def tps(f):
        return [f"tp_{f}_{h}" for h in range(NH)]
    order = (["vec", "xT0", "xT1", "xT2", "xT3", "ax", "ag", "bq", "bkvb", "kcks", "vsg"] + ["cq", "ck", "h1"]
             + fam("swa") + ["lr", "lx"] + fam("diff0") + ["vc", "dq"] + fam("diff1")
             + ["kc2", "vc2", "g0_0", "g0_1"] + tps("swa") + ["sc_a", "sc_b"] + fam("sel") + ["g0_2", "g0_3"]
             + tps("diff") + ["oc"] + fam("win") + ["g1_0", "g1_1", "ycT"] + tps("sel")
             + ["tpc0", "tpc1", "g1_2", "g1_3"] + tps("win"))
    for n2 in range(4):
        order += [f"b{n2}_0", f"b{n2}_1", f"g2_{n2}", f"b{n2}_2", f"g3_{n2}", f"b{n2}_3"]
    order += ["x1_00", "x1_10", "x1_01", "x1_11", "hT0", "hT1", "hT2", "hT3", "rl", "rank"]
    order += [f"xg{k}" for k in range(KT)]
    for i, name in enumerate(order):
        names.append((name, i % ring))
    names += [("yb0", 6), ("yb1", 7), ("yd0", 6), ("yd1", 7)]
    by_head = ("yb0", "yb1", "oc")
    uses, fulls, out = [0] * 8, [0] * 8, {}
    for name, bank in names:
        fulls[bank] += name not in by_head
        out[name] = (bank, uses[bank], fulls[bank])
        uses[bank] += 1
    return out, uses


def decoder_layer(nc, pa, pb, w_in_full, w_in_tail, w1, w_gates, w_branch, w_out, w_moe, x, g_fin, out):
    f32 = mybir.dt.float32
    f32r = mybir.dt.float32r
    bf16 = mybir.dt.bfloat16
    i32 = mybir.dt.int32
    ALU = mybir.AluOpType
    ACT = mybir.ActivationFunctionType
    X = mybir.AxisListType.X

    ctx = ExitStack()
    with ctx:
        def sb(name, n, dt=f32, p=P):
            return ctx.enter_context(nc.sbuf_tensor(name, [p, n], dt))

        def sb_split(name, n):
            at = -(-nc.sbuf_base // 32) * 32
            return sb(name, n), nc.alloc_sbuf_tensor_at(name + "_parts", [P, n], f32r, offset=at)

        def sem(name):
            return ctx.enter_context(nc.semaphore(name))

        bias_rows = nc.dram_tensor("bias_rows", [NB, BIAS_ROWS, MW_BIAS], f32, kind="Internal")

        ring, ring_parts = sb_split("weight_slots", SLOTS * W_SLOT)
        slot = [ring[:, s * W_SLOT:(s + 1) * W_SLOT] for s in range(SLOTS)]
        parts = [(ring_parts[:, s * W_SLOT:s * W_SLOT + HALF], ring_parts[:, s * W_SLOT + HALF:(s + 1) * W_SLOT])
                 for s in range(SLOTS)]
        hT_lo, hT_hi = parts[0]
        offs_a, n_a = column_offsets(FIRST_PART)
        offs_b, n_b = column_offsets(SECOND_PART)
        par_a, par_b = sb("params_a", n_a), sb("params_b", n_b)

        def par(name):
            if name in offs_a:
                o, n = offs_a[name]
                return par_a[:, o:o + n]
            o, n = offs_b[name]
            return par_b[:, o:o + n]

        def cut(t, widths):
            at, parts = 0, []
            for n in widths:
                parts.append(t[:, at:at + n])
                at += n
            return parts

        x_sb = sb("x_sb", TT * D)
        hT = sb("hT", KT * S)
        gates = sb("gates", 2 * KT * S)
        shared, shared_parts = sb_split("shared", 3 * 1536 + 8 * 256 + 4 * 384)
        fam_buf = [shared[:, i * 1536:(i + 1) * 1536] for i in range(3)]
        bias8 = shared[:, 4608:4608 + 2048].rearrange("p (h j) -> p h j", h=8)
        bias4 = shared[:, 6656:6656 + 1536].rearrange("p (h j) -> p h j", h=4)
        xn = shared[:, 0:TT * D]
        merged = shared[:, 0:KT * S]
        branch_tmp = shared[:, 2048:2560]
        late_gate = shared[:, 2560:3072]
        (h2, _, xg0, xg1, tb0, tb1, he, silu_g, gc0, gc1, yexp) = cut(
            shared, [TT * D, D, KT * P, KT * P, 512, 512, 256, 256, 256, 256, D])
        onehot_all, h2_hi, h2_lo = cut(shared_parts[:, TT * D:], [D, TT * D, TT * D])
        h2T = hT
        x1 = x_sb
        gfin = gates[:, D:2 * D]
        x2 = gates[:, 2 * D:4 * D]
        lru_tr, lru_ti, lru_t, lru_s = cut(gates[:, 2048:4096], [512] * 4)
        work = sb("work", KT * SLOT_COLS + 10 * P + 262)
        (ax, ag, xc, lru_w, ya, yb, bq, kb, cq, ck, dq, ks2, kw2, kc2, vc2, v_b, v_sw, v_c) = cut(
            work, [2 * (S + 3)] + [512] * 10 + [256] * 6 + [512])
        xg_all = work[:, 0:KT * SLOT_COLS].rearrange("p (k s) -> p k s", k=KT)
        yd, yc = bq, cq
        pt = sb("pt", 4 * 384)
        vec = pt[0:NB, 0:MW_BIAS]
        o_c = sb("o_c", 512)
        lru_scratch = o_c
        iota512 = o_c
        pc_s = sb("pc_s", 8 * 16)
        pcT = shared[0:16, 1536:2560]
        small = sb("small", 340)
        (ss, rt, rstd, lam4, sp2, sp_a, sp_b, sp_c, bga, bgx, fac, den, negm, mx, es, gsig, h1, h1a, h1b, kcT, vc_d,
         ssc, rc, cmx) = cut(
            small, [2, 2, 2, 8, 2, 2, 2, 2, 2, 2, 8, 40, 40, 40, 8, 24, 15, 15, 15, 15, 64, 8, 8, 8])
        bgh = sb("bgh", 32)
        gsubln = sb("gsubln", 1)
        route = pt[:, 0:640]
        (rlog, mgrp, cgrp, ogrp, gsum, gexp, ing, v1, v2, c8, o1, in2, o2, wts, comb, selm, slotv, cnt,
         cmax, base, place, pos_g, pos_12, grouped) = cut(
            route, [72, 2, 8, 8, 2, 10, 16, 2, 2, 16, 16, 16, 16, 8, 72, 72, 72, 36, 1, 36, 72, 16, 4, 64])
        cmax_i = sb("cmax_i", 1, i32)
        first_slot_i = sb("first_slot_i", 36, i32)
        zeros16 = sb("zeros16", P, bf16)

        psum = [ctx.enter_context(nc.psum_tensor(f"bank{b}", [P, 512], f32)) for b in range(8)]
        items, bank_uses = psum_items()

        params_a_in, params_b_in, norm_g_in = sem("params_a_in"), sem("params_b_in"), sem("norm_g_in")
        x_in = [sem(f"x_in{t}") for t in range(TT)]
        slot_full = [sem(f"slot_full{s}") for s in range(SLOTS)]
        bank_full = [sem(f"bank_full{b}") for b in range(8)]
        bank_free = [sem(f"bank_free{b}") for b in range(8)]
        vec_ready, rows_stored, bias_in = sem("vec_ready"), sem("rows_stored"), sem("bias_in")
        dve_step, act_step = sem("dve_step"), sem("act_step")
        squares_ready, ms_ready, root_ready, xn_ready, hT_a, hT_d = (
            sem(n) for n in ("squares_ready", "ms_ready", "root_ready", "xn_ready", "hT_a", "hT_d"))
        ax_ready, xc_ready, lru_par_ready, lru_tanh_ready, gelu_in, ya_ready = (
            sem(n) for n in ("ax_ready", "xc_ready", "lru_par_ready", "lru_tanh_ready", "gelu_in", "ya_ready"))
        bq_ready, kb_ready, kc_ready, ks_ready, cq_ready, ck_ready, dq_ready = (
            sem(n) for n in ("bq_ready", "kb_ready", "kc_ready", "ks_ready", "cq_ready", "ck_ready", "dq_ready"))
        dgate_raw, dgate_tanh = sem("dgate_raw"), sem("dgate_tanh")
        blocks_ready, h1_raw, h1_tanh, h1_ready, kc2_ready = (
            sem(n) for n in ("blocks_ready", "h1_raw", "h1_tanh", "h1_ready", "kc2_ready"))
        sp_in, sp_exp, lam_in, lam_exp = sem("sp_in"), sem("sp_exp"), sem("lam_in"), sem("lam_exp")
        neg_ready, exp_ready, p_ready = (sem(n) for n in ("neg_ready", "exp_ready", "p_ready"))
        cmp_in, cmp_exp, pc_ready, pcT_ready = (sem(n) for n in ("cmp_in", "cmp_exp", "pc_ready", "pcT_ready"))
        pt_ready, pt_used, v_ready = sem("pt_ready"), sem("pt_used"), sem("v_ready")
        oc_squares, oc_root, oc_ready = sem("oc_squares"), sem("oc_root"), sem("oc_ready")
        yb_ready, yc_ready, yd_ready = sem("yb_ready"), sem("yc_ready"), sem("yd_ready")
        gate_ready, late_used, merged_ready = sem("gate_ready"), sem("late_used"), sem("merged_ready")
        x1_ready, h2_a, h2_d, h2T_ready, rstd_ready, h2_hi_ready, h2_lo_ready = (
            sem(n) for n in ("x1_ready", "h2_a", "h2_d", "h2T_ready", "rstd_ready", "h2_hi_ready", "h2_lo_ready"))
        grp_in, grp_exp, sel_ready, count_ready = (sem(n) for n in ("grp_in", "grp_exp", "sel_ready", "count_ready"))
        xg_a, xg_d, gu_done, silu_done, he_ready = (
            sem(n) for n in ("xg_a", "xg_d", "gu_done", "silu_done", "he_ready"))
        tr_done, tb_ready, down_done, yexp_a, yexp_d = (
            sem(n) for n in ("tr_done", "tb_ready", "down_done", "yexp_a", "yexp_d"))
        x2_ready, fin_in, fin_squares, fin_ms, fin_root, out_ready, out_stored = (
            sem(n) for n in ("x2_ready", "fin_in", "fin_squares", "fin_ms", "fin_root", "out_ready", "out_stored"))
        hT_hi_ready, hT_lo_ready, gate_hi_ready, gate_lo_ready = (
            sem(n) for n in ("hT_hi_ready", "hT_lo_ready", "gate_hi_ready", "gate_lo_ready"))
        ax_pads, slots_moved = sem("ax_pads"), sem("slots_moved")
        weighted_ready, slots_ready = sem("weighted_ready"), sem("slots_ready")
        xg_all_a, xg_all_d = sem("xg_all_a"), sem("xg_all_d")
        pass_begun = sem("pass_begun")
        xg_pad, base_moved = sem("xg_pad"), sem("base_moved")

        FAM_NO = {f: i for i, f in enumerate(FAMILIES)}
        FAM_BUF = {"swa": 0, "diff0": 1, "diff1": 2, "sel": 0, "win": 2}
        TP_FAMS = ("swa", "diff", "sel", "win")
        TP_BUF = {"swa": 0, "diff": 1, "sel": 0, "win": 2}

        def fam_q1(f):
            return fam_buf[FAM_BUF[f]][:, 0:1024].rearrange("p (h k) -> p h k", h=NH)

        def fam_q0(f):
            return fam_buf[FAM_BUF[f]][:, 1024:1536].rearrange("p (h k) -> p h k", h=NH)

        def expert_base(s):
            return CHUNK_SLOT.count(s)

        def wait_past(eng, s, value):
            if not (isinstance(value, int) and value == 0):
                eng.wait_ge(s, value)

        def before_last(n):
            return max(n - 1, 0) if isinstance(n, int) else n - 1

        block = ctx.enter_context(nc.Block())

        @block.sync
        def _(sp):
            for t in range(TT):
                sp.dma_start(x_sb[:, t * D:(t + 1) * D], x[t * P:(t + 1) * P, :]).then_inc(x_in[t], 16)
            sources = {"in_a": w_in_full[0], "in_b": w_in_full[1], "in_cqk": w_in_full[2], "in_cvdq": w_in_full[3],
                       "in_tail": w_in_tail, "w1": w1, "branch01": w_branch[0], "branch23": w_branch[1],
                       "out0": w_out[0], "out1": w_out[1]}
            for br in range(4):
                for n2 in range(4):
                    sources[f"g{br}_{n2}"] = w_gates[4 * br + n2]
            last_in = {}

            def after_last_chunk(s):
                if s in last_in:
                    bank, _, full = items[CHUNK_LAST[last_in[s]]]
                    sp.wait_ge(bank_full[bank], full)

            for i, name in enumerate(CHUNKS):
                s = CHUNK_SLOT[i]
                after_last_chunk(s)
                src = sources[name]
                sp.dma_start(slot[s][:, 0:src.shape[1]], src).then_inc(slot_full[s], 16)
                last_in[s] = name
            last_in[0] = "g%d_%d" % GATE_ORDER[-1]
            for p in range(2):
                for j, s in enumerate(PAIR_SLOTS[p]):
                    after_last_chunk(s)
                    sp.dma_start(slot[s], w_moe[3 * p + j]).then_inc(slot_full[s], 16)

            def load_experts(c, first):
                with sp.Fori(first, PAIRS // 2) as it:
                    for p in range(2):
                        for j, s in enumerate(PAIR_SLOTS[p]):
                            sp.wait_ge(down_done if j == 2 else gu_done, it * 2 + c * PAIRS + (p - 1))
                            sp.dma_start(slot[s], w_moe[bass.ds(it * 6 + (3 * p + j), 1), :, :]
                                         .rearrange("o p n -> (o p) n")).then_inc(slot_full[s], 16)

            load_experts(0, 1)
            sp.wait_ge(count_ready, 1)
            most = sp.value_load(cmax_i[0:1, 0:1], min_val=0, max_val=S)
            with sp.If(most > CAP):
                with sp.Fori(1, PASSES) as c:
                    load_experts(c, 0)
            for t in range(TT):
                sp.wait_ge(out_ready, t + 1)
                sp.dma_start(out[t * P:(t + 1) * P, :], x2[:, t * D:(t + 1) * D]).then_inc(out_stored, 16)
            sp.wait_ge(out_stored, 16 * TT)

        @block.gpsimd
        def _(pool):
            pool.wait_ge(vec_ready, 1)
            pool.dma_start(bias_rows.ap(), vec.unsqueeze(1).broadcast_to([NB, BIAS_ROWS, MW_BIAS])
                           ).then_inc(rows_stored, 16)
            pool.wait_ge(rows_stored, 16)
            for heads, first, dst in ((8, 0, bias8), (4, 8, bias4)):
                for q in range(0, P, BIAS_ROWS):
                    src = bass.AP(tensor=bias_rows, offset=first * BIAS_ROWS * MW_BIAS + P - 1 - q,
                                  ap=[[MW_BIAS - 1, BIAS_ROWS], [BIAS_ROWS * MW_BIAS, heads], [1, dst.shape[2]]])
                    pool.dma_start(dst[q:q + BIAS_ROWS], src).then_inc(bias_in, 16)
            pool.wait_ge(hT_hi_ready, 1)
            nc.gpsimd.tensor_tensor(hT_lo, hT[:, :], hT_hi.bitcast(f32), ALU.subtract).then_inc(hT_lo_ready, 1)
            for i, (br, n2) in enumerate(GATE_ORDER):
                s = CHUNK_SLOT[CHUNKS.index(f"g{br}_{n2}")]
                lo, hi = parts[s]
                pool.wait_ge(gate_hi_ready, i + 1)
                nc.gpsimd.tensor_tensor(lo, slot[s][:, 0:HALF], hi.bitcast(f32), ALU.subtract
                                        ).then_inc(gate_lo_ready, 1)
            pool.wait_ge(merged_ready, 4)
            pool.dma_start(gfin, g_fin.partition_broadcast(P)).then_inc(norm_g_in, 16)
            nc.gpsimd.memset(xg_all[:, :, 2 * S:SLOT_COLS], 0.0).then_inc(xg_pad, 1)
            for t in range(TT):
                pool.wait_ge(h2_hi_ready, t + 1)
                c = slice(t * D, (t + 1) * D)
                nc.gpsimd.tensor_tensor(h2_lo[:, c], h2[:, c], h2_hi[:, c].bitcast(f32), ALU.subtract
                                        ).then_inc(h2_lo_ready, 1)

        @block.tensor
        def _(pe):
            mm = nc.tensor.matmul
            ident = par("ident")

            def begin(name):
                bank, use, _ = items[name]
                if use:
                    pe.wait_ge(bank_free[bank], use)
                return psum[bank]

            def end(name, last):
                last.then_inc(bank_full[items[name][0]], 1)

            def chunk(name):
                i = CHUNKS.index(name)
                pe.wait_ge(slot_full[CHUNK_SLOT[i]], 16 * (chunk_use(i) + 1))
                return slot[CHUNK_SLOT[i]]

            def hT_t(k, t):
                return hT[:, k * S + t * P:k * S + (t + 1) * P]

            def channels(dst, w, width, col, n=P):
                for k in range(KT):
                    last = mm(dst, w[:, k * width + col:k * width + col + n], hT[:, k * S:(k + 1) * S],
                              start=(k == 0), stop=(k == KT - 1))
                return last

            pe.wait_ge(params_a_in, 16)
            b = begin("vec")
            end("vec", mm(b[0:NB, :], par("tab")[0:BUCKETS + 2, :], par("onehot")[0:BUCKETS + 2, :],
                          start=True, stop=True))
            for j in range(4):
                b = begin(f"xT{j}")
                for k in (2 * j, 2 * j + 1):
                    for t in range(TT):
                        if j == 0 and k == 0:
                            pe.wait_ge(xn_ready, t + 1)
                        last = nc.tensor.transpose(b[:, (k % 2) * S + t * P:(k % 2) * S + (t + 1) * P],
                                                   xn[:, t * D + k * P:t * D + (k + 1) * P], ident)
                end(f"xT{j}", last)
            pe.wait_ge(hT_a, 2)
            pe.wait_ge(hT_d, 2)

            def two_blocks(name, w, width, cols):
                b = begin(name)
                for j, col in enumerate(cols):
                    last = channels(b[:, j * S:(j + 1) * S], w, width, col)
                end(name, last)
                return last

            def tokens(dst, w, width, t, col, n):
                for k in range(KT):
                    last = mm(dst, hT_t(k, t), w[:, k * width + col:k * width + col + n],
                              start=(k == 0), stop=(k == KT - 1))
                return last

            w = chunk("in_a")
            two_blocks("ax", w, 512, (0, P))
            last = two_blocks("ag", w, 512, (2 * P, 3 * P))
            w = chunk("in_b")
            two_blocks("bq", w, 512, (0, P))
            b = begin("bkvb")
            channels(b[:, 0:S], w, 512, 2 * P)
            for t in range(TT):
                last = tokens(b[:, S + t * P:S + (t + 1) * P], w, 512, t, 3 * P, P)
            end("bkvb", last)
            w = chunk("in_tail")
            two_blocks("kcks", w, IN_TAIL, (0, P))
            b = begin("vsg")
            for t in range(TT):
                tokens(b[:, t * P:(t + 1) * P], w, IN_TAIL, t, 2 * P, P)
            for t in range(TT):
                last = tokens(b[:, S + t * NB:S + (t + 1) * NB], w, IN_TAIL, t, 384, NB)
            end("vsg", last)

            def scores(f, q, k_of, d, rows_of):
                for part, heads in (("a", (0, 2)), ("b", (1, 3))):
                    b0, b1 = begin(f"s_{f}_{part}0"), begin(f"s_{f}_{part}1")
                    for j, h in enumerate(heads):
                        r, c = rows_of(h)
                        last0 = mm(b0[:, j * P:(j + 1) * P], q[r:r + d, c:c + P], k_of(h)[:, 0:P],
                                   start=True, stop=True)
                        last1 = mm(b1[:, j * S:(j + 1) * S], q[r:r + d, c + P:c + S], k_of(h), start=True, stop=True)
                    end(f"s_{f}_{part}0", last0)
                    end(f"s_{f}_{part}1", last1)

            def rows64(h):
                return DH * (h % 2), S * (h // 2)

            w = chunk("in_cqk")
            two_blocks("cq", w, 512, (0, P))
            two_blocks("ck", w, 512, (2 * P, 3 * P))

            w = chunk("w1")
            pe.wait_ge(blocks_ready, 1)
            b = begin("h1")
            for kv, src in enumerate((kc2, vc2)):
                src3 = src[:, :].rearrange("p (c i) -> p i c", i=16)
                for i in range(16):
                    last = mm(b[kv * DH:(kv + 1) * DH, 0:NCMP], w[:, kv * 1024 + i * DH:kv * 1024 + (i + 1) * DH],
                              src3[:, i, 0:NCMP], start=(i == 0), stop=(i == 15))
            end("h1", last)

            pe.wait_ge(bq_ready, 1)
            pe.wait_ge(kb_ready, 1)
            scores("swa", bq, lambda h: kb[DH * (h % 2):DH * (h % 2) + DH, S * (h // 2):S * (h // 2) + S], DH, rows64)

            pe.wait_ge(params_b_in, 16)
            pe.wait_ge(xc_ready, 1)
            for name, wname in (("lr", "w_a"), ("lx", "w_x")):
                b = begin(name)
                for cb in range(2):
                    for half in range(2):
                        r = DH * half
                        last = mm(b[r:r + DH, cb * S:(cb + 1) * S], par(wname)[r:r + DH, cb * DH:(cb + 1) * DH],
                                  xc[r:r + DH, cb * S:(cb + 1) * S], start=True, stop=True)
                end(name, last)

            def diff_scores(m):
                def k_of(h):
                    r = DH * (h % 2) + 32 * m
                    return ck[r:r + 32, S * (h // 2):S * (h // 2) + S]
                scores(f"diff{m}", cq, k_of, 32, lambda h: (DH * (h % 2) + 32 * m, S * (h // 2)))

            pe.wait_ge(cq_ready, 1)
            pe.wait_ge(ck_ready, 1)
            diff_scores(0)
            w = chunk("in_cvdq")
            b = begin("vc")
            for t in range(TT):
                last = tokens(b[:, t * 256:(t + 1) * 256], w, 512, t, 0, 256)
            end("vc", last)
            two_blocks("dq", w, 512, (2 * P, 3 * P))
            diff_scores(1)

            def gate_item(br, n2):
                name = f"g{br}_{n2}"
                lo, hi = parts[CHUNK_SLOT[CHUNKS.index(name)]]
                pe.wait_ge(hT_lo_ready, 1)
                pe.wait_ge(gate_lo_ready, GATE_ORDER.index((br, n2)) + 1)
                b = begin(name)
                for j in range(2):
                    for k in range(KT):
                        c, h = slice(k * S + j * P, k * S + (j + 1) * P), slice(k * S, (k + 1) * S)
                        mm(b[:, j * S:(j + 1) * S], hi[:, c], hT_hi[:, h], start=(k == 0), stop=False)
                        mm(b[:, j * S:(j + 1) * S], hi[:, c], hT_lo[:, h], start=False, stop=False)
                        last = mm(b[:, j * S:(j + 1) * S], lo[:, c], hT_hi[:, h], start=False, stop=(k == KT - 1))
                end(name, last)

            def transposes(f, h):
                if h == 0:
                    pe.wait_ge(p_ready, TP_FAMS.index(f) + 1)
                buf = fam_buf[TP_BUF[f]]
                b = begin(f"tp_{f}_{h}")
                nc.tensor.transpose(b[:, 0:P], buf[:, 1024 + h * P:1024 + (h + 1) * P], ident)
                nc.tensor.transpose(b[:, P:2 * P], buf[:, h * S:h * S + P], ident)
                last = nc.tensor.transpose(b[:, 2 * P:3 * P], buf[:, h * S + P:(h + 1) * S], ident)
                end(f"tp_{f}_{h}", last)

            def pt_of(f, h):
                u = TP_FAMS.index(f) * NH + h
                pe.wait_ge(pt_ready, u + 1)
                return pt[:, (u % 4) * 384:(u % 4 + 1) * 384]

            def values(dst, f, h, v_of, start=True, stop=True):
                p = pt_of(f, h)
                mm(dst[:, 0:S], v_of(0), p[:, 0:S], start=start, stop=False)
                mm(dst[:, P:S], v_of(1), p[:, S:S + P], start=False, stop=stop).then_inc(pt_used, 1)

            pe.wait_ge(h1_ready, 1)
            b = begin("kc2")
            mm(b[0:DH, 0:NCMP], par("w2")[0:DH, :], h1b[0:DH, :], start=True, stop=True)
            last = mm(b[DH:P, 0:NCMP], par("w2")[0:DH, :], h1b[0:DH, :], start=True, stop=True)
            end("kc2", last)
            b = begin("vc2")
            end("vc2", mm(b[0:NCMP, 0:DH], h1b[DH:P, :], par("w2")[DH:P, :], start=True, stop=True))
            gate_item(0, 0)
            gate_item(0, 1)
            pe.wait_ge(v_ready, 3)
            yb_bank = [begin("yb0"), begin("yb1")]

            def swa_values(h):
                r = DH * (h % 2)
                values(yb_bank[h // 2][r:r + DH, :], "swa", h,
                       lambda t: v_b[:, t * P + DH * (h // 2):t * P + DH * (h // 2) + DH])

            transposes("swa", 0)
            for h in range(1, NH):
                transposes("swa", h)
                swa_values(h - 1)
            swa_values(NH - 1)

            pe.wait_ge(kc2_ready, 1)
            pe.wait_ge(dq_ready, 1)
            for part, heads in (("a", (0, 2)), ("b", (1, 3))):
                b = begin(f"sc_{part}")
                for t in range(TT):
                    for j, h in enumerate(heads):
                        r, c = rows64(h)
                        last = mm(b[:, (t * 2 + j) * 16:(t * 2 + j) * 16 + NCMP],
                                  dq[r:r + DH, c + t * P:c + (t + 1) * P], kcT[r:r + DH, :], start=True, stop=True)
                end(f"sc_{part}", last)
            pe.wait_ge(ks_ready, 1)
            scores("sel", dq, lambda h: ks2[DH * (h % 2):DH * (h % 2) + DH, :], DH, rows64)
            gate_item(0, 2)
            gate_item(0, 3)

            transposes("diff", 0)
            oc_bank = None

            def diff_values(h):
                p = pt_of("diff", h)
                mm(oc_bank[:, h * DH:(h + 1) * DH], p[:, 0:P], v_c[:, h * DH:(h + 1) * DH], start=True, stop=True)
                mm(oc_bank[:, 256 + h * DH:256 + (h + 1) * DH], p[:, P:2 * P], v_c[:, h * DH:(h + 1) * DH],
                   start=True, stop=False)
                return mm(oc_bank[:, 256 + h * DH:256 + (h + 1) * DH], p[:, 2 * P:3 * P],
                          v_c[:, 256 + h * DH:256 + (h + 1) * DH], start=False, stop=True).then_inc(pt_used, 1)

            for h in range(1, NH):
                transposes("diff", h)
            oc_bank = begin("oc")
            for h in range(NH):
                diff_values(h)
            scores("win", dq, lambda h: kw2[DH * (h % 2):DH * (h % 2) + DH, :], DH, rows64)
            gate_item(1, 0)
            gate_item(1, 1)
            pe.wait_ge(oc_ready, 1)
            b = begin("ycT")
            for j in range(2):
                for t in range(TT):
                    last = nc.tensor.transpose(b[:, j * S + t * P:j * S + (t + 1) * P],
                                               o_c[:, t * 256 + j * P:t * 256 + (j + 1) * P], ident)
            end("ycT", last)

            yd_bank = [begin("yd0"), begin("yd1")]

            def nsa_values(f, h, v_at, start):
                r = DH * (h % 2)
                values(yd_bank[h // 2][r:r + DH, :], f, h,
                       lambda t: v_sw[:, t * P + v_at:t * P + v_at + DH], start=start, stop=False)

            transposes("sel", 0)
            for h in range(1, NH):
                transposes("sel", h)
                nsa_values("sel", h - 1, 0, True)
            nsa_values("sel", NH - 1, 0, True)
            pe.wait_ge(pc_ready, 1)
            for j in range(2):
                b = begin(f"tpc{j}")
                for h in (2 * j, 2 * j + 1):
                    for t in range(TT):
                        last = nc.tensor.transpose(b[0:NCMP, (h % 2) * S + t * P:(h % 2) * S + (t + 1) * P],
                                                   pc_s[:, (t * NH + h) * 16:(t * NH + h) * 16 + NCMP], ident)
                end(f"tpc{j}", last)
            gate_item(1, 2)
            gate_item(1, 3)
            transposes("win", 0)
            for h in range(1, NH):
                transposes("win", h)
                nsa_values("win", h - 1, DH, False)
            nsa_values("win", NH - 1, DH, False)
            pe.wait_ge(pcT_ready, 2)
            for h in range(NH):
                r = DH * (h % 2)
                last = mm(yd_bank[h // 2][r:r + DH, 0:S], vc_d[0:NCMP, :], pcT[0:NCMP, h * S:(h + 1) * S],
                          start=False, stop=True)
                if h % 2:
                    last.then_inc(bank_full[6 + h // 2], 1)

            ys = (ya, yb, yc, yd)
            pe.wait_ge(ya_ready, 1)
            pe.wait_ge(yb_ready, 2)
            for n2 in range(4):
                for br in range(4):
                    if br >= 2:
                        gate_item(br, n2)
                    if n2 == 0 and br == 2:
                        pe.wait_ge(yc_ready, 1)
                    if n2 == 0 and br == 3:
                        pe.wait_ge(yd_ready, 2)
                    w = chunk("branch01" if br < 2 else "branch23")
                    b = begin(f"b{n2}_{br}")
                    for j in range(2):
                        n = 2 * n2 + j
                        for k in range(2):
                            last = mm(b[:, j * S:(j + 1) * S], w[:, (br % 2) * 2048 + k * D + n * P:
                                                                 (br % 2) * 2048 + k * D + (n + 1) * P],
                                      ys[br][:, k * S:(k + 1) * S], start=(k == 0), stop=(k == 1))
                    end(f"b{n2}_{br}", last)
            pe.wait_ge(merged_ready, 4)
            for nh in range(2):
                w = chunk(f"out{nh}")
                for t in range(TT):
                    b = begin(f"x1_{t}{nh}")
                    for k in range(KT):
                        last = mm(b[:, :], merged[:, k * S + t * P:k * S + (t + 1) * P],
                                  w[:, k * 512:(k + 1) * 512], start=(k == 0), stop=(k == KT - 1))
                    end(f"x1_{t}{nh}", last)

            h2T_banks = [begin(f"hT{j}") for j in range(4)]
            for t in range(TT):
                pe.wait_ge((h2_a, h2_d)[t], 1)
                for k in range(KT):
                    b = h2T_banks[k // 2]
                    last = nc.tensor.transpose(b[:, (k % 2) * S + t * P:(k % 2) * S + (t + 1) * P],
                                               h2[:, t * D + k * P:t * D + (k + 1) * P], ident)
                    if t and k % 2:
                        end(f"hT{k // 2}", last)
            pe.wait_ge(h2T_ready, 4)
            b = begin("rl")
            for t in range(TT):
                for k in range(KT):
                    last = mm(b[:, t * 36:(t + 1) * 36], hT_t(k, t), par("w_router")[:, k * 36:(k + 1) * 36],
                              start=(k == 0), stop=(k == KT - 1))
            end("rl", last)
            pe.wait_ge(sel_ready, 1)
            b = begin("rank")
            sel3 = selm.rearrange("p (t e) -> p t e", t=TT)
            mm(b[:, 0:36], par("upper"), sel3[:, 0, :], start=True, stop=True)
            mm(b[:, 36:72], par("ones"), sel3[:, 0, :], start=True, stop=False)
            mm(b[:, 36:72], par("upper"), sel3[:, 1, :], start=False, stop=True)
            mm(b[:, 72:108], par("ones"), sel3[:, 0, :], start=True, stop=False)
            last = mm(b[:, 72:108], par("ones"), sel3[:, 1, :], start=False, stop=True)
            end("rank", last)

            pe.wait_ge(h2_hi_ready, 2)
            pe.wait_ge(h2_lo_ready, 2)
            pe.wait_ge(slots_ready, 1)
            for k in range(KT):
                b = begin(f"xg{k}")
                for t in range(TT):
                    for part in (h2_hi, h2_lo):
                        last = mm(b[:, :], part[:, t * D + k * P:t * D + (k + 1) * P],
                                  onehot_all[:, t * 512:(t + 1) * 512], start=(t == 0 and part is h2_hi),
                                  stop=(t == 1 and part is h2_lo))
                end(f"xg{k}", last)

            y_bank, gu_bank, tr_bank, cd = psum[0:4], psum[4], psum[5], psum[6:8]
            for bk in range(8):
                if bank_uses[bk]:
                    pe.wait_ge(bank_free[bk], bank_uses[bk])
            zeros512 = zeros16[:, :].unsqueeze(1).broadcast_to([P, 4, P])
            for bk in y_bank:
                mm(bk[:, :], zeros16[:, :], zeros512, start=True, stop=False, skip_group_check=True)

            def scatter(tb):
                for t in range(TT):
                    for nh in range(2):
                        last = mm(y_bank[2 * t + nh][:, :], tb[:, 256 + t * P:256 + (t + 1) * P],
                                  yexp[:, nh * 512:(nh + 1) * 512], start=False, stop=False, skip_group_check=True)

            tbs, xgs = (tb0, tb1), (xg0, xg1)

            def gate_up(c, i, p, nth_load):
                n = i + c * PAIRS
                pe.wait_ge(xg_a, n + 1)
                pe.wait_ge(xg_d, n + 1)
                wait_past(pe, he_ready, n)
                s_gu = PAIR_SLOTS[p][0:2]
                for s in s_gu:
                    pe.wait_ge(slot_full[s], (nth_load + (c * (PAIRS // 2) + expert_base(s) + 1)) * 16)
                for k in range(KT):
                    for e in range(2):
                        last = mm(gu_bank[e * CAP:(e + 1) * CAP, :], xgs[p][:, k * P + e * CAP:k * P + (e + 1) * CAP],
                                  slot[s_gu[e]][:, k * 512:(k + 1) * 512], start=(k == 0), stop=(k == KT - 1))
                last.then_inc(gu_done, 1)

            def down(c, i, p, nth_load):
                n = i + c * PAIRS
                pe.wait_ge(tb_ready, n + 1)
                wait_past(pe, yexp_a, n)
                wait_past(pe, yexp_d, n)
                s = PAIR_SLOTS[p][2]
                pe.wait_ge(slot_full[s], (nth_load + (c * (PAIRS // 2) + expert_base(s) + 1)) * 16)
                for nh in range(2):
                    for j in range(2):
                        for e in range(2):
                            last = mm(cd[nh][e * CAP:(e + 1) * CAP, :],
                                      tbs[p][:, j * P + e * CAP:j * P + (e + 1) * CAP],
                                      slot[s][:, e * 2048 + j * D + nh * 512:e * 2048 + j * D + (nh + 1) * 512],
                                      start=(j == 0), stop=(j == 1))
                last.then_inc(down_done, 1)

            def transposed(c, i, p):
                n = i + c * PAIRS
                pe.wait_ge(he_ready, n + 1)
                pe.wait_ge(weighted_ready, n + 1)
                wait_past(pe, tb_ready, n)
                for j in range(2):
                    nc.tensor.transpose(tr_bank[:, j * P:(j + 1) * P], he[:, j * P:(j + 1) * P], ident)
                for t in range(TT):
                    last = nc.tensor.transpose(tr_bank[:, 256 + t * P:256 + (t + 1) * P],
                                               (gc0, gc1)[p][:, t * P:(t + 1) * P], ident)
                last.then_inc(tr_done, 1)

            def outputs_onto_tokens(c, i, p):
                n = i + c * PAIRS
                pe.wait_ge(yexp_a, n + 1)
                pe.wait_ge(yexp_d, n + 1)
                scatter(tbs[p])

            def pair_step(c, i, p, nth_load, nth_load_before):
                gate_up(c, i, p, nth_load)
                down(c, i - 1, 1 - p, nth_load_before)
                transposed(c, i, p)
                outputs_onto_tokens(c, i - 1, 1 - p)

            def expert_pass(c):
                gate_up(c, 0, 0, 0)
                transposed(c, 0, 0)
                with pe.Fori(0, PAIRS // 2 - 1) as it:
                    pair_step(c, it * 2 + 1, 1, it, it)
                    pair_step(c, it * 2 + 2, 0, it + 1, it)
                pair_step(c, PAIRS - 1, 1, PAIRS // 2 - 1, PAIRS // 2 - 1)
                down(c, PAIRS - 1, 1, PAIRS // 2 - 1)
                outputs_onto_tokens(c, PAIRS - 1, 1)

            expert_pass(0)
            pe.wait_ge(count_ready, 1)
            most = pe.value_load(cmax_i[0:1, 0:1], min_val=0, max_val=S)
            with pe.If(most > CAP):
                with pe.Fori(1, PASSES) as c:
                    expert_pass(c)
            for bk in y_bank:
                last = mm(bk[:, :], zeros16[:, :], zeros512, start=False, stop=True, skip_group_check=True)
            last.then_inc(x2_ready, 1)

        @block.scalar
        def _(act):
            step = [0]

            def link(ins):
                step[0] += 1
                ins.then_inc(act_step, 1)
                act.wait_ge(act_step, step[0])

            f = nc.scalar.activation

            def full(name):
                bank, _, value = items[name]
                act.wait_ge(bank_full[bank], value)
                return psum[bank]

            def free(name):
                return bank_free[items[name][0]]

            act.dma_start(par_a[:, :], pa).then_inc(params_a_in, 16)
            act.dma_start(par_b[:, :], pb).then_inc(params_b_in, 16)
            for t in range(TT):
                act.wait_ge(x_in[t], 16)
                f(xn[:, t * D:(t + 1) * D], x_sb[:, t * D:(t + 1) * D], ACT.Square,
                  accum_out=ss[:, t:t + 1]).then_inc(squares_ready, 1)
            act.wait_ge(ms_ready, 1)
            f(rt[:, :], ss[:, :], ACT.Sqrt).then_inc(root_ready, 1)
            act.wait_ge(sp_in, 1)
            f(sp_b[:, :], sp_a[:, :], ACT.Exp).then_inc(sp_exp, 1)
            act.wait_ge(lam_in, 1)
            f(lam4[:, 2:4], lam4[:, 0:2], ACT.Exp).then_inc(lam_exp, 1)

            def h_transposed(j):
                b = full(f"xT{j}")
                f(hT[:, 2 * j * S:(2 * j + 1) * S], b[:, 0:S], ACT.Copy, scale=par("mix_g")[:, 2 * j:2 * j + 1])
                f(hT[:, (2 * j + 1) * S:(2 * j + 2) * S], b[:, S:2 * S], ACT.Copy,
                  scale=par("mix_g")[:, 2 * j + 1:2 * j + 2]).then_inc(free(f"xT{j}"), 1)
                act.wait_ge(free(f"xT{j}"), items[f"xT{j}"][1] + 1)
                act.sem_inc(hT_a, 1)

            act.wait_ge(params_a_in, 16)
            h_transposed(0)
            h_transposed(2)
            act.wait_ge(ax_pads, 1)
            b = full("ax")
            f(ax[:, :].rearrange("p (c s) -> p c s", c=2)[:, :, 3:S + 3], b[:, :].rearrange("p (c s) -> p c s", c=2),
              ACT.Copy).then_inc(free("ax"), 1)
            act.wait_ge(free("ax"), items["ax"][1] + 1)
            act.sem_inc(ax_ready, 1)

            def copy_out(name, dst, ready):
                b = full(name)
                f(dst[:, :], b[:, :], ACT.Copy).then_inc(free(name), 1)
                act.wait_ge(free(name), items[name][1] + 1)
                act.sem_inc(ready, 1)

            copy_out("bq", bq, bq_ready)
            f(hT_hi, hT[:, :], ACT.Copy).then_inc(hT_hi_ready, 1)

            def gate_first_part(i):
                br, n2 = GATE_ORDER[i]
                n = CHUNKS.index(f"g{br}_{n2}")
                s = CHUNK_SLOT[n]
                act.wait_ge(slot_full[s], 16 * (chunk_use(n) + 1))
                f(parts[s][1], slot[s][:, 0:HALF], ACT.Copy).then_inc(gate_hi_ready, 1)

            b = full("kcks")
            for half in range(2):
                r = half * DH
                f(kc2[r:r + DH, :], b[0:DH, 0:S], ACT.Copy)
                f(vc2[r:r + DH, :], b[DH:P, 0:S], ACT.Copy)
                f(ks2[r:r + DH, :], b[0:DH, S:2 * S], ACT.Copy)
                last = f(kw2[r:r + DH, :], b[DH:P, S:2 * S], ACT.Copy)
            last.then_inc(free("kcks"), 1)
            act.wait_ge(free("kcks"), items["kcks"][1] + 1)
            act.sem_inc(kc_ready, 1)
            act.sem_inc(ks_ready, 1)
            act.wait_ge(dgate_raw, 1)
            f(gsig[:, :], gsig[:, :], ACT.Tanh, scale=0.5).then_inc(dgate_tanh, 1)

            def exps(fam):
                n = FAM_NO[fam]
                act.wait_ge(neg_ready, n + 1)
                for j, (probs, o) in enumerate(((fam_q1(fam), 0), (fam_q0(fam), 4))):
                    for h in range(NH):
                        c = n * 8 + o + h
                        last = f(probs[:, h, :], probs[:, h, :], ACT.Exp, bias=negm[:, c:c + 1],
                                 accum_out=den[:, c:c + 1])
                if fam == "swa":
                    last.then_inc(act_step, 1)
                    step[0] += 1
                    act.wait_ge(act_step, step[0])
                    last = f(es[:, :], es[:, :], ACT.Exp)
                last.then_inc(exp_ready, 1)

            copy_out("cq", cq, cq_ready)
            gate_first_part(0)
            act.wait_ge(h1_raw, 1)
            f(h1a[:, :], h1a[:, :], ACT.Tanh, scale=GELU_K).then_inc(h1_tanh, 1)
            exps("swa")
            gate_first_part(1)
            act.wait_ge(lru_par_ready, 1)
            act.wait_ge(gelu_in, 1)
            f(lru_w[:, :], lru_w[:, :], ACT.Tanh, scale=GELU_K)
            for name, dst, bias in (("lr", lru_tr, bga), ("lx", lru_ti, bgx)):
                b = full(name)
                for cb in range(2):
                    last = f(dst[:, cb * S:(cb + 1) * S], b[:, cb * S:(cb + 1) * S], ACT.Tanh, scale=0.5,
                             bias=bias[:, cb:cb + 1])
                last.then_inc(free(name), 1)
                act.wait_ge(free(name), items[name][1] + 1)
            for cb in range(2):
                last = f(lru_t[:, cb * S:(cb + 1) * S], lru_tr[:, cb * S:(cb + 1) * S], ACT.Tanh,
                         scale=sp2[:, cb:cb + 1], bias=sp2[:, cb:cb + 1])
            link(last)
            exps("diff0")
            gate_first_part(2)
            copy_out("dq", dq, dq_ready)
            gate_first_part(3)
            exps("diff1")
            f(lru_s[:, :], lru_t[:, :], ACT.Sqrt).then_inc(lru_tanh_ready, 1)

            gate_no = [0]

            def gate_tanh(br, n2, dst):
                b = full(f"g{br}_{n2}")
                for j in range(2):
                    n = 2 * n2 + j
                    last = f(dst[:, j * S:(j + 1) * S], b[:, j * S:(j + 1) * S], ACT.Tanh, scale=0.5,
                             bias=bgh[:, br * KT + n:br * KT + n + 1])
                last.then_inc(free(f"g{br}_{n2}"), 1)
                act.wait_ge(free(f"g{br}_{n2}"), items[f"g{br}_{n2}"][1] + 1)
                act.sem_inc(gate_ready, 1)

            def early_gate(br, n2):
                gate_tanh(br, n2, gates[:, br * KT * S + n2 * 512:br * KT * S + (n2 + 1) * 512])

            def probs_out(fam, h):
                u = TP_FAMS.index(fam) * NH + h
                b = full(f"tp_{fam}_{h}")
                if u >= 4:
                    act.wait_ge(pt_used, u - 3)
                f(pt[:, (u % 4) * 384:(u % 4 + 1) * 384], b[:, 0:384], ACT.Copy).then_inc(pt_ready, 1)
                act.wait_ge(pt_ready, u + 1)
                act.sem_inc(free(f"tp_{fam}_{h}"), 1)

            early_gate(0, 0)
            early_gate(0, 1)
            act.wait_ge(bias_in, 16 * 2 * P // BIAS_ROWS)
            for h in range(NH):
                probs_out("swa", h)
            gate_first_part(4)
            exps("sel")
            act.wait_ge(cmp_in, 1)
            f(pc_s[:, :].rearrange("p (a c) -> p a c", c=16)[:, :, 0:NCMP],
              pc_s[:, :].rearrange("p (a c) -> p a c", c=16)[:, :, 0:NCMP], ACT.Exp).then_inc(cmp_exp, 1)
            early_gate(0, 2)
            early_gate(0, 3)
            for h in range(NH):
                probs_out("diff", h)
            gate_first_part(5)
            gate_first_part(6)
            act.wait_ge(oc_squares, 1)
            f(rc[:, :], ssc[:, :], ACT.Sqrt).then_inc(oc_root, 1)
            exps("win")
            act.wait_ge(ya_ready, 1)
            early_gate(1, 0)
            early_gate(1, 1)
            for h in range(NH):
                probs_out("sel", h)
            gate_first_part(7)
            gate_first_part(8)
            for j in range(2):
                b = full(f"tpc{j}")
                f(pcT[0:NCMP, j * 512:(j + 1) * 512], b[0:NCMP, :], ACT.Copy).then_inc(free(f"tpc{j}"), 1)
                act.wait_ge(free(f"tpc{j}"), items[f"tpc{j}"][1] + 1)
                act.sem_inc(pcT_ready, 1)
            early_gate(1, 2)
            early_gate(1, 3)
            for h in range(NH):
                probs_out("win", h)
            gate_first_part(9)
            gate_first_part(10)
            for n2 in range(4):
                for br in (2, 3):
                    n = 2 * n2 + br - 2
                    if n:
                        act.wait_ge(late_used, n)
                    else:
                        act.wait_ge(pt_used, 12)
                    gate_tanh(br, n2, late_gate)
                    if 8 + n + 3 < len(GATE_ORDER):
                        gate_first_part(8 + n + 3)
            for t in range(TT):
                act.wait_ge(x1_ready, 2 * (t + 1) if t else 3)
                f(x2[:, t * D:(t + 1) * D], x1[:, t * D:(t + 1) * D], ACT.Square,
                  accum_out=ss[:, t:t + 1]).then_inc(squares_ready, 1)
            act.wait_ge(ms_ready, 2)
            f(rt[:, :], ss[:, :], ACT.Sqrt).then_inc(root_ready, 1)
            act.wait_ge(rstd_ready, 1)
            f(h2[:, 0:D], x1[:, 0:D], ACT.Copy, scale=rstd[:, 0:1]).then_inc(h2_a, 1)
            for j in (0, 2):
                b = full(f"hT{j}")
                for k in (2 * j, 2 * j + 1):
                    last = f(h2T[:, k * S:(k + 1) * S], b[:, (k % 2) * S:(k % 2 + 1) * S], ACT.Copy,
                             scale=par("ffn_g")[:, k:k + 1])
                last.then_inc(free(f"hT{j}"), 1)
                act.wait_ge(free(f"hT{j}"), items[f"hT{j}"][1] + 1)
                act.sem_inc(h2T_ready, 1)
            act.wait_ge(h2_a, 1)
            act.wait_ge(h2_d, 1)
            for t in range(TT):
                f(h2_hi[:, t * D:(t + 1) * D], h2[:, t * D:(t + 1) * D], ACT.Copy).then_inc(h2_hi_ready, 1)
            act.wait_ge(grp_in, 1)
            f(gexp[:, 0:10], gexp[:, 0:10], ACT.Exp).then_inc(grp_exp, 1)

            for k in range(0, KT, 2):
                b = full(f"xg{k}")
                f(xg_all[:, k, 0:2 * S], b[:, :], ACT.Copy, scale=par("ffn_g")[:, k:k + 1]).then_inc(free(f"xg{k}"), 1)
                act.wait_ge(free(f"xg{k}"), items[f"xg{k}"][1] + 1)
            act.sem_inc(xg_all_a, 1)
            act.wait_ge(xg_all_d, 1)
            act.wait_ge(count_ready, 1)

            gu_bank, cd, xgs = psum[4], psum[6:8], (xg0, xg1)

            def tokens_in(c, i, p):
                n = i + c * PAIRS
                at = act.value_load(first_slot_i[0:1, bass.ds(i * 2, 1)], min_val=0, max_val=SLOT_COLS - CAP)
                wait_past(act, gu_done, before_last(n))
                f(xgs[p].rearrange("p (k e s) -> p k e s", k=KT, e=2)[:, :, 0, :],
                  xg_all[:, :, bass.ds(at, CAP)], ACT.Copy).then_inc(xg_a, 1)

            def pair_step(c, i, p, last=False):
                n = i + c * PAIRS
                if not last:
                    tokens_in(c, i + 1, 1 - p)
                act.wait_ge(gu_done, n + 1)
                wait_past(act, he_ready, n)
                f(silu_g[:, :], gu_bank[:, 0:FF], ACT.Silu).then_inc(silu_done, 1)

            def outputs_out(c, i):
                act.wait_ge(down_done, i + c * PAIRS + 1)
                f(yexp[:, 0:512], cd[0][:, :], ACT.Copy).then_inc(yexp_a, 1)

            def expert_pass(c):
                tokens_in(c, 0, 0)
                pair_step(c, 0, 0)
                with act.Fori(0, PAIRS // 2 - 1) as it:
                    for p in (1, 0):
                        i = it * 2 + (1 if p else 2)
                        pair_step(c, i, p)
                        outputs_out(c, i - 1)
                pair_step(c, PAIRS - 1, 1, last=True)
                outputs_out(c, PAIRS - 2)
                outputs_out(c, PAIRS - 1)

            expert_pass(0)
            act.wait_ge(count_ready, 1)
            most = act.value_load(cmax_i[0:1, 0:1], min_val=0, max_val=S)
            with act.If(most > CAP):
                with act.Fori(1, PASSES) as c:
                    act.wait_ge(slots_moved, c)
                    act.sem_inc(pass_begun, 1)
                    expert_pass(c)
            for t in range(TT):
                act.wait_ge(fin_in, t + 1)
                f(h2[:, t * D:(t + 1) * D], x2[:, t * D:(t + 1) * D], ACT.Square,
                  accum_out=ss[:, t:t + 1]).then_inc(fin_squares, 1)
            act.wait_ge(fin_ms, 1)
            f(rt[:, :], ss[:, :], ACT.Sqrt).then_inc(fin_root, 1)

        @block.vector
        def _(dve):
            v = nc.vector
            step = [0]

            def link(ins):
                step[0] += 1
                ins.then_inc(dve_step, 1)
                dve.wait_ge(dve_step, step[0])

            counts = {}

            def tell(ins, s):
                counts[s.name] = counts.get(s.name, 0) + 1
                ins.then_inc(s, 1)
                dve.wait_ge(s, counts[s.name])

            def full(name):
                bank, _, value = items[name]
                dve.wait_ge(bank_full[bank], value)
                return psum[bank]

            def release(name, ins):
                bank, use, _ = items[name]
                ins.then_inc(bank_free[bank], 1)
                dve.wait_ge(bank_free[bank], use + 1)

            def mean_root(n):
                dve.wait_ge(squares_ready, 2 * n)
                tell(v.tensor_scalar(ss[:, :], ss[:, :], 1.0 / D, 1e-6, ALU.mult, ALU.add), ms_ready)
                dve.wait_ge(root_ready, n)
                link(v.reciprocal(rstd[:, :], rt[:, :]))

            tell(v.memset(ax[:, :].rearrange("p (c s) -> p c s", c=2)[:, :, 0:3], 0.0), ax_pads)
            link(v.memset(zeros16[:, :], 0.0))
            b = full("vec")
            release("vec", v.tensor_copy(vec, b[0:NB, :]))
            dve.sem_inc(vec_ready, 1)
            mean_root(1)
            for t in range(TT):
                tell(v.tensor_scalar(xn[:, t * D:(t + 1) * D], x_sb[:, t * D:(t + 1) * D], rstd[:, t:t + 1], None,
                                     ALU.mult), xn_ready)
            dve.wait_ge(params_b_in, 16)
            link(v.tensor_scalar(sp_c[:, :], par("lam"), -1.0, None, ALU.mult))
            tell(v.tensor_tensor(sp_a[:, :], par("lam"), sp_c[:, :], ALU.min), sp_in)
            link(v.tensor_tensor(lru_scratch[:, 0:32], par("lq1"), par("lk1"), ALU.mult))
            link(v.tensor_tensor(lru_scratch[:, 32:64], par("lq2"), par("lk2"), ALU.mult))
            tell(v.reduce_sum(lam4[:, 0:2], lru_scratch[:, 0:64].rearrange("p (a b) -> p a b", a=2), axis=X), lam_in)
            link(v.tensor_scalar(bga[:, :], par("b_a"), 0.5, None, ALU.mult))
            link(v.tensor_scalar(bgx[:, :], par("b_x"), 0.5, None, ALU.mult))
            link(v.tensor_scalar(bgh[:, :], par("b_gate"), 0.5, None, ALU.mult))
            link(v.tensor_scalar(gsubln[:, :], par("subln_g"), 0.8, None, ALU.mult))

            def h_transposed(j):
                b = full(f"xT{j}")
                link(v.tensor_scalar(hT[:, 2 * j * S:(2 * j + 1) * S], b[:, 0:S], par("mix_g")[:, 2 * j:2 * j + 1],
                                     None, ALU.mult))
                release(f"xT{j}", v.tensor_scalar(hT[:, (2 * j + 1) * S:(2 * j + 2) * S], b[:, S:2 * S],
                                                  par("mix_g")[:, 2 * j + 1:2 * j + 2], None, ALU.mult))
                dve.sem_inc(hT_d, 1)

            h_transposed(1)
            h_transposed(3)
            dve.wait_ge(sp_exp, 1)
            link(v.tensor_scalar(sp_a[:, :], sp_b[:, :], 2.0, None, ALU.add))
            link(v.reciprocal(sp_a[:, :], sp_a[:, :]))
            link(v.tensor_tensor(sp_a[:, :], sp_a[:, :], sp_b[:, :], ALU.mult))
            link(v.tensor_tensor(sp_b[:, :], sp_a[:, :], sp_a[:, :], ALU.mult))
            link(v.tensor_scalar(sp2[:, :], sp_b[:, :], 1.0 / 17, 1.0 / 15, ALU.mult, ALU.add))
            for n in (13, 11, 9, 7, 5, 3, 1):
                link(v.tensor_tensor(sp2[:, :], sp2[:, :], sp_b[:, :], ALU.mult))
                link(v.tensor_scalar(sp2[:, :], sp2[:, :], 1.0 / n, None, ALU.add))
            link(v.tensor_tensor(sp2[:, :], sp2[:, :], sp_a[:, :], ALU.mult))
            link(v.tensor_scalar(sp_c[:, :], sp_c[:, :], 0.0, None, ALU.max))
            link(v.tensor_scalar(sp2[:, :], sp2[:, :], 2.0, None, ALU.mult))
            link(v.tensor_tensor(sp2[:, :], sp2[:, :], sp_c[:, :], ALU.add))
            tell(v.tensor_scalar(sp2[:, :], sp2[:, :], 2.0, None, ALU.mult), lru_par_ready)
            dve.wait_ge(lam_exp, 1)
            link(v.tensor_tensor(lam4[:, 4:5], lam4[:, 3:4], lam4[:, 2:3], ALU.subtract))
            link(v.tensor_scalar(lam4[:, 4:5], lam4[:, 4:5], -0.2, None, ALU.add))

            b = full("ag")
            release("ag", v.tensor_copy(ag[:, :], b[:, :]))
            b = full("bkvb")
            for kv in range(2):
                for half in range(2):
                    r = half * DH
                    v.tensor_copy(kb[r:r + DH, kv * S:(kv + 1) * S], b[kv * DH:(kv + 1) * DH, 0:S])
            release("bkvb", v.tensor_copy(v_b[:, :], b[:, S:2 * S]))
            dve.sem_inc(kb_ready, 1)
            dve.sem_inc(v_ready, 1)
            b = full("vsg")
            v.tensor_copy(v_sw[:, :], b[:, 0:S])
            release("vsg", v.tensor_copy(gsig[:, :], b[:, S:S + 2 * NB]))
            dve.sem_inc(dgate_raw, 1)
            dve.sem_inc(v_ready, 1)

            def to_sigmoid():
                dve.wait_ge(dgate_tanh, 1)
                link(v.tensor_scalar(gsig[:, :], gsig[:, :], 0.5, 0.5, ALU.mult, ALU.add))

            def family_scores(fam, scale, bias_h, first):
                n = FAM_NO[fam]
                q1, q0 = fam_q1(fam), fam_q0(fam)
                for part, h in (("a", 0), ("b", 1)):
                    for qt, dst, keys in ((0, q0, slice(P, S)), (1, q1, slice(0, S))):
                        name = f"s_{fam}_{part}{qt}"
                        width = keys.stop - keys.start
                        release(name, v.scalar_tensor_tensor(
                            dst[:, h:NH:2, :], full(name)[:, 0:2 * width].rearrange("p (h k) -> p h k", h=2), scale,
                            bias_h[:, first + h:first + NH:2, keys], ALU.mult, ALU.add))
                c = n * 8
                link(v.reduce_max(mx[:, c:c + 4], q1, axis=X))
                link(v.reduce_max(mx[:, c + 4:c + 8], q0, axis=X))
                if fam == "swa":
                    for j in (0, 4):
                        link(v.tensor_tensor(mx[:, j:j + 4], mx[:, j:j + 4], par("sinks"), ALU.max))
                        link(v.tensor_tensor(es[:, j:j + 4], par("sinks"), mx[:, j:j + 4], ALU.subtract))
                tell(v.tensor_scalar(negm[:, c:c + 8], mx[:, c:c + 8], -1.0, None, ALU.mult), neg_ready)

            def inverse_sums(fam):
                n = FAM_NO[fam]
                dve.wait_ge(exp_ready, n + 1)
                d = den[:, n * 8:n * 8 + 8]
                if fam == "swa":
                    link(v.tensor_tensor(d, d, es[:, :], ALU.add))
                link(v.tensor_scalar(d, d, TINY, None, ALU.max))
                link(v.reciprocal(fac[:, :], d))

            def scale_probs(fam):
                for o, probs in ((0, fam_q1(fam)), (4, fam_q0(fam))):
                    for h in range(NH):
                        last = v.tensor_scalar(probs[:, h, :], probs[:, h, :], fac[:, o + h:o + h + 1], None, ALU.mult)
                return last

            def gate_factors(which):
                g = gsig[:, :].rearrange("p (t h g) -> p t h g", t=TT, h=NH)
                link(v.tensor_tensor(fac[:, 0:4], fac[:, 0:4], g[:, 1, :, which], ALU.mult))
                link(v.tensor_tensor(fac[:, 4:8], fac[:, 4:8], g[:, 0, :, which], ALU.mult))

            dve.wait_ge(kc_ready, 1)
            for src, pos in ((kc2, "pos_k"), (vc2, "pos_v")):
                lo = src[0:DH, :].rearrange("p (c i) -> p c i", i=16)
                hi = src[DH:P, :].rearrange("p (c i) -> p c i", i=16)
                link(v.tensor_tensor(lo, lo, par(pos)[0:DH, :].unsqueeze(1).broadcast_to([DH, 16, 16]), ALU.add))
                link(v.tensor_tensor(hi[:, 0:15, :], hi[:, 1:16, :],
                                     par(pos)[DH:P, :].unsqueeze(1).broadcast_to([DH, 15, 16]), ALU.add))
            dve.sem_inc(blocks_ready, 1)
            dve.wait_ge(ax_ready, 1)
            for cb in range(2):
                src = ax[:, cb * (S + 3):(cb + 1) * (S + 3)]
                dst = xc[:, cb * S:(cb + 1) * S]
                link(v.tensor_scalar(dst, src[:, 0:S], par("conv_w")[:, cb:cb + 1], par("conv_b")[:, cb:cb + 1],
                                     ALU.mult, ALU.add))
                for i in range(1, 4):
                    link(v.scalar_tensor_tensor(dst, src[:, i:i + S], par("conv_w")[:, 2 * i + cb:2 * i + cb + 1], dst,
                                                ALU.mult, ALU.add))
            dve.sem_inc(xc_ready, 1)
            link(v.tensor_tensor(lru_w[:, :], ag[:, :], ag[:, :], ALU.mult))
            link(v.tensor_scalar(lru_w[:, :], lru_w[:, :], GELU_C, 1.0, ALU.mult, ALU.add))
            tell(v.tensor_tensor(lru_w[:, :], lru_w[:, :], ag[:, :], ALU.mult), gelu_in)
            b = full("ck")
            release("ck", v.tensor_copy(ck[:, :], b[:, :]))
            dve.sem_inc(ck_ready, 1)
            b = full("h1")
            release("h1", v.tensor_copy(h1[:, :], b[:, 0:NCMP]))
            link(v.tensor_tensor(h1a[:, :], h1[:, :], h1[:, :], ALU.mult))
            link(v.tensor_scalar(h1a[:, :], h1a[:, :], GELU_C, 1.0, ALU.mult, ALU.add))
            tell(v.tensor_tensor(h1a[:, :], h1a[:, :], h1[:, :], ALU.mult), h1_raw)
            dve.wait_ge(bias_in, 16 * 2 * P // BIAS_ROWS)
            family_scores("swa", DH ** -0.5, bias8, 0)
            dve.wait_ge(h1_tanh, 1)
            link(v.scalar_tensor_tensor(h1b[:, :], h1a[:, :], 1.0, h1[:, :], ALU.add, ALU.mult))
            tell(v.tensor_scalar(h1b[:, :], h1b[:, :], 0.5, None, ALU.mult), h1_ready)
            family_scores("diff0", 32 ** -0.5, bias8, 4)
            inverse_sums("swa")
            tell(scale_probs("swa"), p_ready)
            b = full("vc")
            release("vc", v.tensor_copy(v_c[:, :], b[:, :]))
            dve.sem_inc(v_ready, 1)
            family_scores("diff1", 32 ** -0.5, bias8, 4)
            b = full("kc2")
            release("kc2", v.tensor_copy(kcT[:, :], b[:, 0:NCMP]))
            b = full("vc2")
            release("vc2", v.tensor_copy(vc_d[0:NCMP, :], b[0:NCMP, 0:DH]))
            dve.sem_inc(kc2_ready, 1)
            to_sigmoid()
            inverse_sums("diff1")
            link(v.tensor_scalar(fac[:, :], fac[:, :], lam4[:, 4:5], None, ALU.mult))
            link(scale_probs("diff1"))
            inverse_sums("diff0")
            for o, p0, p1 in ((0, fam_q1("diff0"), fam_q1("diff1")), (4, fam_q0("diff0"), fam_q0("diff1"))):
                for h in range(NH):
                    last = v.scalar_tensor_tensor(p0[:, h, :], p0[:, h, :], fac[:, o + h:o + h + 1], p1[:, h, :],
                                                  ALU.mult, ALU.add)
            tell(last, p_ready)
            for j in range(2):
                dve.wait_ge(pt_used, 2 * j + 2)
                b = psum[items[f"yb{j}"][0]]
                release(f"yb{j}", v.tensor_copy(yb[:, j * S:(j + 1) * S], b[:, 0:S]))
                dve.sem_inc(yb_ready, 1)
            pc3 = pc_s[:, :].rearrange("p (a c) -> p a c", c=16)
            cmask = o_c[:, 256:384].rearrange("p (a c) -> p a c", c=16)
            for t in range(TT):
                at = 31 + P * (1 - t)
                link(v.tensor_scalar(cmask[:, t * 4:t * 4 + 4, 0:NCMP], bias4[:, :, at:at + 16 * (NCMP - 1) + 1:16],
                                     -1e29, None, ALU.is_gt))
            for part, h in (("a", 0), ("b", 1)):
                b = full(f"sc_{part}")
                sc3 = b[:, 0:DH].rearrange("p (a c) -> p a c", c=16)
                for t in range(TT):
                    at = 31 + P * (1 - t)
                    ins = v.scalar_tensor_tensor(pc3[:, t * 4 + h:t * 4 + 4:2, 0:NCMP],
                                                 sc3[:, t * 2:t * 2 + 2, 0:NCMP], DH ** -0.5,
                                                 bias4[:, h:NH:2, at:at + 16 * (NCMP - 1) + 1:16],
                                                 ALU.mult, ALU.add)
                    if t == TT - 1:
                        release(f"sc_{part}", ins)
                    else:
                        link(ins)
            pcv, cmv = pc3[:, :, 0:NCMP], cmask[:, :, 0:NCMP]
            link(v.reduce_max(cmx[:, :], pcv, axis=X))
            tell(v.tensor_tensor(pcv, pcv, cmx[:, :].unsqueeze(2).broadcast_to([P, 8, NCMP]), ALU.subtract), cmp_in)
            family_scores("sel", DH ** -0.5, bias4, 0)
            dve.wait_ge(cmp_exp, 1)
            link(v.tensor_tensor(pcv, pcv, cmv, ALU.mult))
            link(v.reduce_sum(cmx[:, :], pcv, axis=X))
            link(v.tensor_scalar(cmx[:, :], cmx[:, :], TINY, None, ALU.max))
            link(v.reciprocal(cmx[:, :], cmx[:, :]))
            g4 = gsig[:, :].rearrange("p (a g) -> p a g", g=3)
            link(v.tensor_tensor(cmx[:, :], cmx[:, :], g4[:, :, 0], ALU.mult))
            tell(v.tensor_tensor(pcv, pcv, cmx[:, :].unsqueeze(2).broadcast_to([P, 8, NCMP]), ALU.mult), pc_ready)
            inverse_sums("sel")
            gate_factors(1)
            tell(scale_probs("sel"), p_ready)
            dve.wait_ge(lru_tanh_ready, 1)
            link(v.scalar_tensor_tensor(xc[:, :], lru_ti[:, :], 1.0, xc[:, :], ALU.add, ALU.mult))
            xc3 = xc[:, :].rearrange("p (c s) -> p c s", c=2)
            link(v.tensor_scalar(lru_scratch[:, 0:2].unsqueeze(2), xc3[:, :, 0:1], 0.5, None, ALU.mult))
            link(v.tensor_scalar(lru_tr[:, :], lru_t[:, :], 1.0, None, ALU.add))
            link(v.reciprocal(lru_tr[:, :], lru_tr[:, :]))
            link(v.tensor_scalar(lru_t[:, :], lru_t[:, :], -1.0, 1.0, ALU.mult, ALU.add))
            link(v.tensor_tensor(lru_t[:, :], lru_t[:, :], lru_tr[:, :], ALU.mult))
            link(v.tensor_tensor(xc[:, :], xc[:, :], lru_s[:, :], ALU.mult))
            link(v.tensor_tensor(xc[:, :], xc[:, :], lru_tr[:, :], ALU.mult))
            link(v.tensor_copy(xc3[:, :, 0:1], lru_scratch[:, 0:2].unsqueeze(2)))
            for cb in range(2):
                c = slice(cb * S, (cb + 1) * S)
                link(v.tensor_tensor_scan(lru_s[:, c], lru_t[:, c], xc[:, c], 0.0, ALU.mult, ALU.add))
            link(v.scalar_tensor_tensor(ag[:, :], lru_w[:, :], 1.0, ag[:, :], ALU.add, ALU.mult))
            link(v.scalar_tensor_tensor(ya[:, :], lru_s[:, :], 0.5, ag[:, :], ALU.mult, ALU.mult))
            dve.sem_inc(ya_ready, 1)
            dve.wait_ge(pt_used, 8)
            b = psum[items["oc"][0]]
            release("oc", v.tensor_copy(o_c[:, :], b[:, :]))
            link(v.tensor_tensor(xc[:, :], o_c[:, :], o_c[:, :], ALU.mult))
            link(v.reduce_sum(ssc[:, :], xc[:, :].rearrange("p (a d) -> p a d", d=DH), axis=X))
            tell(v.tensor_scalar(ssc[:, :], ssc[:, :], 1.0 / DH, 1e-5, ALU.mult, ALU.add), oc_squares)
            family_scores("win", DH ** -0.5, bias4, 0)
            dve.wait_ge(oc_root, 1)
            link(v.reciprocal(rc[:, :], rc[:, :]))
            oc3 = o_c[:, :].rearrange("p (a d) -> p a d", d=DH)
            tell(v.tensor_tensor(oc3, oc3, rc[:, :].unsqueeze(2).broadcast_to([P, 8, DH]), ALU.mult), oc_ready)
            b = full("ycT")
            release("ycT", v.tensor_scalar(yc[:, :], b[:, :], gsubln[:, 0:1], None, ALU.mult))
            dve.sem_inc(yc_ready, 1)
            inverse_sums("win")
            gate_factors(2)
            tell(scale_probs("win"), p_ready)
            for j in range(2):
                b = full(f"yd{j}")
                release(f"yd{j}", v.tensor_copy(yd[:, j * S:(j + 1) * S], b[:, 0:S]))
                dve.sem_inc(yd_ready, 1)
            dve.wait_ge(pt_used, 16)
            for n2 in range(4):
                dst = merged[:, n2 * 512:(n2 + 1) * 512]
                for br in range(4):
                    dve.wait_ge(gate_ready, 8 if br < 2 else 8 + 2 * n2 + br - 1)
                    g = gates[:, br * KT * S + n2 * 512:br * KT * S + (n2 + 1) * 512] if br < 2 else late_gate
                    b = full(f"b{n2}_{br}")
                    release(f"b{n2}_{br}", v.scalar_tensor_tensor(branch_tmp if br else dst, g, 1.0, b[:, :],
                                                                  ALU.add, ALU.mult))
                    if br >= 2:
                        dve.sem_inc(late_used, 1)
                    if br == 3:
                        tell(v.tensor_tensor(dst, dst, branch_tmp, ALU.add), merged_ready)
                    elif br:
                        link(v.tensor_tensor(dst, dst, branch_tmp, ALU.add))
            for j in range(8):
                last = v.tensor_scalar(iota512[:, j * CAP:(j + 1) * CAP], par("iota"), float(j * CAP), None, ALU.add)
            link(last)
            for nh in range(2):
                for t in range(TT):
                    c = slice(t * D + nh * 512, t * D + (nh + 1) * 512)
                    b = full(f"x1_{t}{nh}")
                    release(f"x1_{t}{nh}", v.scalar_tensor_tensor(x1[:, c], b[:, :], 0.5, x_sb[:, c], ALU.mult,
                                                                  ALU.add))
                    dve.sem_inc(x1_ready, 1)
            mean_root(2)
            dve.sem_inc(rstd_ready, 1)
            tell(v.tensor_scalar(h2[:, D:2 * D], x1[:, D:2 * D], rstd[:, 1:2], None, ALU.mult), h2_d)
            for j in (1, 3):
                b = full(f"hT{j}")
                for k in (2 * j, 2 * j + 1):
                    last = v.tensor_scalar(h2T[:, k * S:(k + 1) * S], b[:, (k % 2) * S:(k % 2 + 1) * S],
                                           par("ffn_g")[:, k:k + 1], None, ALU.mult)
                release(f"hT{j}", last)
                dve.sem_inc(h2T_ready, 1)

            link(v.memset(selm[:, :], 0.0))
            link(v.memset(comb[:, :], 0.0))
            b = full("rl")
            r3 = rlog.rearrange("p (t n) -> p t n", t=TT)
            release("rl", v.tensor_tensor(r3, b[:, 0:72].rearrange("p (t n) -> p t n", t=TT),
                                          par("b_router").unsqueeze(1).broadcast_to([P, TT, 36]), ALU.add))
            lg, le = r3[:, :, 0:GRP], r3[:, :, GRP:36]

            def first_of(onehot, vals, top, n, cand):
                link(v.reduce_max(top, vals, axis=X))
                link(v.tensor_tensor(cand, vals, top.unsqueeze(2).broadcast_to([P, TT, n]), ALU.not_equal))
                iota = par("iota8")[:, 0:n].unsqueeze(1).broadcast_to([P, TT, n])
                link(v.tensor_scalar(cand, cand, 100.0, None, ALU.mult))
                link(v.tensor_tensor(cand, cand, iota, ALU.add))
                link(v.tensor_reduce(wts[:, 6:8], cand, X, ALU.min))
                link(v.tensor_tensor(onehot, iota, wts[:, 6:8].unsqueeze(2).broadcast_to([P, TT, n]), ALU.is_equal))

            og, cg = ogrp.rearrange("p (t n) -> p t n", t=TT), cgrp.rearrange("p (t n) -> p t n", t=TT)
            first_of(og, lg, mgrp, GRP, cg)
            ge = grouped.rearrange("p (t g n) -> p t g n", t=TT, g=GRP)
            og_n = og.unsqueeze(3).broadcast_to([P, TT, GRP, EPG])
            i3 = ing.rearrange("p (t n) -> p t n", t=TT)

            def of_group(dst, by_expert):
                link(v.tensor_tensor(ge, by_expert[:, :, 0:E].rearrange("p t (g n) -> p t g n", g=GRP), og_n, ALU.mult))
                link(v.reduce_sum(dst, ge.rearrange("p t g n -> p t n g"), axis=X))

            def into_group(dst, in_group, ready=None):
                ins = v.tensor_tensor(dst[:, :, 0:E].rearrange("p t (g n) -> p t g n", g=GRP),
                                      in_group.unsqueeze(2).broadcast_to([P, TT, GRP, EPG]), og_n, ALU.mult)
                link(ins)
                if ready is not None:
                    dve.sem_inc(ready, 1)

            of_group(i3, le)
            o13, o23 = o1.rearrange("p (t n) -> p t n", t=TT), o2.rearrange("p (t n) -> p t n", t=TT)
            c83, in23 = c8.rearrange("p (t n) -> p t n", t=TT), in2.rearrange("p (t n) -> p t n", t=TT)
            first_of(o13, i3, v1, EPG, c83)
            link(v.scalar_tensor_tensor(in23, o13, NEG, i3, ALU.mult, ALU.add))
            first_of(o23, in23, v2, EPG, c83)
            s3 = selm.rearrange("p (t n) -> p t n", t=TT)
            k3 = comb.rearrange("p (t n) -> p t n", t=TT)
            link(v.tensor_tensor(c83, o13, o23, ALU.add))
            into_group(s3, c83, sel_ready)
            link(v.tensor_tensor(gexp[:, 0:8].rearrange("p (t n) -> p t n", t=TT), lg,
                                 mgrp.unsqueeze(2).broadcast_to([P, TT, GRP]), ALU.subtract))
            tell(v.tensor_tensor(gexp[:, 8:10], v2, v1, ALU.subtract), grp_in)
            b = full("rank")
            link(v.tensor_copy(cnt[:, :], b[:, 72:108]))
            link(v.tensor_tensor_scan(base[:, :], cnt[:, :], cnt[:, :], 0.0, ALU.add, ALU.max))
            link(v.tensor_tensor(base[:, :], base[:, :], cnt[:, :], ALU.subtract))
            pos3 = place.rearrange("p (t n) -> p t n", t=TT)
            rank3 = b[:, 0:72].rearrange("p (t n) -> p t n", t=TT)
            link(v.tensor_tensor(pos3, rank3, base.unsqueeze(1).broadcast_to([P, TT, 36]), ALU.add))
            pg3 = pos_g.rearrange("p (t n) -> p t n", t=TT)
            of_group(pg3, pos3)
            for j, o in enumerate((o13, o23)):
                link(v.tensor_tensor(c83, pg3, o, ALU.mult))
                link(v.reduce_sum(pos_12[:, 2 * j:2 * j + 2], c83, axis=X))
            for t in range(TT):
                g = onehot_all[:, t * 512:(t + 1) * 512]
                link(v.tensor_scalar(g, iota512[:, :], pos_12[:, t:t + 1], None, ALU.is_equal))
                link(v.scalar_tensor_tensor(g, iota512[:, :], pos_12[:, 2 + t:3 + t], g.bitcast(f32), ALU.is_equal, ALU.add))
            dve.sem_inc(slots_ready, 1)
            sl3 = slotv.rearrange("p (t n) -> p t n", t=TT)
            link(v.scalar_tensor_tensor(sl3, rank3, 1.0, s3, ALU.add, ALU.mult))
            release("rank", v.tensor_scalar(slotv[:, :], slotv[:, :], -1.0, None, ALU.add))
            link(v.reduce_max(cmax[:, :], cnt[:, :], axis=X))
            link(v.tensor_copy(first_slot_i[:, :], base[:, :]))
            tell(v.tensor_copy(cmax_i[:, :], cmax[:, :]), count_ready)
            dve.wait_ge(grp_exp, 1)
            link(v.reduce_sum(gsum, gexp[:, 0:8].rearrange("p (t n) -> p t n", t=TT), axis=X))
            link(v.tensor_scalar(wts[:, 0:2], gexp[:, 8:10], 1.0, None, ALU.add))
            link(v.tensor_tensor(wts[:, 0:2], wts[:, 0:2], gsum, ALU.mult))
            link(v.reciprocal(wts[:, 0:2], wts[:, 0:2]))
            link(v.tensor_tensor(wts[:, 2:4], wts[:, 0:2], gexp[:, 8:10], ALU.mult))
            link(v.tensor_tensor(o13, o13, wts[:, 0:2].unsqueeze(2).broadcast_to([P, TT, EPG]), ALU.mult))
            link(v.tensor_tensor(o23, o23, wts[:, 2:4].unsqueeze(2).broadcast_to([P, TT, EPG]), ALU.mult))
            link(v.tensor_tensor(o13, o13, o23, ALU.add))
            into_group(k3, o13)
            for k in range(1, KT, 2):
                b = full(f"xg{k}")
                release(f"xg{k}", v.tensor_scalar(xg_all[:, k, 0:2 * S], b[:, :], par("ffn_g")[:, k:k + 1], None,
                                                   ALU.mult))
            dve.wait_ge(xg_pad, 1)
            dve.sem_inc(xg_all_d, 1)
            dve.wait_ge(xg_all_a, 1)

            gu_bank, tr_bank, cd = psum[4], psum[5], psum[6:8]
            xgs, gcs, tbs = (xg0, xg1), (gc0, gc1), (tb0, tb1)

            def tokens_in(c, i, p):
                n = i + c * PAIRS
                at = dve.value_load(first_slot_i[0:1, bass.ds(i * 2 + 1, 1)], min_val=0, max_val=SLOT_COLS - CAP)
                wait_past(dve, gu_done, before_last(n))
                v.tensor_copy(xgs[p].rearrange("p (k e s) -> p k e s", k=KT, e=2)[:, :, 1, :],
                              xg_all[:, :, bass.ds(at, CAP)]).then_inc(xg_d, 1)

            def way_back(c, i, p):
                for t in range(TT):
                    for e in range(2):
                        at = bass.ds(i * 2 + (t * 36 + e), 1)
                        last = v.scalar_tensor_tensor(
                            gcs[p][:, t * P + e * CAP:t * P + (e + 1) * CAP], par("iota"), slotv[:, at],
                            comb[:, at].broadcast_to([P, CAP]), ALU.is_equal, ALU.mult)
                last.then_inc(weighted_ready, 1)

            def outputs_out(c, i):
                dve.wait_ge(down_done, i + c * PAIRS + 1)
                v.tensor_copy(yexp[:, 512:1024], cd[1][:, :]).then_inc(yexp_d, 1)

            def pair_step(c, i, p, first=False, last=False):
                n = i + c * PAIRS
                if not last:
                    tokens_in(c, i + 1, 1 - p)
                dve.wait_ge(silu_done, n + 1)
                v.tensor_tensor(he[:, :], silu_g[:, :], gu_bank[:, FF:2 * FF], ALU.mult).then_inc(he_ready, 1)
                if not first:
                    outputs_out(c, i - 1)
                dve.wait_ge(tr_done, n + 1)
                v.tensor_copy(tbs[p], tr_bank[:, :]).then_inc(tb_ready, 1)
                if not last:
                    way_back(c, i + 1, 1 - p)

            def expert_pass(c):
                way_back(c, 0, 0)
                tokens_in(c, 0, 0)
                pair_step(c, 0, 0, first=True)
                with dve.Fori(0, PAIRS // 2 - 1) as it:
                    pair_step(c, it * 2 + 1, 1)
                    pair_step(c, it * 2 + 2, 0)
                pair_step(c, PAIRS - 1, 1, last=True)
                outputs_out(c, PAIRS - 1)

            expert_pass(0)
            most = dve.value_load(cmax_i[0:1, 0:1], min_val=0, max_val=S)
            with dve.If(most > CAP):
                with dve.Fori(1, PASSES) as c:
                    dve.wait_ge(xg_a, c * PAIRS)
                    v.tensor_scalar(slotv[:, :], slotv[:, :], -float(CAP), None, ALU.add)
                    v.tensor_scalar(base[:, :], base[:, :], float(CAP), None, ALU.add).then_inc(base_moved, 1)
                    dve.wait_ge(base_moved, c)
                    v.tensor_copy(first_slot_i[:, :], base[:, :]).then_inc(slots_moved, 1)
                    dve.wait_ge(slots_moved, c)
                    expert_pass(c)
            dve.wait_ge(x2_ready, 1)
            for t in range(TT):
                for nh in range(2):
                    c = slice(t * D + nh * 512, t * D + (nh + 1) * 512)
                    ins = v.tensor_tensor(x2[:, c], psum[2 * t + nh][:, :], x1[:, c], ALU.add)
                ins.then_inc(fin_in, 1)
            dve.wait_ge(norm_g_in, 16)
            dve.wait_ge(fin_squares, 2)
            tell(v.tensor_scalar(ss[:, :], ss[:, :], 1.0 / D, 1e-6, ALU.mult, ALU.add), fin_ms)
            dve.wait_ge(fin_root, 1)
            link(v.reciprocal(rstd[:, :], rt[:, :]))
            for t in range(TT):
                v.scalar_tensor_tensor(x2[:, t * D:(t + 1) * D], x2[:, t * D:(t + 1) * D], rstd[:, t:t + 1], gfin,
                                       ALU.mult, ALU.mult).then_inc(out_ready, 1)


def kernel(**inputs):
    import concourse.bacc as _bacc
    from concourse import mybir as _mybir
    from concourse.bass_utils import run_bass_kernel_spmd as _run

    a = {k: np.asarray(v) for k, v in inputs.items()}
    f32 = np.float32

    def by_rows(w):
        k, n = w.shape
        return np.ascontiguousarray(w.reshape(k // P, P, n).transpose(1, 0, 2).reshape(P, -1))

    def by_channel(v):
        return np.ascontiguousarray(v.reshape(-1, P).T)

    def rows_of(v):
        return np.broadcast_to(v.reshape(1, -1), (P, v.size))

    dist = 255 - np.arange(MW_BIAS)
    n = np.maximum(dist, 0)
    exact = BUCKETS // 2
    scaled = np.log(np.maximum(n, 1).astype(f32) / f32(exact)) / f32(math.log(MAXD / exact))
    large = np.minimum(exact + (scaled * f32(BUCKETS - exact)).astype(np.int32), BUCKETS - 1)
    bucket = np.where(n < exact, n, large)
    onehot = np.zeros((P, MW_BIAS), f32)
    onehot[bucket, np.arange(MW_BIAS)] = 1.0
    onehot[0:BUCKETS, dist < 0] = 0.0
    onehot[BUCKETS] = dist < 0
    onehot[BUCKETS + 1] = dist >= 128
    tab = np.zeros((P, NB), f32)
    tab[0:BUCKETS] = a["rel_bias"]
    tab[BUCKETS] = NEG
    tab[BUCKETS + 1, 0:NH] = NEG

    def lru_blocks(w):
        return w.reshape(2, 2, DH, DH).transpose(1, 2, 0, 3).reshape(P, 2 * DH)

    def positions(p):
        return p.reshape(2, 16, DH).transpose(0, 2, 1).reshape(P, 16)

    def w1_of(w):
        return w.reshape(2, 16, DH, DH).transpose(0, 2, 1, 3).reshape(P, 16 * DH)

    parts = {
        "ident": np.eye(P, dtype=f32), "mix_g": by_channel(a["mix_norm_g"][0]),
        "ffn_g": by_channel(a["ffn_norm_g"][0]), "tab": tab, "onehot": onehot,
        "conv_w": by_channel(a["conv_w"][0]), "conv_b": by_channel(a["conv_b"][0]),
        "b_a": by_channel(a["lru_b_a"][0]), "b_x": by_channel(a["lru_b_x"][0]),
        "lam": by_channel(a["lru_lambda"][0]),
        "subln_g": np.concatenate([a["diff_subln_g"][0]] * 2).reshape(P, 1),
        "b_gate": by_channel(a["b_gate"][0]), "sinks": rows_of(a["swa_sinks"][0]),
        "lq1": rows_of(a["diff_lq1"][0]), "lk1": rows_of(a["diff_lk1"][0]),
        "lq2": rows_of(a["diff_lq2"][0]), "lk2": rows_of(a["diff_lk2"][0]),
        "w_a": lru_blocks(a["lru_w_a"][0]), "w_x": lru_blocks(a["lru_w_x"][0]),
        "w2": np.concatenate([a["nsa_w2_k"][0], a["nsa_w2_v"][0]]),
        "pos_k": positions(a["nsa_pos_k"][0]), "pos_v": positions(a["nsa_pos_v"][0]),
        "upper": np.triu(np.ones((P, P), f32), 1), "ones": np.ones((P, P), f32),
        "iota": rows_of(np.arange(CAP, dtype=f32)), "iota8": rows_of(np.arange(8, dtype=f32)),
        "b_router": rows_of(np.concatenate([a["b_router_grp"][0], a["b_router_exp"][0]])),
        "w_router": by_rows(np.concatenate([a["w_router_grp"][0], a["w_router_exp"][0]], axis=1)),
    }

    def packed(names):
        return np.ascontiguousarray(np.concatenate([parts[n] for n, _ in COLUMNS if n in names], axis=1))

    w_in = a["w_in"][0]
    gate = a["w_gate"][0]
    eg, eu, ed = a["w_exp_gate"][0], a["w_exp_up"][0], a["w_exp_down"][0]
    w_moe = np.empty((PAIRS, 3, P, W_SLOT), f32)
    for e in range(2):
        gu = w_moe[:, e].reshape(PAIRS, P, KT, 2, FF)
        for j, w in enumerate((eg, eu)):
            gu[:, :, :, j, :] = w[e::2].reshape(PAIRS, KT, P, FF).transpose(0, 2, 1, 3)
        w_moe[:, 2].reshape(PAIRS, P, 2, 2, D)[:, :, e] = ed[e::2].reshape(PAIRS, 2, P, D).transpose(0, 2, 1, 3)
    arrays = {
        "pa": packed(FIRST_PART), "pb": packed(SECOND_PART),
        "w_in_full": np.stack([by_rows(w_in[:, c:c + 512]) for c in (0, 512, 1024, 1536)]),
        "w_in_tail": by_rows(np.concatenate([w_in[:, c:c + n] for c, n in (
            (2048, 128), (2176, 64), (2304, 64), (2240, 64), (2368, 64), (2432, 12))], axis=1)),
        "w1": np.concatenate([w1_of(a["nsa_w1_k"][0]), w1_of(a["nsa_w1_v"][0])], axis=1),
        "w_gates": np.stack([by_rows(gate[br][:, c:c + S]) for br in range(4) for c in range(0, D, S)]),
        "w_branch": np.stack([np.concatenate([by_rows(a["w_branch"][0][br + j]) for j in range(2)], axis=1)
                              for br in (0, 2)]),
        "w_out": np.stack([by_rows(a["w_out"][0][:, c:c + 512]) for c in (0, 512)]),
        "w_moe": w_moe.reshape(PAIRS * 3, P, W_SLOT),
        "x": a["x"][0], "g_fin": a["final_norm_g"],
    }
    nc = _bacc.Bacc("TRN2", target_bir_lowering=False, num_devices=1)
    dt = _mybir.dt.float32
    args = {n: nc.dram_tensor(f"in_{n}_dram", v.shape, dt, kind="ExternalInput").ap() for n, v in arrays.items()}
    out = nc.dram_tensor("out_0_dram", (S, D), dt, kind="ExternalOutput").ap()
    decoder_layer(nc, out=out, **args)
    r = _run(nc, [{f"in_{n}_dram": np.ascontiguousarray(v) for n, v in arrays.items()}], core_ids=[0])
    return r.results[0]["out_0_dram"].reshape(1, S, D)
```

```python
import math

import numpy as np

import concourse.bass as bass
from concourse import mybir
from contextlib import ExitStack

P = 128
S, D = 256, 1024
TT = S // P
KT = D // P
MW, DH = 256, 64
NH = 4
NB = 12
BUCKETS, MAXD = 32, 128
NCMP = (S - 32) // 16 + 1
E, GRP, EPG, FF = 32, 4, 8, 256
CAP = 64
PAIRS = E // 2
PASSES = S // CAP
NEG = -1e30
TINY = 1e-30
SLOT_COLS = 2 * S + CAP
W_SLOT = 4096
SLOTS = 6
BIAS_ROWS = 32
MW_BIAS = 512
IN_TAIL = 396
GELU_C, GELU_K = 0.044715, math.sqrt(2.0 / math.pi)
FAMILIES = ("swa", "diff0", "diff1", "sel", "win")

COLUMNS = [("ident", 128), ("mix_g", KT), ("ffn_g", KT), ("tab", NB), ("onehot", MW_BIAS),
           ("conv_w", 8), ("conv_b", 2), ("b_a", 2), ("b_x", 2), ("lam", 2),
           ("subln_g", 1), ("b_gate", 32), ("sinks", NH), ("lq1", 32), ("lq2", 32), ("lk1", 32), ("lk2", 32),
           ("w_a", 128), ("w_x", 128), ("w2", DH), ("pos_k", 16), ("pos_v", 16),
           ("upper", 128), ("ones", 128), ("iota", CAP), ("iota8", 8), ("b_router", 36), ("w_router", KT * 36)]


def column_offsets(names):
    at, out = 0, {}
    for name, n in COLUMNS:
        if name in names:
            out[name] = (at, n)
            at += n
    return out, at


FIRST_PART = {"ident", "mix_g", "tab", "onehot"}
SECOND_PART = {name for name, _ in COLUMNS} - FIRST_PART

GATE_ORDER = [(br, n2) for br in (0, 1) for n2 in range(4)] + [(br, n2) for n2 in range(4) for br in (2, 3)]
CHUNK_TABLE = [("in_a", 0, "ag"), ("in_b", 1, "dq"), ("in_tail", 2, "vsg"), ("in_cqk", 3, "ck"), ("w1", 4, "h1"),
               ("in_cvdq", 5, "dq"), ("g0_0", 2, "g0_0"), ("g0_1", 3, "g0_1"), ("g0_2", 4, "g0_2"),
               ("g0_3", 1, "g0_3"), ("g1_0", 5, "g1_0"), ("branch01", 2, "b3_1"), ("branch23", 3, "b3_3")]
CHUNK_TABLE += [(f"g{br}_{n2}", (4, 1, 5)[i % 3], f"g{br}_{n2}") for i, (br, n2) in enumerate(GATE_ORDER[5:])]
CHUNK_TABLE += [("out0", 5, "x1_10"), ("out1", 4, "x1_10"), ("out2", 1, "x1_11"), ("out3", 0, "x1_11")]
SPLIT = [f"g{br}_{n2}" for br, n2 in GATE_ORDER] + [f"out{q}" for q in range(4)]
CHUNKS = [name for name, _, _ in CHUNK_TABLE]
CHUNK_SLOT = [s for _, s, _ in CHUNK_TABLE]
CHUNK_LAST = {name: item for name, _, item in CHUNK_TABLE}
GATE_UP_SLOTS = ((2, 3), (4, 1))
EARLY, BESIDE = 6, 2
DOWN_SLOT = (5, 0)
HALF = W_SLOT // 2


def chunk_use(i):
    return CHUNK_SLOT[:i].count(CHUNK_SLOT[i])


def psum_items():
    ring, names = 6, []

    def fam(f):
        return [f"s_{f}_{part}" for part in ("a0", "a1", "b0", "b1")]

    def tps(f):
        return [f"tp_{f}_{h}" for h in range(NH)]
    order = (["vec", "xT0", "xT1", "xT2", "xT3", "ax", "ag", "bq", "bkvb", "kcks", "vsg"] + ["cq", "ck", "h1"]
             + ["lr", "lx"] + fam("swa") + fam("diff0") + ["vc", "dq"] + fam("diff1")
             + ["kc2", "vc2", "g0_0", "g0_1"] + tps("swa") + ["sc_a", "sc_b"] + fam("sel") + ["g0_2", "g0_3"]
             + tps("diff") + ["oc"] + fam("win") + ["g1_0", "g1_1", "ycT"] + tps("sel")
             + ["tpc0", "tpc1", "g1_2", "g1_3"] + tps("win"))
    for n2 in range(4):
        order += [f"b{n2}_0", f"b{n2}_1", f"g2_{n2}", f"b{n2}_2", f"g3_{n2}", f"b{n2}_3"]
    order += ["x1_00", "x1_10", "x1_01", "x1_11", "hT0", "hT1", "hT2", "hT3", "rlT", "rl", "rank"]
    order += [f"xg{k}" for k in range(KT)]
    for i, name in enumerate(order):
        names.append((name, i % ring))
    names += [("yb0", 6), ("yb1", 7), ("yd0", 6), ("yd1", 7)]
    by_head = ("yb0", "yb1", "oc")
    uses, fulls, out = [0] * 8, [0] * 8, {}
    for name, bank in names:
        fulls[bank] += name not in by_head
        out[name] = (bank, uses[bank], fulls[bank])
        uses[bank] += 1
    return out, uses


def decoder_layer(nc, pa, pb, w_in_full, w_in_tail, w1, w_gates, w_branch, w_out, w_moe, x, g_fin, out):
    f32 = mybir.dt.float32
    f32r = mybir.dt.float32r
    bf16 = mybir.dt.bfloat16
    i32 = mybir.dt.int32
    ALU = mybir.AluOpType
    ACT = mybir.ActivationFunctionType
    X = mybir.AxisListType.X

    ctx = ExitStack()
    with ctx:
        def sb(name, n, dt=f32, p=P):
            return ctx.enter_context(nc.sbuf_tensor(name, [p, n], dt))

        def sb_split(name, n):
            at = -(-nc.sbuf_base // 32) * 32
            return sb(name, n), nc.alloc_sbuf_tensor_at(name + "_parts", [P, n], f32r, offset=at)

        def sem(name):
            return ctx.enter_context(nc.semaphore(name))

        bias_rows = nc.dram_tensor("bias_rows", [NB, BIAS_ROWS, MW_BIAS], f32, kind="Internal")

        ring, ring_parts = sb_split("weight_slots", SLOTS * W_SLOT)
        slot = [ring[:, s * W_SLOT:(s + 1) * W_SLOT] for s in range(SLOTS)]
        parts = [(ring_parts[:, s * W_SLOT:s * W_SLOT + HALF], ring_parts[:, s * W_SLOT + HALF:(s + 1) * W_SLOT])
                 for s in range(SLOTS)]
        hT_lo, hT_hi = parts[0]
        offs_a, n_a = column_offsets(FIRST_PART)
        offs_b, n_b = column_offsets(SECOND_PART)
        par_a, par_b = sb("params_a", n_a), sb("params_b", n_b)

        def par(name):
            if name in offs_a:
                o, n = offs_a[name]
                return par_a[:, o:o + n]
            o, n = offs_b[name]
            return par_b[:, o:o + n]

        def cut(t, widths):
            at, parts = 0, []
            for n in widths:
                parts.append(t[:, at:at + n])
                at += n
            return parts

        x_sb = sb("x_sb", TT * D)
        hT = sb("hT", KT * S)
        gates, gates_parts = sb_split("gates", 2 * KT * S)
        slot_parts = [ring_parts[:, s * W_SLOT:(s + 1) * W_SLOT] for s in range(SLOTS)]
        cqk_lo, cqk_hi = slot_parts[CHUNK_SLOT[CHUNKS.index("in_cqk")]], gates_parts[:, :]
        cvdq_lo, cvdq_hi = slot_parts[CHUNK_SLOT[CHUNKS.index("in_cvdq")]], slot_parts[1]
        shared, shared_parts = sb_split("shared", 3 * 1536 + 8 * 256 + 4 * 384)
        fam_buf = [shared[:, i * 1536:(i + 1) * 1536] for i in range(3)]
        bias8 = shared[:, 4608:4608 + 2048].rearrange("p (h j) -> p h j", h=8)
        bias4 = shared[:, 6656:6656 + 1536].rearrange("p (h j) -> p h j", h=4)
        xn = shared[:, 0:TT * D]
        merged = shared[:, 0:KT * S]
        branch_tmp = shared[:, 2048:2560]
        late_gate = shared[:, 2560:3072]
        (h2, _, xg0, xg1, tb0, tb1, he, silu_g, gc0, gc1, yexp) = cut(
            shared, [TT * D, D, KT * P, KT * P, 512, 512, 256, 256, 256, 256, D])
        onehot_all, h2_hi, h2_lo = cut(shared_parts[:, TT * D:], [D, TT * D, TT * D])
        merged_hi, merged_lo = h2_hi, h2_lo
        h2T = hT
        x1 = x_sb
        lru_tr, lru_ti, lru_t, lru_s = cut(gates[:, 2048:4096], [512] * 4)
        work = sb("work", 2 * (S + 3) + 10 * 512 + 6 * 256 + 512)
        (ax, ag, xc, lru_w, ya, yb, bq, kb, cq, ck, dq, ks2, kw2, kc2, vc2, v_b, v_sw, v_c) = cut(
            work, [2 * (S + 3)] + [512] * 10 + [256] * 6 + [512])
        xg_all = work[:, 0:KT * SLOT_COLS].rearrange("p (k s) -> p k s", k=KT)
        beside_a = [gates[:, k * 512:(k + 1) * 512] for k in range(KT)]
        beside_b1, beside_b2 = work[:, KT * SLOT_COLS:KT * SLOT_COLS + HALF], hT
        beside_b = [half[:, k * 512:(k + 1) * 512] for half in (beside_b1, beside_b2) for k in range(KT // 2)]
        gfin = shared[:, TT * D:TT * D + D]
        yd, yc = bq, cq
        pt = sb("pt", 4 * 384)
        vec = pt[0:NB, 0:MW_BIAS]
        o_c = sb("o_c", 512)
        lru_scratch = o_c
        iota512 = o_c
        pc_s = sb("pc_s", 8 * 16)
        pcT = shared[0:16, 1536:2560]
        small = sb("small", 340)
        (ss, rt, rstd, lam4, sp2, sp_a, sp_b, sp_c, bga, bgx, fac, den, negm, mx, es, gsig, h1, h1a, h1b, kcT, vc_d,
         ssc, rc, cmx) = cut(
            small, [2, 2, 2, 8, 2, 2, 2, 2, 2, 2, 8, 40, 40, 40, 8, 24, 15, 15, 15, 15, 64, 8, 8, 8])
        bgh = sb("bgh", 32)
        spare = sb("spare", 2)
        gsubln = sb("gsubln", 1)
        logitsT = pt[0:36, 640:640 + S]
        route = pt[:, 0:640]
        (rlog, mgrp, cgrp, ogrp, gsum, gexp, ing, v1, v2, c8, o1, in2, o2, wts, comb, selm, slotv, cnt,
         cmax, base, place, pos_g, pos_12, grouped) = cut(
            route, [72, 2, 8, 8, 2, 10, 16, 2, 2, 16, 16, 16, 16, 8, 72, 72, 72, 36, 1, 36, 72, 16, 4, 64])
        cmax_i = sb("cmax_i", 1, i32)
        first_slot_i = sb("first_slot_i", 36, i32)
        zeros16 = sb("zeros16", P, bf16)

        psum = [ctx.enter_context(nc.psum_tensor(f"bank{b}", [P, 512], f32)) for b in range(8)]
        items, bank_uses = psum_items()

        params_a_in, params_b_in, norm_g_in = sem("params_a_in"), sem("params_b_in"), sem("norm_g_in")
        x_in = [sem(f"x_in{t}") for t in range(TT)]
        slot_full = [sem(f"slot_full{s}") for s in range(SLOTS)]
        bank_full = [sem(f"bank_full{b}") for b in range(8)]
        bank_free = [sem(f"bank_free{b}") for b in range(8)]
        vec_ready, rows_stored, bias_in = sem("vec_ready"), sem("rows_stored"), sem("bias_in")
        dve_step, act_step = sem("dve_step"), sem("act_step")
        squares_ready, ms_ready, root_ready, xn_ready, hT_a, hT_d = (
            sem(n) for n in ("squares_ready", "ms_ready", "root_ready", "xn_ready", "hT_a", "hT_d"))
        ax_ready, xc_ready, lru_par_ready, lru_tanh_ready, gelu_in, ya_ready = (
            sem(n) for n in ("ax_ready", "xc_ready", "lru_par_ready", "lru_tanh_ready", "gelu_in", "ya_ready"))
        bq_ready, kb_ready, kc_ready, ks_ready, cq_ready, ck_ready, dq_ready = (
            sem(n) for n in ("bq_ready", "kb_ready", "kc_ready", "ks_ready", "cq_ready", "ck_ready", "dq_ready"))
        dgate_raw, dgate_tanh = sem("dgate_raw"), sem("dgate_tanh")
        blocks_ready, h1_raw, h1_tanh, h1_ready, kc2_ready = (
            sem(n) for n in ("blocks_ready", "h1_raw", "h1_tanh", "h1_ready", "kc2_ready"))
        sp_in, sp_exp, lam_in, lam_exp = sem("sp_in"), sem("sp_exp"), sem("lam_in"), sem("lam_exp")
        neg_ready, exp_ready, p_ready = (sem(n) for n in ("neg_ready", "exp_ready", "p_ready"))
        cmp_in, cmp_exp, pc_ready, pcT_ready = (sem(n) for n in ("cmp_in", "cmp_exp", "pc_ready", "pcT_ready"))
        pt_ready, pt_used, v_ready = sem("pt_ready"), sem("pt_used"), sem("v_ready")
        oc_squares, oc_root, oc_ready = sem("oc_squares"), sem("oc_root"), sem("oc_ready")
        yb_ready, yc_ready, yd_ready = sem("yb_ready"), sem("yc_ready"), sem("yd_ready")
        gate_ready, late_used, merged_ready = sem("gate_ready"), sem("late_used"), sem("merged_ready")
        x1_ready, h2_a, h2_d, h2T_a, h2T_d, rlT_ready, rstd_ready, h2_hi_ready, h2_lo_ready = (
            sem(n) for n in ("x1_ready", "h2_a", "h2_d", "h2T_a", "h2T_d", "rlT_ready", "rstd_ready",
                             "h2_hi_ready", "h2_lo_ready"))
        grp_in, grp_exp, sel_ready, count_ready = (sem(n) for n in ("grp_in", "grp_exp", "sel_ready", "count_ready"))
        xg_a, xg_d, gu_done, silu_done, he_ready = (
            sem(n) for n in ("xg_a", "xg_d", "gu_done", "silu_done", "he_ready"))
        tr_done, tb_ready, down_done, yexp_a, yexp_d = (
            sem(n) for n in ("tr_done", "tb_ready", "down_done", "yexp_a", "yexp_d"))
        x2_ready, fin_in, fin_squares, fin_ms, fin_root, out_ready, out_stored = (
            sem(n) for n in ("x2_ready", "fin_in", "fin_squares", "fin_ms", "fin_root", "out_ready", "out_stored"))
        cqk_hi_ready, cqk_lo_ready, cvdq_hi_ready, cvdq_lo_ready = (
            sem(n) for n in ("cqk_hi_ready", "cqk_lo_ready", "cvdq_hi_ready", "cvdq_lo_ready"))
        hT_hi_ready, hT_lo_ready, part_hi_ready, part_lo_ready = (
            sem(n) for n in ("hT_hi_ready", "hT_lo_ready", "part_hi_ready", "part_lo_ready"))
        beside_a_in, beside_b_in = sem("beside_a_in"), sem("beside_b_in")
        ax_pads, spare_set, slots_moved = sem("ax_pads"), sem("spare_set"), sem("slots_moved")
        weighted_ready, slots_ready = sem("weighted_ready"), sem("slots_ready")
        xg_all_a, xg_all_d = sem("xg_all_a"), sem("xg_all_d")
        pass_begun = sem("pass_begun")
        xg_pad, base_moved = sem("xg_pad"), sem("base_moved")

        FAM_NO = {f: i for i, f in enumerate(FAMILIES)}
        FAM_BUF = {"swa": 0, "diff0": 1, "diff1": 2, "sel": 0, "win": 2}
        TP_FAMS = ("swa", "diff", "sel", "win")
        TP_BUF = {"swa": 0, "diff": 1, "sel": 0, "win": 2}

        def fam_q1(f):
            return fam_buf[FAM_BUF[f]][:, 0:1024].rearrange("p (h k) -> p h k", h=NH)

        def fam_q0(f):
            return fam_buf[FAM_BUF[f]][:, 1024:1536].rearrange("p (h k) -> p h k", h=NH)

        def expert_base(s):
            return CHUNK_SLOT.count(s)

        def wait_past(eng, s, value):
            if not (isinstance(value, int) and value == 0):
                eng.wait_ge(s, value)

        def before_last(n):
            return max(n - 1, 0) if isinstance(n, int) else n - 1

        block = ctx.enter_context(nc.Block())

        @block.sync
        def _(sp):
            sp.dma_start(x_sb[:, 0:D], x[0:P, :]).then_inc(x_in[0], 16)
            sp.dma_start(par_a[:, :], pa).then_inc(params_a_in, 16)
            sources = {"in_a": w_in_full[0], "in_b": w_in_full[1], "in_cqk": w_in_full[2], "in_cvdq": w_in_full[3],
                       "in_tail": w_in_tail, "w1": w1, "branch01": w_branch[0], "branch23": w_branch[1],
                       **{f"out{q}": w_out[q] for q in range(4)}}
            for br in range(4):
                for n2 in range(4):
                    sources[f"g{br}_{n2}"] = w_gates[4 * br + n2]
            last_in = {}
            parts_of_h = "g%d_%d" % GATE_ORDER[-1]

            def after_last_chunk(s):
                if s in last_in:
                    bank, _, full = items[CHUNK_LAST[last_in[s]]]
                    sp.wait_ge(bank_full[bank], full)

            for i, name in enumerate(CHUNKS):
                s = CHUNK_SLOT[i]
                after_last_chunk(s)
                src = sources[name]
                sp.dma_start(slot[s][:, 0:src.shape[1]], src).then_inc(slot_full[s], 16)
                last_in[s] = parts_of_h if name == "in_a" else name
            def load_pair(n, j, s):
                src = w_moe[3 * n + j] if isinstance(n, int) else w_moe[bass.ds(n * 3 + j, 1), :, :].rearrange(
                    "o p n -> (o p) n")
                sp.dma_start(slot[s], src).then_inc(slot_full[s], 16)

            def load_beside_a(n):
                sp.dma_start(gates[:, :], w_moe[3 * n]).then_inc(beside_a_in, 16)

            def load_beside_b(n):
                for half, dst in enumerate((beside_b1, beside_b2)):
                    sp.dma_start(dst[:, :], w_moe[3 * n + 1][:, half * HALF:(half + 1) * HALF]
                                 ).then_inc(beside_b_in, 16)

            for j, s in enumerate(GATE_UP_SLOTS[0]):
                after_last_chunk(s)
                load_pair(0, j, s)
            sp.wait_ge(merged_ready, 4)
            load_beside_a(2)
            for n, j, s in ((0, 2, DOWN_SLOT[0]), (1, 0, GATE_UP_SLOTS[1][0]), (1, 1, GATE_UP_SLOTS[1][1]),
                            (1, 2, DOWN_SLOT[1])):
                after_last_chunk(s)
                load_pair(n, j, s)
            sp.wait_ge(bank_full[items["rlT"][0]], items["rlT"][2])
            load_beside_b(2)

            def load_gate_up(c, n, p, pairs_before=2):
                sp.wait_ge(gu_done, n + c * PAIRS + (1 - pairs_before))
                for j, s in enumerate(GATE_UP_SLOTS[p]):
                    load_pair(n, j, s)

            def load_down(c, n, p):
                sp.wait_ge(down_done, n + c * PAIRS - 1)
                load_pair(n, 2, DOWN_SLOT[p])

            load_gate_up(0, 3, 0, pairs_before=3)
            load_gate_up(0, 4, 1, pairs_before=3)
            load_down(0, 2, 0)
            load_down(0, 3, 1)
            sp.wait_ge(gu_done, 3)
            load_beside_a(5)
            load_beside_b(5)
            load_down(0, 4, 0)
            load_gate_up(0, 6, 0, pairs_before=3)
            load_down(0, 5, 1)
            load_gate_up(0, 7, 1, pairs_before=3)
            load_down(0, 6, 0)
            load_gate_up(0, 8, 0)
            load_down(0, 7, 1)

            def load_rest(c, first):
                with sp.Fori(first, PAIRS // 2 - 1) as it:
                    load_gate_up(c, it * 2 + 1, 1)
                    load_down(c, it * 2, 0)
                    load_gate_up(c, it * 2 + 2, 0)
                    load_down(c, it * 2 + 1, 1)
                load_gate_up(c, PAIRS - 1, 1)
                load_down(c, PAIRS - 2, 0)
                load_down(c, PAIRS - 1, 1)

            load_rest(0, 4)
            sp.wait_ge(count_ready, 1)
            most = sp.value_load(cmax_i[0:1, 0:1], min_val=0, max_val=S)
            with sp.If(most > CAP):
                with sp.Fori(1, PASSES) as c:
                    load_gate_up(c, 0, 0)
                    load_rest(c, 0)
            for t in range(TT):
                for nh in range(2):
                    sp.wait_ge(out_ready, 2 * t + nh + 1)
                    sp.dma_start(out[t * P:(t + 1) * P, nh * 512:(nh + 1) * 512],
                                 x1[:, t * D + nh * 512:t * D + (nh + 1) * 512]).then_inc(out_stored, 16)
            sp.wait_ge(out_stored, 16 * 2 * TT)

        @block.gpsimd
        def _(pool):
            pool.wait_ge(vec_ready, 1)
            pool.dma_start(bias_rows.ap(), vec.unsqueeze(1).broadcast_to([NB, BIAS_ROWS, MW_BIAS])
                           ).then_inc(rows_stored, 16)
            pool.wait_ge(rows_stored, 16)
            for heads, first, dst in ((8, 0, bias8), (4, 8, bias4)):
                for q in range(0, P, BIAS_ROWS):
                    src = bass.AP(tensor=bias_rows, offset=first * BIAS_ROWS * MW_BIAS + P - 1 - q,
                                  ap=[[MW_BIAS - 1, BIAS_ROWS], [BIAS_ROWS * MW_BIAS, heads], [1, dst.shape[2]]])
                    pool.dma_start(dst[q:q + BIAS_ROWS], src).then_inc(bias_in, 16)
            pool.wait_ge(hT_hi_ready, 1)
            nc.gpsimd.tensor_tensor(hT_lo, hT[:, :], hT_hi.bitcast(f32), ALU.subtract).then_inc(hT_lo_ready, 1)
            pool.wait_ge(cvdq_hi_ready, 1)
            nc.gpsimd.tensor_tensor(cvdq_lo, slot[CHUNK_SLOT[CHUNKS.index("in_cvdq")]], cvdq_hi.bitcast(f32),
                                    ALU.subtract).then_inc(cvdq_lo_ready, 1)
            for i, name in enumerate(SPLIT):
                s = CHUNK_SLOT[CHUNKS.index(name)]
                lo, hi = parts[s]
                pool.wait_ge(part_hi_ready, i + 1)
                nc.gpsimd.tensor_tensor(lo, slot[s][:, 0:HALF], hi.bitcast(f32), ALU.subtract
                                        ).then_inc(part_lo_ready, 1)
            pool.wait_ge(merged_ready, 4)
            nc.gpsimd.memset(xg_all[:, :, 2 * S:SLOT_COLS], 0.0).then_inc(xg_pad, 1)
            for t in range(TT):
                pool.wait_ge(h2_hi_ready, t + 1)
                c = slice(t * D, (t + 1) * D)
                nc.gpsimd.tensor_tensor(h2_lo[:, c], h2[:, c], h2_hi[:, c].bitcast(f32), ALU.subtract
                                        ).then_inc(h2_lo_ready, 1)
            pool.wait_ge(xg_all_a, 1)
            pool.wait_ge(xg_all_d, 1)
            pool.dma_start(gfin, g_fin.partition_broadcast(P)).then_inc(norm_g_in, 16)

        @block.tensor
        def _(pe):
            mm = nc.tensor.matmul
            ident = par("ident")

            def begin(name):
                bank, use, _ = items[name]
                if use:
                    pe.wait_ge(bank_free[bank], use)
                return psum[bank]

            def end(name, last):
                last.then_inc(bank_full[items[name][0]], 1)

            def chunk(name):
                i = CHUNKS.index(name)
                pe.wait_ge(slot_full[CHUNK_SLOT[i]], 16 * (chunk_use(i) + 1))
                return slot[CHUNK_SLOT[i]]

            def hT_t(k, t):
                return hT[:, k * S + t * P:k * S + (t + 1) * P]

            def channels(dst, w, width, col, n=P):
                for k in range(KT):
                    last = mm(dst, w[:, k * width + col:k * width + col + n], hT[:, k * S:(k + 1) * S],
                              start=(k == 0), stop=(k == KT - 1))
                return last

            pe.wait_ge(params_a_in, 16)
            b = begin("vec")
            end("vec", mm(b[0:NB, :], par("tab")[0:BUCKETS + 2, :], par("onehot")[0:BUCKETS + 2, :],
                          start=True, stop=True))
            for j in range(4):
                b = begin(f"xT{j}")
                for k in (2 * j, 2 * j + 1):
                    for t in range(TT):
                        if j == 0 and k == 0:
                            pe.wait_ge(xn_ready, t + 1)
                        last = nc.tensor.transpose(b[:, (k % 2) * S + t * P:(k % 2) * S + (t + 1) * P],
                                                   xn[:, t * D + k * P:t * D + (k + 1) * P], ident)
                end(f"xT{j}", last)
            pe.wait_ge(hT_a, 2)
            pe.wait_ge(hT_d, 2)

            def split_product(dst, left, right):
                for k in range(KT):
                    (l_hi, l_lo), (r_hi, r_lo) = left(k), right(k)
                    mm(dst, l_hi, r_hi, start=(k == 0), stop=False)
                    mm(dst, l_hi, r_lo, start=False, stop=False)
                    last = mm(dst, l_lo, r_hi, start=False, stop=(k == KT - 1))
                return last

            def h_parts(t=None):
                at, n = (0, S) if t is None else (t * P, P)
                return lambda k: (hT_hi[:, k * S + at:k * S + at + n], hT_lo[:, k * S + at:k * S + at + n])

            def w_parts(hi, lo, width, col, n):
                return lambda k: (hi[:, k * width + col:k * width + col + n], lo[:, k * width + col:k * width + col + n])

            def two_blocks_split(name, hi, lo, width, cols):
                b = begin(name)
                for j, col in enumerate(cols):
                    last = split_product(b[:, j * S:(j + 1) * S], w_parts(hi, lo, width, col, P), h_parts())
                end(name, last)

            def two_blocks(name, w, width, cols):
                b = begin(name)
                for j, col in enumerate(cols):
                    last = channels(b[:, j * S:(j + 1) * S], w, width, col)
                end(name, last)
                return last

            def tokens(dst, w, width, t, col, n):
                for k in range(KT):
                    last = mm(dst, hT_t(k, t), w[:, k * width + col:k * width + col + n],
                              start=(k == 0), stop=(k == KT - 1))
                return last

            w = chunk("in_a")
            two_blocks("ax", w, 512, (0, P))
            last = two_blocks("ag", w, 512, (2 * P, 3 * P))
            w = chunk("in_b")
            two_blocks("bq", w, 512, (0, P))
            b = begin("bkvb")
            channels(b[:, 0:S], w, 512, 2 * P)
            for t in range(TT):
                last = tokens(b[:, S + t * P:S + (t + 1) * P], w, 512, t, 3 * P, P)
            end("bkvb", last)
            w = chunk("in_tail")
            two_blocks("kcks", w, IN_TAIL, (0, P))
            b = begin("vsg")
            for t in range(TT):
                tokens(b[:, t * P:(t + 1) * P], w, IN_TAIL, t, 2 * P, P)
            for t in range(TT):
                last = tokens(b[:, S + t * NB:S + (t + 1) * NB], w, IN_TAIL, t, 384, NB)
            end("vsg", last)

            def scores(f, q, k_of, d, rows_of):
                for part, heads in (("a", (0, 2)), ("b", (1, 3))):
                    b0, b1 = begin(f"s_{f}_{part}0"), begin(f"s_{f}_{part}1")
                    for j, h in enumerate(heads):
                        r, c = rows_of(h)
                        last0 = mm(b0[:, j * P:(j + 1) * P], q[r:r + d, c:c + P], k_of(h)[:, 0:P],
                                   start=True, stop=True)
                        last1 = mm(b1[:, j * S:(j + 1) * S], q[r:r + d, c + P:c + S], k_of(h), start=True, stop=True)
                    end(f"s_{f}_{part}0", last0)
                    end(f"s_{f}_{part}1", last1)

            def rows64(h):
                return DH * (h % 2), S * (h // 2)

            pe.wait_ge(hT_lo_ready, 1)
            pe.wait_ge(cqk_lo_ready, 1)
            two_blocks_split("cq", cqk_hi, cqk_lo, 512, (0, P))
            two_blocks_split("ck", cqk_hi, cqk_lo, 512, (2 * P, 3 * P))

            w = chunk("w1")
            pe.wait_ge(blocks_ready, 1)
            b = begin("h1")
            for kv, src in enumerate((kc2, vc2)):
                src3 = src[:, :].rearrange("p (c i) -> p i c", i=16)
                for i in range(16):
                    last = mm(b[kv * DH:(kv + 1) * DH, 0:NCMP], w[:, kv * 1024 + i * DH:kv * 1024 + (i + 1) * DH],
                              src3[:, i, 0:NCMP], start=(i == 0), stop=(i == 15))
            end("h1", last)

            pe.wait_ge(params_b_in, 16)
            pe.wait_ge(xc_ready, 1)
            for name, wname in (("lr", "w_a"), ("lx", "w_x")):
                b = begin(name)
                for cb in range(2):
                    for half in range(2):
                        r = DH * half
                        last = mm(b[r:r + DH, cb * S:(cb + 1) * S], par(wname)[r:r + DH, cb * DH:(cb + 1) * DH],
                                  xc[r:r + DH, cb * S:(cb + 1) * S], start=True, stop=True)
                end(name, last)

            pe.wait_ge(bq_ready, 1)
            pe.wait_ge(kb_ready, 1)
            scores("swa", bq, lambda h: kb[DH * (h % 2):DH * (h % 2) + DH, S * (h // 2):S * (h // 2) + S], DH, rows64)

            def diff_scores(m):
                def k_of(h):
                    r = DH * (h % 2) + 32 * m
                    return ck[r:r + 32, S * (h // 2):S * (h // 2) + S]
                scores(f"diff{m}", cq, k_of, 32, lambda h: (DH * (h % 2) + 32 * m, S * (h // 2)))

            pe.wait_ge(cq_ready, 1)
            pe.wait_ge(ck_ready, 1)
            diff_scores(0)
            pe.wait_ge(cvdq_lo_ready, 1)
            b = begin("vc")
            for t in range(TT):
                last = split_product(b[:, t * 256:(t + 1) * 256], h_parts(t), w_parts(cvdq_hi, cvdq_lo, 512, 0, 256))
            end("vc", last)
            two_blocks_split("dq", cvdq_hi, cvdq_lo, 512, (2 * P, 3 * P))
            diff_scores(1)

            def gate_item(br, n2):
                name = f"g{br}_{n2}"
                lo, hi = parts[CHUNK_SLOT[CHUNKS.index(name)]]
                pe.wait_ge(part_lo_ready, SPLIT.index(name) + 1)
                two_blocks_split(name, hi, lo, S, (0, P))

            def transposes(f, h):
                if h == 0:
                    pe.wait_ge(p_ready, TP_FAMS.index(f) + 1)
                buf = fam_buf[TP_BUF[f]]
                b = begin(f"tp_{f}_{h}")
                nc.tensor.transpose(b[:, 0:P], buf[:, 1024 + h * P:1024 + (h + 1) * P], ident)
                nc.tensor.transpose(b[:, P:2 * P], buf[:, h * S:h * S + P], ident)
                last = nc.tensor.transpose(b[:, 2 * P:3 * P], buf[:, h * S + P:(h + 1) * S], ident)
                end(f"tp_{f}_{h}", last)

            def pt_of(f, h):
                u = TP_FAMS.index(f) * NH + h
                pe.wait_ge(pt_ready, u + 1)
                return pt[:, (u % 4) * 384:(u % 4 + 1) * 384]

            def values(dst, f, h, v_of, start=True, stop=True):
                p = pt_of(f, h)
                mm(dst[:, 0:S], v_of(0), p[:, 0:S], start=start, stop=False)
                mm(dst[:, P:S], v_of(1), p[:, S:S + P], start=False, stop=stop).then_inc(pt_used, 1)

            pe.wait_ge(h1_ready, 1)
            b = begin("kc2")
            mm(b[0:DH, 0:NCMP], par("w2")[0:DH, :], h1b[0:DH, :], start=True, stop=True)
            last = mm(b[DH:P, 0:NCMP], par("w2")[0:DH, :], h1b[0:DH, :], start=True, stop=True)
            end("kc2", last)
            b = begin("vc2")
            end("vc2", mm(b[0:NCMP, 0:DH], h1b[DH:P, :], par("w2")[DH:P, :], start=True, stop=True))
            gate_item(0, 0)
            gate_item(0, 1)
            pe.wait_ge(v_ready, 3)
            yb_bank = [begin("yb0"), begin("yb1")]

            def swa_values(h):
                r = DH * (h % 2)
                values(yb_bank[h // 2][r:r + DH, :], "swa", h,
                       lambda t: v_b[:, t * P + DH * (h // 2):t * P + DH * (h // 2) + DH])

            transposes("swa", 0)
            for h in range(1, NH):
                transposes("swa", h)
                swa_values(h - 1)
            swa_values(NH - 1)

            pe.wait_ge(kc2_ready, 1)
            pe.wait_ge(dq_ready, 1)
            for part, heads in (("a", (0, 2)), ("b", (1, 3))):
                b = begin(f"sc_{part}")
                for t in range(TT):
                    for j, h in enumerate(heads):
                        r, c = rows64(h)
                        last = mm(b[:, (t * 2 + j) * 16:(t * 2 + j) * 16 + NCMP],
                                  dq[r:r + DH, c + t * P:c + (t + 1) * P], kcT[r:r + DH, :], start=True, stop=True)
                end(f"sc_{part}", last)
            pe.wait_ge(ks_ready, 1)
            scores("sel", dq, lambda h: ks2[DH * (h % 2):DH * (h % 2) + DH, :], DH, rows64)
            gate_item(0, 2)
            gate_item(0, 3)

            transposes("diff", 0)
            oc_bank = None

            def diff_values(h):
                p = pt_of("diff", h)
                mm(oc_bank[:, h * DH:(h + 1) * DH], p[:, 0:P], v_c[:, h * DH:(h + 1) * DH], start=True, stop=True)
                mm(oc_bank[:, 256 + h * DH:256 + (h + 1) * DH], p[:, P:2 * P], v_c[:, h * DH:(h + 1) * DH],
                   start=True, stop=False)
                return mm(oc_bank[:, 256 + h * DH:256 + (h + 1) * DH], p[:, 2 * P:3 * P],
                          v_c[:, 256 + h * DH:256 + (h + 1) * DH], start=False, stop=True).then_inc(pt_used, 1)

            for h in range(1, NH):
                transposes("diff", h)
            oc_bank = begin("oc")
            for h in range(NH):
                diff_values(h)
            scores("win", dq, lambda h: kw2[DH * (h % 2):DH * (h % 2) + DH, :], DH, rows64)
            gate_item(1, 0)
            gate_item(1, 1)
            pe.wait_ge(oc_ready, 1)
            b = begin("ycT")
            for j in range(2):
                for t in range(TT):
                    last = nc.tensor.transpose(b[:, j * S + t * P:j * S + (t + 1) * P],
                                               o_c[:, t * 256 + j * P:t * 256 + (j + 1) * P], ident)
            end("ycT", last)

            yd_bank = [begin("yd0"), begin("yd1")]

            def nsa_values(f, h, v_at, start):
                r = DH * (h % 2)
                values(yd_bank[h // 2][r:r + DH, :], f, h,
                       lambda t: v_sw[:, t * P + v_at:t * P + v_at + DH], start=start, stop=False)

            transposes("sel", 0)
            for h in range(1, NH):
                transposes("sel", h)
                nsa_values("sel", h - 1, 0, True)
            nsa_values("sel", NH - 1, 0, True)
            pe.wait_ge(pc_ready, 1)
            for j in range(2):
                b = begin(f"tpc{j}")
                for h in (2 * j, 2 * j + 1):
                    for t in range(TT):
                        last = nc.tensor.transpose(b[0:NCMP, (h % 2) * S + t * P:(h % 2) * S + (t + 1) * P],
                                                   pc_s[:, (t * NH + h) * 16:(t * NH + h) * 16 + NCMP], ident)
                end(f"tpc{j}", last)
            gate_item(1, 2)
            gate_item(1, 3)
            transposes("win", 0)
            for h in range(1, NH):
                transposes("win", h)
                nsa_values("win", h - 1, DH, False)
            nsa_values("win", NH - 1, DH, False)
            pe.wait_ge(pcT_ready, 2)
            for h in range(NH):
                r = DH * (h % 2)
                last = mm(yd_bank[h // 2][r:r + DH, 0:S], vc_d[0:NCMP, :], pcT[0:NCMP, h * S:(h + 1) * S],
                          start=False, stop=True)
                if h % 2:
                    last.then_inc(bank_full[6 + h // 2], 1)

            ys = (ya, yb, yc, yd)
            pe.wait_ge(ya_ready, 1)
            pe.wait_ge(yb_ready, 2)
            for n2 in range(4):
                for br in range(4):
                    if br >= 2:
                        gate_item(br, n2)
                    if n2 == 0 and br == 2:
                        pe.wait_ge(yc_ready, 1)
                    if n2 == 0 and br == 3:
                        pe.wait_ge(yd_ready, 2)
                    w = chunk("branch01" if br < 2 else "branch23")
                    b = begin(f"b{n2}_{br}")
                    for j in range(2):
                        n = 2 * n2 + j
                        for k in range(2):
                            last = mm(b[:, j * S:(j + 1) * S], w[:, (br % 2) * 2048 + k * D + n * P:
                                                                 (br % 2) * 2048 + k * D + (n + 1) * P],
                                      ys[br][:, k * S:(k + 1) * S], start=(k == 0), stop=(k == 1))
                    end(f"b{n2}_{br}", last)
            for nh in range(2):
                banks = [begin(f"x1_{t}{nh}") for t in range(TT)]
                for q in (2 * nh, 2 * nh + 1):
                    lo, hi = parts[CHUNK_SLOT[CHUNKS.index(f"out{q}")]]
                    pe.wait_ge(part_lo_ready, SPLIT.index(f"out{q}") + 1)
                    for t in range(TT):
                        dst = banks[t][:, (q % 2) * S:(q % 2 + 1) * S]
                        for k in range(KT):
                            if q == 0 and t == 0 and k % 2 == 0:
                                pe.wait_ge(merged_ready, k // 2 + 1)
                            m, c = slice(k * S + t * P, k * S + (t + 1) * P), slice(k * S, (k + 1) * S)
                            mm(dst, merged_hi[:, m], hi[:, c], start=(k == 0), stop=False)
                            mm(dst, merged_hi[:, m], lo[:, c], start=False, stop=False)
                            last = mm(dst, merged_lo[:, m], hi[:, c], start=False, stop=(k == KT - 1))
                        if q % 2:
                            end(f"x1_{t}{nh}", last)

            h2T_banks = [begin(f"hT{j}") for j in range(4)]
            for t in range(TT):
                pe.wait_ge((h2_a, h2_d)[t], 1)
                for k in range(KT):
                    b = h2T_banks[k // 2]
                    last = nc.tensor.transpose(b[:, (k % 2) * S + t * P:(k % 2) * S + (t + 1) * P],
                                               h2[:, t * D + k * P:t * D + (k + 1) * P], ident)
                    if t and k % 2:
                        end(f"hT{k // 2}", last)
            b = begin("rlT")
            for k in range(KT):
                if k % 2 == 0:
                    pe.wait_ge((h2T_a, h2T_d)[k // 2 % 2], k // 4 + 1)
                last = mm(b[0:36, 0:S], par("w_router")[:, k * 36:(k + 1) * 36], hT[:, k * S:(k + 1) * S],
                          start=(k == 0), stop=(k == KT - 1))
            end("rlT", last)
            pe.wait_ge(rlT_ready, 1)
            b = begin("rl")
            for t in range(TT):
                last = nc.tensor.transpose(b[:, t * 36:(t + 1) * 36], logitsT[:, t * P:(t + 1) * P], ident[0:36, 0:36])
            end("rl", last)
            pe.wait_ge(sel_ready, 1)
            b = begin("rank")
            sel3 = selm.rearrange("p (t e) -> p t e", t=TT)
            mm(b[:, 0:36], par("upper"), sel3[:, 0, :], start=True, stop=True)
            mm(b[:, 36:72], par("ones"), sel3[:, 0, :], start=True, stop=False)
            mm(b[:, 36:72], par("upper"), sel3[:, 1, :], start=False, stop=True)
            mm(b[:, 72:108], par("ones"), sel3[:, 0, :], start=True, stop=False)
            last = mm(b[:, 72:108], par("ones"), sel3[:, 1, :], start=False, stop=True)
            end("rank", last)

            pe.wait_ge(h2_hi_ready, 2)
            pe.wait_ge(h2_lo_ready, 2)
            for ks in (range(0, 4), range(4, KT)):
                banks = [begin(f"xg{k}") for k in ks]
                for t in range(TT):
                    pe.wait_ge(slots_ready, t + 1)
                    for k, b in zip(ks, banks):
                        for part in (h2_hi, h2_lo):
                            last = mm(b[:, :], part[:, t * D + k * P:t * D + (k + 1) * P],
                                      onehot_all[:, t * 512:(t + 1) * 512], start=(t == 0 and part is h2_hi),
                                      stop=(t == 1 and part is h2_lo))
                        if t:
                            end(f"xg{k}", last)

            y_bank, gu_bank, tr_bank, cd = psum[0:4], psum[4], psum[5], psum[6:8]
            for bk in range(8):
                if bank_uses[bk]:
                    pe.wait_ge(bank_free[bk], bank_uses[bk])
            zeros512 = zeros16[:, :].unsqueeze(1).broadcast_to([P, 4, P])
            for bk in y_bank:
                mm(bk[:, :], zeros16[:, :], zeros512, start=True, stop=False, skip_group_check=True)

            def scatter(tb):
                for t in range(TT):
                    for nh in range(2):
                        last = mm(y_bank[2 * t + nh][:, :], tb[:, 256 + t * P:256 + (t + 1) * P],
                                  yexp[:, nh * 512:(nh + 1) * 512], start=False, stop=False, skip_group_check=True)

            tbs, xgs = (tb0, tb1), (xg0, xg1)

            def ring_weights(slots):
                return [[slot[s][:, k * 512:(k + 1) * 512] for k in range(KT)] for s in slots]

            def gate_up(c, i, p, nth_load, weights=None):
                n = i + c * PAIRS
                pe.wait_ge(xg_a, n + 1)
                pe.wait_ge(xg_d, n + 1)
                wait_past(pe, he_ready, n)
                if weights is None:
                    weights = ring_weights(GATE_UP_SLOTS[p])
                    for s in GATE_UP_SLOTS[p]:
                        pe.wait_ge(slot_full[s], (nth_load + (c * (PAIRS // 2) + expert_base(s))) * 16)
                for k in range(KT):
                    for e in range(2):
                        last = mm(gu_bank[e * CAP:(e + 1) * CAP, :], xgs[p][:, k * P + e * CAP:k * P + (e + 1) * CAP],
                                  weights[e][k], start=(k == 0), stop=(k == KT - 1))
                last.then_inc(gu_done, 1)

            def down(c, i, p, nth_load):
                n = i + c * PAIRS
                pe.wait_ge(tb_ready, n + 1)
                wait_past(pe, yexp_a, n)
                wait_past(pe, yexp_d, n)
                s = DOWN_SLOT[p]
                pe.wait_ge(slot_full[s], (nth_load + (c * (PAIRS // 2) + expert_base(s) + 1)) * 16)
                for nh in range(2):
                    for j in range(2):
                        for e in range(2):
                            last = mm(cd[nh][e * CAP:(e + 1) * CAP, :],
                                      tbs[p][:, j * P + e * CAP:j * P + (e + 1) * CAP],
                                      slot[s][:, e * 2048 + j * D + nh * 512:e * 2048 + j * D + (nh + 1) * 512],
                                      start=(j == 0), stop=(j == 1))
                last.then_inc(down_done, 1)

            def transposed(c, i, p):
                n = i + c * PAIRS
                pe.wait_ge(he_ready, n + 1)
                pe.wait_ge(weighted_ready, n + 1)
                wait_past(pe, tb_ready, n)
                for j in range(2):
                    nc.tensor.transpose(tr_bank[:, j * P:(j + 1) * P], he[:, j * P:(j + 1) * P], ident)
                for t in range(TT):
                    last = nc.tensor.transpose(tr_bank[:, 256 + t * P:256 + (t + 1) * P],
                                               (gc0, gc1)[p][:, t * P:(t + 1) * P], ident)
                last.then_inc(tr_done, 1)

            def outputs_onto_tokens(c, i, p):
                n = i + c * PAIRS
                pe.wait_ge(yexp_a, n + 1)
                pe.wait_ge(yexp_d, n + 1)
                scatter(tbs[p])

            def pair_step(c, i, p, nth_load, nth_load_before, weights=None):
                gate_up(c, i, p, nth_load, weights)
                down(c, i - 1, 1 - p, nth_load_before)
                transposed(c, i, p)
                outputs_onto_tokens(c, i - 1, 1 - p)

            def pairs_from(c, first):
                with pe.Fori(first, PAIRS // 2 - 1) as it:
                    pair_step(c, it * 2 + 1, 1, it, it)
                    pair_step(c, it * 2 + 2, 0, it + 1, it)
                pair_step(c, PAIRS - 1, 1, PAIRS // 2 - 1, PAIRS // 2 - 1)
                down(c, PAIRS - 1, 1, PAIRS // 2 - 1)
                outputs_onto_tokens(c, PAIRS - 1, 1)

            def early_weights(i):
                turn, place = divmod(i, 3)
                if place == BESIDE:
                    pe.wait_ge(beside_a_in, 16 * (turn + 1))
                    pe.wait_ge(beside_b_in, 32 * (turn + 1))
                    return beside_a, beside_b
                for s in GATE_UP_SLOTS[place]:
                    pe.wait_ge(slot_full[s], 16 * (expert_base(s) + turn + 1))
                return ring_weights(GATE_UP_SLOTS[place])

            gate_up(0, 0, 0, 0, early_weights(0))
            transposed(0, 0, 0)
            for i in range(1, EARLY):
                pair_step(0, i, i % 2, i // 2, (i - 1) // 2, early_weights(i))
            pair_step(0, EARLY, 0, EARLY // 2, (EARLY - 1) // 2)
            pairs_from(0, EARLY // 2)
            pe.wait_ge(count_ready, 1)
            most = pe.value_load(cmax_i[0:1, 0:1], min_val=0, max_val=S)
            with pe.If(most > CAP):
                with pe.Fori(1, PASSES) as c:
                    gate_up(c, 0, 0, 0)
                    transposed(c, 0, 0)
                    pairs_from(c, 0)
            for t in range(TT):
                for nh in range(2):
                    last = mm(y_bank[2 * t + nh][:, :], zeros16[:, :], zeros512, start=False, stop=True,
                              skip_group_check=True)
                last.then_inc(x2_ready, 1)

        @block.scalar
        def _(act):
            step = [0]

            def link(ins):
                step[0] += 1
                ins.then_inc(act_step, 1)
                act.wait_ge(act_step, step[0])

            f = nc.scalar.activation

            def full(name):
                bank, _, value = items[name]
                act.wait_ge(bank_full[bank], value)
                return psum[bank]

            def free(name):
                return bank_free[items[name][0]]

            def root_table():
                f(spare[:, 1:2], spare[:, 0:1], ACT.Sqrt)

            act.dma_start(x_sb[:, D:2 * D], x[P:2 * P, :]).then_inc(x_in[1], 16)
            act.dma_start(par_b[:, :], pb).then_inc(params_b_in, 16)
            act.wait_ge(spare_set, 1)
            root_table()
            for t in range(TT):
                act.wait_ge(x_in[t], 16)
                f(xn[:, t * D:(t + 1) * D], x_sb[:, t * D:(t + 1) * D], ACT.Square,
                  accum_out=ss[:, t:t + 1]).then_inc(squares_ready, 1)
            act.wait_ge(ms_ready, 1)
            f(rt[:, :], ss[:, :], ACT.Sqrt).then_inc(root_ready, 1)
            act.wait_ge(sp_in, 1)
            f(sp_b[:, :], sp_a[:, :], ACT.Exp).then_inc(sp_exp, 1)
            act.wait_ge(lam_in, 1)
            f(lam4[:, 2:4], lam4[:, 0:2], ACT.Exp).then_inc(lam_exp, 1)

            def h_transposed(j):
                b = full(f"xT{j}")
                f(hT[:, 2 * j * S:(2 * j + 1) * S], b[:, 0:S], ACT.Copy, scale=par("mix_g")[:, 2 * j:2 * j + 1])
                f(hT[:, (2 * j + 1) * S:(2 * j + 2) * S], b[:, S:2 * S], ACT.Copy,
                  scale=par("mix_g")[:, 2 * j + 1:2 * j + 2]).then_inc(free(f"xT{j}"), 1)
                act.wait_ge(free(f"xT{j}"), items[f"xT{j}"][1] + 1)
                act.sem_inc(hT_a, 1)

            act.wait_ge(params_a_in, 16)
            h_transposed(0)
            h_transposed(2)
            act.wait_ge(ax_pads, 1)
            b = full("ax")
            f(ax[:, :].rearrange("p (c s) -> p c s", c=2)[:, :, 3:S + 3], b[:, :].rearrange("p (c s) -> p c s", c=2),
              ACT.Copy).then_inc(free("ax"), 1)
            act.wait_ge(free("ax"), items["ax"][1] + 1)
            act.sem_inc(ax_ready, 1)

            def copy_out(name, dst, ready):
                b = full(name)
                f(dst[:, :], b[:, :], ACT.Copy).then_inc(free(name), 1)
                act.wait_ge(free(name), items[name][1] + 1)
                act.sem_inc(ready, 1)

            copy_out("bq", bq, bq_ready)
            f(hT_hi, hT[:, :], ACT.Copy).then_inc(hT_hi_ready, 1)

            def chunk_first_part(name, hi, ready):
                s = CHUNK_SLOT[CHUNKS.index(name)]
                act.wait_ge(slot_full[s], 16)
                f(hi, slot[s], ACT.Copy).then_inc(ready, 1)

            chunk_first_part("in_cqk", cqk_hi, cqk_hi_ready)

            def first_part(i):
                n = CHUNKS.index(SPLIT[i])
                s = CHUNK_SLOT[n]
                act.wait_ge(slot_full[s], 16 * (chunk_use(n) + 1))
                f(parts[s][1], slot[s][:, 0:HALF], ACT.Copy).then_inc(part_hi_ready, 1)

            b = full("kcks")
            for half in range(2):
                r = half * DH
                f(kc2[r:r + DH, :], b[0:DH, 0:S], ACT.Copy)
                f(vc2[r:r + DH, :], b[DH:P, 0:S], ACT.Copy)
                f(ks2[r:r + DH, :], b[0:DH, S:2 * S], ACT.Copy)
                last = f(kw2[r:r + DH, :], b[DH:P, S:2 * S], ACT.Copy)
            last.then_inc(free("kcks"), 1)
            act.wait_ge(free("kcks"), items["kcks"][1] + 1)
            act.sem_inc(kc_ready, 1)
            act.sem_inc(ks_ready, 1)
            chunk_first_part("in_cvdq", cvdq_hi, cvdq_hi_ready)
            act.wait_ge(dgate_raw, 1)
            f(gsig[:, :], gsig[:, :], ACT.Tanh, scale=0.5).then_inc(dgate_tanh, 1)

            def exps(fam):
                n = FAM_NO[fam]
                act.wait_ge(neg_ready, n + 1)
                for j, (probs, o) in enumerate(((fam_q1(fam), 0), (fam_q0(fam), 4))):
                    for h in range(NH):
                        c = n * 8 + o + h
                        last = f(probs[:, h, :], probs[:, h, :], ACT.Exp, bias=negm[:, c:c + 1],
                                 accum_out=den[:, c:c + 1])
                if fam == "swa":
                    last.then_inc(act_step, 1)
                    step[0] += 1
                    act.wait_ge(act_step, step[0])
                    last = f(es[:, :], es[:, :], ACT.Exp)
                last.then_inc(exp_ready, 1)

            copy_out("cq", cq, cq_ready)
            first_part(0)
            act.wait_ge(h1_raw, 1)
            f(h1a[:, :], h1a[:, :], ACT.Tanh, scale=GELU_K).then_inc(h1_tanh, 1)
            act.wait_ge(lru_par_ready, 1)
            act.wait_ge(gelu_in, 1)
            f(lru_w[:, :], lru_w[:, :], ACT.Tanh, scale=GELU_K)
            for name, dst, bias in (("lr", lru_tr, bga), ("lx", lru_ti, bgx)):
                b = full(name)
                for cb in range(2):
                    last = f(dst[:, cb * S:(cb + 1) * S], b[:, cb * S:(cb + 1) * S], ACT.Tanh, scale=0.5,
                             bias=bias[:, cb:cb + 1])
                last.then_inc(free(name), 1)
                act.wait_ge(free(name), items[name][1] + 1)
            for cb in range(2):
                last = f(lru_t[:, cb * S:(cb + 1) * S], lru_tr[:, cb * S:(cb + 1) * S], ACT.Tanh,
                         scale=sp2[:, cb:cb + 1], bias=sp2[:, cb:cb + 1])
            link(last)
            exps("swa")
            first_part(1)
            f(lru_s[:, :], lru_t[:, :], ACT.Sqrt).then_inc(lru_tanh_ready, 1)
            exps("diff0")
            first_part(2)
            copy_out("dq", dq, dq_ready)
            first_part(3)
            exps("diff1")

            gate_no = [0]

            def gate_tanh(br, n2, dst):
                b = full(f"g{br}_{n2}")
                for j in range(2):
                    n = 2 * n2 + j
                    last = f(dst[:, j * S:(j + 1) * S], b[:, j * S:(j + 1) * S], ACT.Tanh, scale=0.5,
                             bias=bgh[:, br * KT + n:br * KT + n + 1])
                last.then_inc(free(f"g{br}_{n2}"), 1)
                act.wait_ge(free(f"g{br}_{n2}"), items[f"g{br}_{n2}"][1] + 1)
                act.sem_inc(gate_ready, 1)

            def early_gate(br, n2):
                gate_tanh(br, n2, gates[:, br * KT * S + n2 * 512:br * KT * S + (n2 + 1) * 512])

            def probs_out(fam, h):
                u = TP_FAMS.index(fam) * NH + h
                b = full(f"tp_{fam}_{h}")
                if u >= 4:
                    act.wait_ge(pt_used, u - 3)
                f(pt[:, (u % 4) * 384:(u % 4 + 1) * 384], b[:, 0:384], ACT.Copy).then_inc(pt_ready, 1)
                act.wait_ge(pt_ready, u + 1)
                act.sem_inc(free(f"tp_{fam}_{h}"), 1)

            early_gate(0, 0)
            early_gate(0, 1)
            act.wait_ge(bias_in, 16 * 2 * P // BIAS_ROWS)
            for h in range(NH):
                probs_out("swa", h)
            first_part(4)
            exps("sel")
            act.wait_ge(cmp_in, 1)
            f(pc_s[:, :].rearrange("p (a c) -> p a c", c=16)[:, :, 0:NCMP],
              pc_s[:, :].rearrange("p (a c) -> p a c", c=16)[:, :, 0:NCMP], ACT.Exp).then_inc(cmp_exp, 1)
            early_gate(0, 2)
            early_gate(0, 3)
            for h in range(NH):
                probs_out("diff", h)
            first_part(5)
            first_part(6)
            act.wait_ge(oc_squares, 1)
            f(rc[:, :], ssc[:, :], ACT.Sqrt).then_inc(oc_root, 1)
            act.wait_ge(ya_ready, 1)
            early_gate(1, 0)
            early_gate(1, 1)
            for h in range(NH):
                probs_out("sel", h)
            first_part(7)
            exps("win")
            first_part(8)
            for j in range(2):
                b = full(f"tpc{j}")
                f(pcT[0:NCMP, j * 512:(j + 1) * 512], b[0:NCMP, :], ACT.Copy).then_inc(free(f"tpc{j}"), 1)
                act.wait_ge(free(f"tpc{j}"), items[f"tpc{j}"][1] + 1)
                act.sem_inc(pcT_ready, 1)
            early_gate(1, 2)
            early_gate(1, 3)
            for h in range(NH):
                probs_out("win", h)
            first_part(9)
            first_part(10)
            for n2 in range(4):
                for br in (2, 3):
                    n = 2 * n2 + br - 2
                    if n:
                        act.wait_ge(late_used, n)
                    else:
                        act.wait_ge(pt_used, 12)
                    gate_tanh(br, n2, late_gate)
                    first_part(8 + n + 3)
            first_part(len(SPLIT) - 1)
            root_table()
            for t in range(TT):
                act.wait_ge(x1_ready, 2 * (t + 1) if t else 3)
                f(h2[:, t * D:(t + 1) * D], x1[:, t * D:(t + 1) * D], ACT.Square,
                  accum_out=ss[:, t:t + 1]).then_inc(squares_ready, 1)
                act.wait_ge(ms_ready, 2 + t)
                f(rt[:, t:t + 1], ss[:, t:t + 1], ACT.Sqrt).then_inc(root_ready, 1)
                if t == 0:
                    act.wait_ge(rstd_ready, 1)
                    f(h2[:, 0:D], x1[:, 0:D], ACT.Copy, scale=rstd[:, 0:1]).then_inc(h2_a, 1)
            for j in (0, 2):
                b = full(f"hT{j}")
                for k in (2 * j, 2 * j + 1):
                    last = f(h2T[:, k * S:(k + 1) * S], b[:, (k % 2) * S:(k % 2 + 1) * S], ACT.Copy,
                             scale=par("ffn_g")[:, k:k + 1])
                last.then_inc(free(f"hT{j}"), 1)
                act.wait_ge(free(f"hT{j}"), items[f"hT{j}"][1] + 1)
                act.sem_inc(h2T_a, 1)
            act.wait_ge(h2_a, 1)
            act.wait_ge(h2_d, 1)
            for t in range(TT):
                f(h2_hi[:, t * D:(t + 1) * D], h2[:, t * D:(t + 1) * D], ACT.Copy).then_inc(h2_hi_ready, 1)
            act.wait_ge(grp_in, 1)
            f(gexp[:, 0:10], gexp[:, 0:10], ACT.Exp).then_inc(grp_exp, 1)

            for k in range(0, KT, 2):
                b = full(f"xg{k}")
                f(xg_all[:, k, 0:2 * S], b[:, :], ACT.Copy, scale=par("ffn_g")[:, k:k + 1]).then_inc(free(f"xg{k}"), 1)
                act.wait_ge(free(f"xg{k}"), items[f"xg{k}"][1] + 1)
            act.sem_inc(xg_all_a, 1)
            act.wait_ge(xg_all_d, 1)
            act.wait_ge(count_ready, 1)

            gu_bank, cd, xgs = psum[4], psum[6:8], (xg0, xg1)

            def tokens_in(c, i, p):
                n = i + c * PAIRS
                at = act.value_load(first_slot_i[0:1, bass.ds(i * 2, 1)], min_val=0, max_val=SLOT_COLS - CAP)
                wait_past(act, gu_done, before_last(n))
                f(xgs[p].rearrange("p (k e s) -> p k e s", k=KT, e=2)[:, :, 0, :],
                  xg_all[:, :, bass.ds(at, CAP)], ACT.Copy).then_inc(xg_a, 1)

            def pair_step(c, i, p, last=False):
                n = i + c * PAIRS
                if not last:
                    tokens_in(c, i + 1, 1 - p)
                act.wait_ge(gu_done, n + 1)
                wait_past(act, he_ready, n)
                f(silu_g[:, :], gu_bank[:, 0:FF], ACT.Silu).then_inc(silu_done, 1)

            def outputs_out(c, i):
                act.wait_ge(down_done, i + c * PAIRS + 1)
                f(yexp[:, 0:512], cd[0][:, :], ACT.Copy).then_inc(yexp_a, 1)

            def expert_pass(c):
                tokens_in(c, 0, 0)
                pair_step(c, 0, 0)
                with act.Fori(0, PAIRS // 2 - 1) as it:
                    for p in (1, 0):
                        i = it * 2 + (1 if p else 2)
                        pair_step(c, i, p)
                        outputs_out(c, i - 1)
                pair_step(c, PAIRS - 1, 1, last=True)
                outputs_out(c, PAIRS - 2)
                outputs_out(c, PAIRS - 1)

            expert_pass(0)
            act.wait_ge(count_ready, 1)
            most = act.value_load(cmax_i[0:1, 0:1], min_val=0, max_val=S)
            with act.If(most > CAP):
                with act.Fori(1, PASSES) as c:
                    act.wait_ge(slots_moved, c)
                    act.sem_inc(pass_begun, 1)
                    expert_pass(c)
            root_table()
            for t in range(TT):
                act.wait_ge(fin_in, t + 1)
                f(h2[:, t * D:(t + 1) * D], x1[:, t * D:(t + 1) * D], ACT.Square,
                  accum_out=ss[:, t:t + 1]).then_inc(fin_squares, 1)
            for t in range(TT):
                act.wait_ge(fin_ms, t + 1)
                f(rt[:, t:t + 1], ss[:, t:t + 1], ACT.Sqrt).then_inc(fin_root, 1)

        @block.vector
        def _(dve):
            v = nc.vector
            step = [0]

            def link(ins):
                step[0] += 1
                ins.then_inc(dve_step, 1)
                dve.wait_ge(dve_step, step[0])

            counts = {}

            def tell(ins, s):
                counts[s.name] = counts.get(s.name, 0) + 1
                ins.then_inc(s, 1)
                dve.wait_ge(s, counts[s.name])

            def full(name):
                bank, _, value = items[name]
                dve.wait_ge(bank_full[bank], value)
                return psum[bank]

            def release(name, ins):
                bank, use, _ = items[name]
                ins.then_inc(bank_free[bank], 1)
                dve.wait_ge(bank_free[bank], use + 1)

            tell(v.memset(spare[:, :], 1.0), spare_set)
            tell(v.memset(ax[:, :].rearrange("p (c s) -> p c s", c=2)[:, :, 0:3], 0.0), ax_pads)
            link(v.memset(zeros16[:, :], 0.0))
            dve.wait_ge(squares_ready, 2)
            tell(v.tensor_scalar(ss[:, :], ss[:, :], 1.0 / D, 1e-6, ALU.mult, ALU.add), ms_ready)
            dve.wait_ge(root_ready, 1)
            link(v.reciprocal(rstd[:, :], rt[:, :]))
            for t in range(TT):
                tell(v.tensor_scalar(xn[:, t * D:(t + 1) * D], x_sb[:, t * D:(t + 1) * D], rstd[:, t:t + 1], None,
                                     ALU.mult), xn_ready)
            b = full("vec")
            release("vec", v.tensor_copy(vec, b[0:NB, :]))
            dve.sem_inc(vec_ready, 1)
            dve.wait_ge(params_b_in, 16)
            link(v.tensor_scalar(sp_c[:, :], par("lam"), -1.0, None, ALU.mult))
            tell(v.tensor_tensor(sp_a[:, :], par("lam"), sp_c[:, :], ALU.min), sp_in)
            link(v.tensor_tensor(lru_scratch[:, 0:32], par("lq1"), par("lk1"), ALU.mult))
            link(v.tensor_tensor(lru_scratch[:, 32:64], par("lq2"), par("lk2"), ALU.mult))
            tell(v.reduce_sum(lam4[:, 0:2], lru_scratch[:, 0:64].rearrange("p (a b) -> p a b", a=2), axis=X), lam_in)
            link(v.tensor_scalar(bga[:, :], par("b_a"), 0.5, None, ALU.mult))
            link(v.tensor_scalar(bgx[:, :], par("b_x"), 0.5, None, ALU.mult))
            link(v.tensor_scalar(bgh[:, :], par("b_gate"), 0.5, None, ALU.mult))
            link(v.tensor_scalar(gsubln[:, :], par("subln_g"), 0.8, None, ALU.mult))

            def h_transposed(j):
                b = full(f"xT{j}")
                link(v.tensor_scalar(hT[:, 2 * j * S:(2 * j + 1) * S], b[:, 0:S], par("mix_g")[:, 2 * j:2 * j + 1],
                                     None, ALU.mult))
                release(f"xT{j}", v.tensor_scalar(hT[:, (2 * j + 1) * S:(2 * j + 2) * S], b[:, S:2 * S],
                                                  par("mix_g")[:, 2 * j + 1:2 * j + 2], None, ALU.mult))
                dve.sem_inc(hT_d, 1)

            h_transposed(1)
            h_transposed(3)
            dve.wait_ge(sp_exp, 1)
            link(v.tensor_scalar(sp_a[:, :], sp_b[:, :], 2.0, None, ALU.add))
            link(v.reciprocal(sp_a[:, :], sp_a[:, :]))
            link(v.tensor_tensor(sp_a[:, :], sp_a[:, :], sp_b[:, :], ALU.mult))
            link(v.tensor_tensor(sp_b[:, :], sp_a[:, :], sp_a[:, :], ALU.mult))
            link(v.tensor_scalar(sp2[:, :], sp_b[:, :], 1.0 / 17, 1.0 / 15, ALU.mult, ALU.add))
            for n in (13, 11, 9, 7, 5, 3, 1):
                link(v.tensor_tensor(sp2[:, :], sp2[:, :], sp_b[:, :], ALU.mult))
                link(v.tensor_scalar(sp2[:, :], sp2[:, :], 1.0 / n, None, ALU.add))
            link(v.tensor_tensor(sp2[:, :], sp2[:, :], sp_a[:, :], ALU.mult))
            link(v.tensor_scalar(sp_c[:, :], sp_c[:, :], 0.0, None, ALU.max))
            link(v.tensor_scalar(sp2[:, :], sp2[:, :], 2.0, None, ALU.mult))
            link(v.tensor_tensor(sp2[:, :], sp2[:, :], sp_c[:, :], ALU.add))
            tell(v.tensor_scalar(sp2[:, :], sp2[:, :], 2.0, None, ALU.mult), lru_par_ready)
            dve.wait_ge(lam_exp, 1)
            link(v.tensor_tensor(lam4[:, 4:5], lam4[:, 3:4], lam4[:, 2:3], ALU.subtract))
            link(v.tensor_scalar(lam4[:, 4:5], lam4[:, 4:5], -0.2, None, ALU.add))

            b = full("ag")
            release("ag", v.tensor_copy(ag[:, :], b[:, :]))
            b = full("bkvb")
            for kv in range(2):
                for half in range(2):
                    r = half * DH
                    v.tensor_copy(kb[r:r + DH, kv * S:(kv + 1) * S], b[kv * DH:(kv + 1) * DH, 0:S])
            release("bkvb", v.tensor_copy(v_b[:, :], b[:, S:2 * S]))
            dve.sem_inc(kb_ready, 1)
            dve.sem_inc(v_ready, 1)
            dve.wait_ge(cqk_hi_ready, 1)
            v.tensor_tensor(cqk_lo, slot[CHUNK_SLOT[CHUNKS.index("in_cqk")]], cqk_hi.bitcast(f32), ALU.subtract
                            ).then_inc(cqk_lo_ready, 1)
            b = full("vsg")
            v.tensor_copy(v_sw[:, :], b[:, 0:S])
            release("vsg", v.tensor_copy(gsig[:, :], b[:, S:S + 2 * NB]))
            dve.sem_inc(dgate_raw, 1)
            dve.sem_inc(v_ready, 1)

            def to_sigmoid():
                dve.wait_ge(dgate_tanh, 1)
                link(v.tensor_scalar(gsig[:, :], gsig[:, :], 0.5, 0.5, ALU.mult, ALU.add))

            def family_scores(fam, scale, bias_h, first):
                n = FAM_NO[fam]
                q1, q0 = fam_q1(fam), fam_q0(fam)
                for part, h in (("a", 0), ("b", 1)):
                    for qt, dst, keys in ((0, q0, slice(P, S)), (1, q1, slice(0, S))):
                        name = f"s_{fam}_{part}{qt}"
                        width = keys.stop - keys.start
                        release(name, v.scalar_tensor_tensor(
                            dst[:, h:NH:2, :], full(name)[:, 0:2 * width].rearrange("p (h k) -> p h k", h=2), scale,
                            bias_h[:, first + h:first + NH:2, keys], ALU.mult, ALU.add))
                c = n * 8
                link(v.reduce_max(mx[:, c:c + 4], q1, axis=X))
                link(v.reduce_max(mx[:, c + 4:c + 8], q0, axis=X))
                if fam == "swa":
                    for j in (0, 4):
                        link(v.tensor_tensor(mx[:, j:j + 4], mx[:, j:j + 4], par("sinks"), ALU.max))
                        link(v.tensor_tensor(es[:, j:j + 4], par("sinks"), mx[:, j:j + 4], ALU.subtract))
                tell(v.tensor_scalar(negm[:, c:c + 8], mx[:, c:c + 8], -1.0, None, ALU.mult), neg_ready)

            def inverse_sums(fam):
                n = FAM_NO[fam]
                dve.wait_ge(exp_ready, n + 1)
                d = den[:, n * 8:n * 8 + 8]
                if fam == "swa":
                    link(v.tensor_tensor(d, d, es[:, :], ALU.add))
                link(v.tensor_scalar(d, d, TINY, None, ALU.max))
                link(v.reciprocal(fac[:, :], d))

            def scale_probs(fam):
                for o, probs in ((0, fam_q1(fam)), (4, fam_q0(fam))):
                    for h in range(NH):
                        last = v.tensor_scalar(probs[:, h, :], probs[:, h, :], fac[:, o + h:o + h + 1], None, ALU.mult)
                return last

            def gate_factors(which):
                g = gsig[:, :].rearrange("p (t h g) -> p t h g", t=TT, h=NH)
                link(v.tensor_tensor(fac[:, 0:4], fac[:, 0:4], g[:, 1, :, which], ALU.mult))
                link(v.tensor_tensor(fac[:, 4:8], fac[:, 4:8], g[:, 0, :, which], ALU.mult))

            dve.wait_ge(kc_ready, 1)
            for src, pos in ((kc2, "pos_k"), (vc2, "pos_v")):
                lo = src[0:DH, :].rearrange("p (c i) -> p c i", i=16)
                hi = src[DH:P, :].rearrange("p (c i) -> p c i", i=16)
                link(v.tensor_tensor(lo, lo, par(pos)[0:DH, :].unsqueeze(1).broadcast_to([DH, 16, 16]), ALU.add))
                link(v.tensor_tensor(hi[:, 0:15, :], hi[:, 1:16, :],
                                     par(pos)[DH:P, :].unsqueeze(1).broadcast_to([DH, 15, 16]), ALU.add))
            dve.sem_inc(blocks_ready, 1)
            dve.wait_ge(ax_ready, 1)
            for cb in range(2):
                src = ax[:, cb * (S + 3):(cb + 1) * (S + 3)]
                dst = xc[:, cb * S:(cb + 1) * S]
                link(v.tensor_scalar(dst, src[:, 0:S], par("conv_w")[:, cb:cb + 1], par("conv_b")[:, cb:cb + 1],
                                     ALU.mult, ALU.add))
                for i in range(1, 4):
                    link(v.scalar_tensor_tensor(dst, src[:, i:i + S], par("conv_w")[:, 2 * i + cb:2 * i + cb + 1], dst,
                                                ALU.mult, ALU.add))
            dve.sem_inc(xc_ready, 1)
            link(v.tensor_tensor(lru_w[:, :], ag[:, :], ag[:, :], ALU.mult))
            link(v.tensor_scalar(lru_w[:, :], lru_w[:, :], GELU_C, 1.0, ALU.mult, ALU.add))
            tell(v.tensor_tensor(lru_w[:, :], lru_w[:, :], ag[:, :], ALU.mult), gelu_in)
            b = full("ck")
            release("ck", v.tensor_copy(ck[:, :], b[:, :]))
            dve.sem_inc(ck_ready, 1)
            b = full("h1")
            release("h1", v.tensor_copy(h1[:, :], b[:, 0:NCMP]))
            link(v.tensor_tensor(h1a[:, :], h1[:, :], h1[:, :], ALU.mult))
            link(v.tensor_scalar(h1a[:, :], h1a[:, :], GELU_C, 1.0, ALU.mult, ALU.add))
            tell(v.tensor_tensor(h1a[:, :], h1a[:, :], h1[:, :], ALU.mult), h1_raw)
            dve.wait_ge(bias_in, 16 * 2 * P // BIAS_ROWS)
            family_scores("swa", DH ** -0.5, bias8, 0)
            dve.wait_ge(h1_tanh, 1)
            link(v.scalar_tensor_tensor(h1b[:, :], h1a[:, :], 1.0, h1[:, :], ALU.add, ALU.mult))
            tell(v.tensor_scalar(h1b[:, :], h1b[:, :], 0.5, None, ALU.mult), h1_ready)
            family_scores("diff0", 32 ** -0.5, bias8, 4)
            inverse_sums("swa")
            tell(scale_probs("swa"), p_ready)
            b = full("vc")
            release("vc", v.tensor_copy(v_c[:, :], b[:, :]))
            dve.sem_inc(v_ready, 1)
            dve.wait_ge(lru_tanh_ready, 1)
            link(v.scalar_tensor_tensor(xc[:, :], lru_ti[:, :], 1.0, xc[:, :], ALU.add, ALU.mult))
            xc3 = xc[:, :].rearrange("p (c s) -> p c s", c=2)
            link(v.tensor_scalar(lru_scratch[:, 0:2].unsqueeze(2), xc3[:, :, 0:1], 0.5, None, ALU.mult))
            link(v.tensor_scalar(lru_tr[:, :], lru_t[:, :], 1.0, None, ALU.add))
            link(v.reciprocal(lru_tr[:, :], lru_tr[:, :]))
            link(v.tensor_scalar(lru_t[:, :], lru_t[:, :], -1.0, 1.0, ALU.mult, ALU.add))
            link(v.tensor_tensor(lru_t[:, :], lru_t[:, :], lru_tr[:, :], ALU.mult))
            link(v.tensor_tensor(xc[:, :], xc[:, :], lru_s[:, :], ALU.mult))
            link(v.tensor_tensor(xc[:, :], xc[:, :], lru_tr[:, :], ALU.mult))
            link(v.tensor_copy(xc3[:, :, 0:1], lru_scratch[:, 0:2].unsqueeze(2)))
            family_scores("diff1", 32 ** -0.5, bias8, 4)
            for cb in range(2):
                c = slice(cb * S, (cb + 1) * S)
                link(v.tensor_tensor_scan(lru_s[:, c], lru_t[:, c], xc[:, c], 0.0, ALU.mult, ALU.add))
            link(v.scalar_tensor_tensor(ag[:, :], lru_w[:, :], 1.0, ag[:, :], ALU.add, ALU.mult))
            link(v.scalar_tensor_tensor(ya[:, :], lru_s[:, :], 0.5, ag[:, :], ALU.mult, ALU.mult))
            dve.sem_inc(ya_ready, 1)
            b = full("kc2")
            release("kc2", v.tensor_copy(kcT[:, :], b[:, 0:NCMP]))
            b = full("vc2")
            release("vc2", v.tensor_copy(vc_d[0:NCMP, :], b[0:NCMP, 0:DH]))
            dve.sem_inc(kc2_ready, 1)
            to_sigmoid()
            inverse_sums("diff1")
            link(v.tensor_scalar(fac[:, :], fac[:, :], lam4[:, 4:5], None, ALU.mult))
            link(scale_probs("diff1"))
            inverse_sums("diff0")
            for o, p0, p1 in ((0, fam_q1("diff0"), fam_q1("diff1")), (4, fam_q0("diff0"), fam_q0("diff1"))):
                for h in range(NH):
                    last = v.scalar_tensor_tensor(p0[:, h, :], p0[:, h, :], fac[:, o + h:o + h + 1], p1[:, h, :],
                                                  ALU.mult, ALU.add)
            tell(last, p_ready)
            for j in range(2):
                dve.wait_ge(pt_used, 2 * j + 2)
                b = psum[items[f"yb{j}"][0]]
                release(f"yb{j}", v.tensor_copy(yb[:, j * S:(j + 1) * S], b[:, 0:S]))
                dve.sem_inc(yb_ready, 1)
            pc3 = pc_s[:, :].rearrange("p (a c) -> p a c", c=16)
            cmask = o_c[:, 256:384].rearrange("p (a c) -> p a c", c=16)
            for t in range(TT):
                at = 31 + P * (1 - t)
                link(v.tensor_scalar(cmask[:, t * 4:t * 4 + 4, 0:NCMP], bias4[:, :, at:at + 16 * (NCMP - 1) + 1:16],
                                     -1e29, None, ALU.is_gt))
            for part, h in (("a", 0), ("b", 1)):
                b = full(f"sc_{part}")
                sc3 = b[:, 0:DH].rearrange("p (a c) -> p a c", c=16)
                for t in range(TT):
                    at = 31 + P * (1 - t)
                    ins = v.scalar_tensor_tensor(pc3[:, t * 4 + h:t * 4 + 4:2, 0:NCMP],
                                                 sc3[:, t * 2:t * 2 + 2, 0:NCMP], DH ** -0.5,
                                                 bias4[:, h:NH:2, at:at + 16 * (NCMP - 1) + 1:16],
                                                 ALU.mult, ALU.add)
                    if t == TT - 1:
                        release(f"sc_{part}", ins)
                    else:
                        link(ins)
            pcv, cmv = pc3[:, :, 0:NCMP], cmask[:, :, 0:NCMP]
            link(v.reduce_max(cmx[:, :], pcv, axis=X))
            tell(v.tensor_tensor(pcv, pcv, cmx[:, :].unsqueeze(2).broadcast_to([P, 8, NCMP]), ALU.subtract), cmp_in)
            family_scores("sel", DH ** -0.5, bias4, 0)
            dve.wait_ge(cmp_exp, 1)
            link(v.tensor_tensor(pcv, pcv, cmv, ALU.mult))
            link(v.reduce_sum(cmx[:, :], pcv, axis=X))
            link(v.tensor_scalar(cmx[:, :], cmx[:, :], TINY, None, ALU.max))
            link(v.reciprocal(cmx[:, :], cmx[:, :]))
            g4 = gsig[:, :].rearrange("p (a g) -> p a g", g=3)
            link(v.tensor_tensor(cmx[:, :], cmx[:, :], g4[:, :, 0], ALU.mult))
            tell(v.tensor_tensor(pcv, pcv, cmx[:, :].unsqueeze(2).broadcast_to([P, 8, NCMP]), ALU.mult), pc_ready)
            inverse_sums("sel")
            gate_factors(1)
            tell(scale_probs("sel"), p_ready)
            dve.wait_ge(pt_used, 8)
            b = psum[items["oc"][0]]
            release("oc", v.tensor_copy(o_c[:, :], b[:, :]))
            link(v.tensor_tensor(xc[:, :], o_c[:, :], o_c[:, :], ALU.mult))
            link(v.reduce_sum(ssc[:, :], xc[:, :].rearrange("p (a d) -> p a d", d=DH), axis=X))
            tell(v.tensor_scalar(ssc[:, :], ssc[:, :], 1.0 / DH, 1e-5, ALU.mult, ALU.add), oc_squares)
            family_scores("win", DH ** -0.5, bias4, 0)
            dve.wait_ge(oc_root, 1)
            link(v.reciprocal(rc[:, :], rc[:, :]))
            oc3 = o_c[:, :].rearrange("p (a d) -> p a d", d=DH)
            tell(v.tensor_tensor(oc3, oc3, rc[:, :].unsqueeze(2).broadcast_to([P, 8, DH]), ALU.mult), oc_ready)
            b = full("ycT")
            release("ycT", v.tensor_scalar(yc[:, :], b[:, :], gsubln[:, 0:1], None, ALU.mult))
            dve.sem_inc(yc_ready, 1)
            inverse_sums("win")
            gate_factors(2)
            tell(scale_probs("win"), p_ready)
            for j in range(2):
                b = full(f"yd{j}")
                release(f"yd{j}", v.tensor_copy(yd[:, j * S:(j + 1) * S], b[:, 0:S]))
                dve.sem_inc(yd_ready, 1)
            dve.wait_ge(pt_used, 16)
            for n2 in range(4):
                dst = merged[:, n2 * 512:(n2 + 1) * 512]
                for br in range(4):
                    dve.wait_ge(gate_ready, 8 if br < 2 else 8 + 2 * n2 + br - 1)
                    g = gates[:, br * KT * S + n2 * 512:br * KT * S + (n2 + 1) * 512] if br < 2 else late_gate
                    b = full(f"b{n2}_{br}")
                    release(f"b{n2}_{br}", v.scalar_tensor_tensor(branch_tmp if br else dst, g, 1.0, b[:, :],
                                                                  ALU.add, ALU.mult))
                    if br >= 2:
                        dve.sem_inc(late_used, 1)
                    if br == 3:
                        link(v.tensor_tensor(dst, dst, branch_tmp, ALU.add))
                        hi, lo = merged_hi[:, n2 * 512:(n2 + 1) * 512], merged_lo[:, n2 * 512:(n2 + 1) * 512]
                        link(v.tensor_copy(hi, dst))
                        tell(v.tensor_tensor(lo, dst, hi.bitcast(f32), ALU.subtract), merged_ready)
                    elif br:
                        link(v.tensor_tensor(dst, dst, branch_tmp, ALU.add))
            for j in range(8):
                last = v.tensor_scalar(iota512[:, j * CAP:(j + 1) * CAP], par("iota"), float(j * CAP), None, ALU.add)
            link(last)
            def residual(t, nh):
                c = slice(t * D + nh * 512, t * D + (nh + 1) * 512)
                b = full(f"x1_{t}{nh}")
                release(f"x1_{t}{nh}", v.scalar_tensor_tensor(x1[:, c], b[:, :], 0.5, x_sb[:, c], ALU.mult, ALU.add))
                dve.sem_inc(x1_ready, 1)

            residual(0, 0)
            residual(1, 0)
            for t in range(TT):
                residual(t, 1)
                dve.wait_ge(squares_ready, 3 + t)
                tell(v.tensor_scalar(ss[:, t:t + 1], ss[:, t:t + 1], 1.0 / D, 1e-6, ALU.mult, ALU.add), ms_ready)
                dve.wait_ge(root_ready, 2 + t)
                link(v.reciprocal(rstd[:, t:t + 1], rt[:, t:t + 1]))
                if t == 0:
                    dve.sem_inc(rstd_ready, 1)
            tell(v.tensor_scalar(h2[:, D:2 * D], x1[:, D:2 * D], rstd[:, 1:2], None, ALU.mult), h2_d)
            for j in (1, 3):
                b = full(f"hT{j}")
                for k in (2 * j, 2 * j + 1):
                    last = v.tensor_scalar(h2T[:, k * S:(k + 1) * S], b[:, (k % 2) * S:(k % 2 + 1) * S],
                                           par("ffn_g")[:, k:k + 1], None, ALU.mult)
                release(f"hT{j}", last)
                dve.sem_inc(h2T_d, 1)

            link(v.memset(selm[:, :], 0.0))
            link(v.memset(comb[:, :], 0.0))
            b = full("rlT")
            release("rlT", v.tensor_copy(logitsT, b[0:36, 0:S]))
            dve.sem_inc(rlT_ready, 1)
            b = full("rl")
            r3 = rlog.rearrange("p (t n) -> p t n", t=TT)
            release("rl", v.tensor_tensor(r3, b[:, 0:72].rearrange("p (t n) -> p t n", t=TT),
                                          par("b_router").unsqueeze(1).broadcast_to([P, TT, 36]), ALU.add))
            lg, le = r3[:, :, 0:GRP], r3[:, :, GRP:36]

            def first_of(onehot, vals, top, n, cand):
                link(v.reduce_max(top, vals, axis=X))
                link(v.tensor_tensor(cand, vals, top.unsqueeze(2).broadcast_to([P, TT, n]), ALU.not_equal))
                iota = par("iota8")[:, 0:n].unsqueeze(1).broadcast_to([P, TT, n])
                link(v.scalar_tensor_tensor(cand, cand, 100.0, iota, ALU.mult, ALU.add))
                link(v.tensor_reduce(wts[:, 6:8], cand, X, ALU.min))
                link(v.tensor_tensor(onehot, iota, wts[:, 6:8].unsqueeze(2).broadcast_to([P, TT, n]), ALU.is_equal))

            og, cg = ogrp.rearrange("p (t n) -> p t n", t=TT), cgrp.rearrange("p (t n) -> p t n", t=TT)
            first_of(og, lg, mgrp, GRP, cg)
            ge = grouped.rearrange("p (t g n) -> p t g n", t=TT, g=GRP)
            og_n = og.unsqueeze(3).broadcast_to([P, TT, GRP, EPG])
            i3 = ing.rearrange("p (t n) -> p t n", t=TT)

            def of_group(dst, by_expert):
                link(v.tensor_tensor(ge, by_expert[:, :, 0:E].rearrange("p t (g n) -> p t g n", g=GRP), og_n, ALU.mult))
                link(v.reduce_sum(dst, ge.rearrange("p t g n -> p t n g"), axis=X))

            def into_group(dst, in_group, ready=None):
                ins = v.tensor_tensor(dst[:, :, 0:E].rearrange("p t (g n) -> p t g n", g=GRP),
                                      in_group.unsqueeze(2).broadcast_to([P, TT, GRP, EPG]), og_n, ALU.mult)
                link(ins)
                if ready is not None:
                    dve.sem_inc(ready, 1)

            of_group(i3, le)
            o13, o23 = o1.rearrange("p (t n) -> p t n", t=TT), o2.rearrange("p (t n) -> p t n", t=TT)
            c83, in23 = c8.rearrange("p (t n) -> p t n", t=TT), in2.rearrange("p (t n) -> p t n", t=TT)
            first_of(o13, i3, v1, EPG, c83)
            link(v.scalar_tensor_tensor(in23, o13, NEG, i3, ALU.mult, ALU.add))
            first_of(o23, in23, v2, EPG, c83)
            s3 = selm.rearrange("p (t n) -> p t n", t=TT)
            k3 = comb.rearrange("p (t n) -> p t n", t=TT)
            link(v.tensor_tensor(c83, o13, o23, ALU.add))
            into_group(s3, c83, sel_ready)
            link(v.tensor_tensor(gexp[:, 0:8].rearrange("p (t n) -> p t n", t=TT), lg,
                                 mgrp.unsqueeze(2).broadcast_to([P, TT, GRP]), ALU.subtract))
            tell(v.tensor_tensor(gexp[:, 8:10], v2, v1, ALU.subtract), grp_in)
            b = full("rank")
            link(v.tensor_copy(cnt[:, :], b[:, 72:108]))
            link(v.tensor_tensor_scan(base[:, :], cnt[:, :], cnt[:, :], 0.0, ALU.add, ALU.max))
            link(v.tensor_tensor(base[:, :], base[:, :], cnt[:, :], ALU.subtract))
            pos3 = place.rearrange("p (t n) -> p t n", t=TT)
            rank3 = b[:, 0:72].rearrange("p (t n) -> p t n", t=TT)
            link(v.tensor_tensor(pos3, rank3, base.unsqueeze(1).broadcast_to([P, TT, 36]), ALU.add))
            pg3 = pos_g.rearrange("p (t n) -> p t n", t=TT)
            of_group(pg3, pos3)
            for j, o in enumerate((o13, o23)):
                link(v.tensor_tensor(c83, pg3, o, ALU.mult))
                link(v.reduce_sum(pos_12[:, 2 * j:2 * j + 2], c83, axis=X))
            for t in range(TT):
                g = onehot_all[:, t * 512:(t + 1) * 512]
                link(v.tensor_scalar(g, iota512[:, :], pos_12[:, t:t + 1], None, ALU.is_equal))
                tell(v.scalar_tensor_tensor(g, iota512[:, :], pos_12[:, 2 + t:3 + t], g.bitcast(f32), ALU.is_equal,
                                            ALU.add), slots_ready)
            sl3 = slotv.rearrange("p (t n) -> p t n", t=TT)
            link(v.scalar_tensor_tensor(sl3, rank3, 1.0, s3, ALU.add, ALU.mult))
            release("rank", v.tensor_scalar(slotv[:, :], slotv[:, :], -1.0, None, ALU.add))
            link(v.reduce_max(cmax[:, :], cnt[:, :], axis=X))
            link(v.tensor_copy(first_slot_i[:, :], base[:, :]))
            tell(v.tensor_copy(cmax_i[:, :], cmax[:, :]), count_ready)
            dve.wait_ge(grp_exp, 1)
            link(v.reduce_sum(gsum, gexp[:, 0:8].rearrange("p (t n) -> p t n", t=TT), axis=X))
            link(v.tensor_scalar(wts[:, 0:2], gexp[:, 8:10], 1.0, None, ALU.add))
            link(v.tensor_tensor(wts[:, 0:2], wts[:, 0:2], gsum, ALU.mult))
            link(v.reciprocal(wts[:, 0:2], wts[:, 0:2]))
            link(v.tensor_tensor(wts[:, 2:4], wts[:, 0:2], gexp[:, 8:10], ALU.mult))
            link(v.tensor_tensor(o13, o13, wts[:, 0:2].unsqueeze(2).broadcast_to([P, TT, EPG]), ALU.mult))
            link(v.tensor_tensor(o23, o23, wts[:, 2:4].unsqueeze(2).broadcast_to([P, TT, EPG]), ALU.mult))
            link(v.tensor_tensor(o13, o13, o23, ALU.add))
            into_group(k3, o13)
            for k in range(1, KT, 2):
                b = full(f"xg{k}")
                release(f"xg{k}", v.tensor_scalar(xg_all[:, k, 0:2 * S], b[:, :], par("ffn_g")[:, k:k + 1], None,
                                                   ALU.mult))
            dve.wait_ge(xg_pad, 1)
            dve.sem_inc(xg_all_d, 1)
            dve.wait_ge(xg_all_a, 1)

            gu_bank, tr_bank, cd = psum[4], psum[5], psum[6:8]
            xgs, gcs, tbs = (xg0, xg1), (gc0, gc1), (tb0, tb1)

            def tokens_in(c, i, p):
                n = i + c * PAIRS
                at = dve.value_load(first_slot_i[0:1, bass.ds(i * 2 + 1, 1)], min_val=0, max_val=SLOT_COLS - CAP)
                wait_past(dve, gu_done, before_last(n))
                v.tensor_copy(xgs[p].rearrange("p (k e s) -> p k e s", k=KT, e=2)[:, :, 1, :],
                              xg_all[:, :, bass.ds(at, CAP)]).then_inc(xg_d, 1)

            def way_back(c, i, p):
                for t in range(TT):
                    for e in range(2):
                        at = bass.ds(i * 2 + (t * 36 + e), 1)
                        last = v.scalar_tensor_tensor(
                            gcs[p][:, t * P + e * CAP:t * P + (e + 1) * CAP], par("iota"), slotv[:, at],
                            comb[:, at].broadcast_to([P, CAP]), ALU.is_equal, ALU.mult)
                last.then_inc(weighted_ready, 1)

            def outputs_out(c, i):
                dve.wait_ge(down_done, i + c * PAIRS + 1)
                v.tensor_copy(yexp[:, 512:1024], cd[1][:, :]).then_inc(yexp_d, 1)

            def pair_step(c, i, p, first=False, last=False):
                n = i + c * PAIRS
                if not last:
                    tokens_in(c, i + 1, 1 - p)
                dve.wait_ge(silu_done, n + 1)
                v.tensor_tensor(he[:, :], silu_g[:, :], gu_bank[:, FF:2 * FF], ALU.mult).then_inc(he_ready, 1)
                if not first:
                    outputs_out(c, i - 1)
                dve.wait_ge(tr_done, n + 1)
                v.tensor_copy(tbs[p], tr_bank[:, :]).then_inc(tb_ready, 1)
                if not last:
                    way_back(c, i + 1, 1 - p)

            def expert_pass(c):
                way_back(c, 0, 0)
                tokens_in(c, 0, 0)
                pair_step(c, 0, 0, first=True)
                with dve.Fori(0, PAIRS // 2 - 1) as it:
                    pair_step(c, it * 2 + 1, 1)
                    pair_step(c, it * 2 + 2, 0)
                pair_step(c, PAIRS - 1, 1, last=True)
                outputs_out(c, PAIRS - 1)

            expert_pass(0)
            most = dve.value_load(cmax_i[0:1, 0:1], min_val=0, max_val=S)
            with dve.If(most > CAP):
                with dve.Fori(1, PASSES) as c:
                    dve.wait_ge(xg_a, c * PAIRS)
                    v.tensor_scalar(slotv[:, :], slotv[:, :], -float(CAP), None, ALU.add)
                    v.tensor_scalar(base[:, :], base[:, :], float(CAP), 2.0 * S, ALU.add, ALU.min
                                    ).then_inc(base_moved, 1)
                    dve.wait_ge(base_moved, c)
                    v.tensor_copy(first_slot_i[:, :], base[:, :]).then_inc(slots_moved, 1)
                    dve.wait_ge(slots_moved, c)
                    expert_pass(c)
            for t in range(TT):
                dve.wait_ge(x2_ready, t + 1)
                for nh in range(2):
                    c = slice(t * D + nh * 512, t * D + (nh + 1) * 512)
                    ins = v.tensor_tensor(x1[:, c], psum[2 * t + nh][:, :], x1[:, c], ALU.add)
                ins.then_inc(fin_in, 1)
            dve.wait_ge(norm_g_in, 16)
            for t in range(TT):
                dve.wait_ge(fin_squares, t + 1)
                tell(v.tensor_scalar(ss[:, t:t + 1], ss[:, t:t + 1], 1.0 / D, 1e-6, ALU.mult, ALU.add), fin_ms)
            for t in range(TT):
                dve.wait_ge(fin_root, t + 1)
                link(v.reciprocal(rstd[:, t:t + 1], rt[:, t:t + 1]))
                for nh in range(2):
                    c = slice(t * D + nh * 512, t * D + (nh + 1) * 512)
                    v.scalar_tensor_tensor(x1[:, c], x1[:, c], rstd[:, t:t + 1], gfin[:, nh * 512:(nh + 1) * 512],
                                           ALU.mult, ALU.mult).then_inc(out_ready, 1)


def kernel(**inputs):
    import concourse.bacc as _bacc
    from concourse import mybir as _mybir
    from concourse.bass_utils import run_bass_kernel_spmd as _run

    a = {k: np.asarray(v) for k, v in inputs.items()}
    f32 = np.float32

    def by_rows(w):
        k, n = w.shape
        return np.ascontiguousarray(w.reshape(k // P, P, n).transpose(1, 0, 2).reshape(P, -1))

    def by_channel(v):
        return np.ascontiguousarray(v.reshape(-1, P).T)

    def rows_of(v):
        return np.broadcast_to(v.reshape(1, -1), (P, v.size))

    dist = 255 - np.arange(MW_BIAS)
    n = np.maximum(dist, 0)
    exact = BUCKETS // 2
    scaled = np.log(np.maximum(n, 1).astype(f32) / f32(exact)) / f32(math.log(MAXD / exact))
    large = np.minimum(exact + (scaled * f32(BUCKETS - exact)).astype(np.int32), BUCKETS - 1)
    bucket = np.where(n < exact, n, large)
    onehot = np.zeros((P, MW_BIAS), f32)
    onehot[bucket, np.arange(MW_BIAS)] = 1.0
    onehot[0:BUCKETS, dist < 0] = 0.0
    onehot[BUCKETS] = dist < 0
    onehot[BUCKETS + 1] = dist >= 128
    tab = np.zeros((P, NB), f32)
    tab[0:BUCKETS] = a["rel_bias"]
    tab[BUCKETS] = NEG
    tab[BUCKETS + 1, 0:NH] = NEG

    def lru_blocks(w):
        return w.reshape(2, 2, DH, DH).transpose(1, 2, 0, 3).reshape(P, 2 * DH)

    def positions(p):
        return p.reshape(2, 16, DH).transpose(0, 2, 1).reshape(P, 16)

    def w1_of(w):
        return w.reshape(2, 16, DH, DH).transpose(0, 2, 1, 3).reshape(P, 16 * DH)

    parts = {
        "ident": np.eye(P, dtype=f32), "mix_g": by_channel(a["mix_norm_g"][0]),
        "ffn_g": by_channel(a["ffn_norm_g"][0]), "tab": tab, "onehot": onehot,
        "conv_w": by_channel(a["conv_w"][0]), "conv_b": by_channel(a["conv_b"][0]),
        "b_a": by_channel(a["lru_b_a"][0]), "b_x": by_channel(a["lru_b_x"][0]),
        "lam": by_channel(a["lru_lambda"][0]),
        "subln_g": np.concatenate([a["diff_subln_g"][0]] * 2).reshape(P, 1),
        "b_gate": by_channel(a["b_gate"][0]), "sinks": rows_of(a["swa_sinks"][0]),
        "lq1": rows_of(a["diff_lq1"][0]), "lk1": rows_of(a["diff_lk1"][0]),
        "lq2": rows_of(a["diff_lq2"][0]), "lk2": rows_of(a["diff_lk2"][0]),
        "w_a": lru_blocks(a["lru_w_a"][0]), "w_x": lru_blocks(a["lru_w_x"][0]),
        "w2": np.concatenate([a["nsa_w2_k"][0], a["nsa_w2_v"][0]]),
        "pos_k": positions(a["nsa_pos_k"][0]), "pos_v": positions(a["nsa_pos_v"][0]),
        "upper": np.triu(np.ones((P, P), f32), 1), "ones": np.ones((P, P), f32),
        "iota": rows_of(np.arange(CAP, dtype=f32)), "iota8": rows_of(np.arange(8, dtype=f32)),
        "b_router": rows_of(np.concatenate([a["b_router_grp"][0], a["b_router_exp"][0]])),
        "w_router": by_rows(np.concatenate([a["w_router_grp"][0], a["w_router_exp"][0]], axis=1)),
    }

    def packed(names):
        return np.ascontiguousarray(np.concatenate([parts[n] for n, _ in COLUMNS if n in names], axis=1))

    w_in = a["w_in"][0]
    gate = a["w_gate"][0]
    eg, eu, ed = a["w_exp_gate"][0], a["w_exp_up"][0], a["w_exp_down"][0]
    w_moe = np.empty((PAIRS, 3, P, W_SLOT), f32)
    for e in range(2):
        gu = w_moe[:, e].reshape(PAIRS, P, KT, 2, FF)
        for j, w in enumerate((eg, eu)):
            gu[:, :, :, j, :] = w[e::2].reshape(PAIRS, KT, P, FF).transpose(0, 2, 1, 3)
        w_moe[:, 2].reshape(PAIRS, P, 2, 2, D)[:, :, e] = ed[e::2].reshape(PAIRS, 2, P, D).transpose(0, 2, 1, 3)
    arrays = {
        "pa": packed(FIRST_PART), "pb": packed(SECOND_PART),
        "w_in_full": np.stack([by_rows(w_in[:, c:c + 512]) for c in (0, 512, 1024, 1536)]),
        "w_in_tail": by_rows(np.concatenate([w_in[:, c:c + n] for c, n in (
            (2048, 128), (2176, 64), (2304, 64), (2240, 64), (2368, 64), (2432, 12))], axis=1)),
        "w1": np.concatenate([w1_of(a["nsa_w1_k"][0]), w1_of(a["nsa_w1_v"][0])], axis=1),
        "w_gates": np.stack([by_rows(gate[br][:, c:c + S]) for br in range(4) for c in range(0, D, S)]),
        "w_branch": np.stack([np.concatenate([by_rows(a["w_branch"][0][br + j]) for j in range(2)], axis=1)
                              for br in (0, 2)]),
        "w_out": np.stack([by_rows(a["w_out"][0][:, c:c + S]) for c in range(0, D, S)]),
        "w_moe": w_moe.reshape(PAIRS * 3, P, W_SLOT),
        "x": a["x"][0], "g_fin": a["final_norm_g"],
    }
    nc = _bacc.Bacc("TRN2", target_bir_lowering=False, num_devices=1)
    dt = _mybir.dt.float32
    args = {n: nc.dram_tensor(f"in_{n}_dram", v.shape, dt, kind="ExternalInput").ap() for n, v in arrays.items()}
    out = nc.dram_tensor("out_0_dram", (S, D), dt, kind="ExternalOutput").ap()
    decoder_layer(nc, out=out, **args)
    r = _run(nc, [{f"in_{n}_dram": np.ascontiguousarray(v) for n, v in arrays.items()}], core_ids=[0])
    return r.results[0]["out_0_dram"].reshape(1, S, D)
```
